# Optimizing a Trainium2 kernel written in Bass

```python
import math
import jax
import jax.numpy as jnp
from jax import lax
import numpy as np

D_MODEL = 1024
BATCH = 1
SEQ = 512
DEPTH = 2

CTX_LEN = 256
GRID_W = 64
N_MIXERS = 2
EPS = 1e-6
ADA_SCALE = 0.5

M_INNER = 2 * D_MODEL
M_HEADS = 4
M_DH_IN = M_INNER // M_HEADS
M_DQK = M_DH_IN // 2
M_DV = M_DH_IN
M_CONV = 3
M_CHUNK = 64

H_ORDER = 2
H_SCONV = 3
H_BANDS = 16
H_EMB = 2 * H_BANDS + 1
H_FH = 64
H_DECAY_MIN = -math.log(1e-2) / 1.5
H_DECAY_MAX = -math.log(1e-2) / 0.3

N_GROUPS = 4
EXP_PER_GROUP = 8
N_EXPERTS = N_GROUPS * EXP_PER_GROUP
TOP_K = 2
D_EXPERT = D_MODEL // 2
MOE_BLOCK = 128

kernel_name = 'hybrid_mlstm_hyena_hmoe_flow_backbone'

def rmsnorm(x, g):
    xf = x.astype(jnp.float32)
    y = xf * lax.rsqrt(jnp.mean(xf * xf, axis=-1, keepdims=True) + EPS)
    return (y * g.astype(jnp.float32)).astype(x.dtype)

def conv_centred(u, w, b):
    K = w.shape[0]
    L = u.shape[1]
    pad = K // 2
    up = jnp.pad(u, ((0, 0), (pad, pad), (0, 0)))
    out = b
    for kk in range(K):
        out = out + up[:, kk:kk + L] * w[kk]
    return out

def to_scan_order(x, col_major):
    if not col_major:
        return x
    B, L, D = x.shape
    rows = L // GRID_W
    return x.reshape(B, rows, GRID_W, D).transpose(0, 2, 1, 3).reshape(B, L, D)

def from_scan_order(x, col_major):
    if not col_major:
        return x
    B, L, D = x.shape
    rows = L // GRID_W
    return x.reshape(B, GRID_W, rows, D).transpose(0, 2, 1, 3).reshape(B, L, D)

def zero_state(B):
    f32 = jnp.float32
    return (jnp.zeros((B, M_HEADS, M_DV, M_DQK), f32),
            jnp.zeros((B, M_HEADS, M_DQK), f32),
            jnp.zeros((B, M_HEADS), f32))

def mlstm_scan(q, k, v, logi, logf, state):
    B, H, L, _ = q.shape
    nc = L // M_CHUNK

    def chunks(a):
        a = a.reshape(B, H, nc, M_CHUNK, *a.shape[3:])
        return jnp.moveaxis(a, 2, 0)

    mask = jnp.tril(jnp.ones((M_CHUNK, M_CHUNK), dtype=bool))

    def step(carry, xs):
        C, n, m = carry
        qc, kc, vc, ic, fc = xs
        b = jnp.cumsum(fc, axis=-1)
        log_d = b[..., :, None] - b[..., None, :] + ic[..., None, :]
        log_d = jnp.where(mask, log_d, -jnp.inf)
        inter = b + m[..., None]
        mj = jnp.maximum(inter, jnp.max(log_d, axis=-1))
        s = jnp.einsum('bhjd,bhsd->bhjs', qc, kc) * jnp.exp(log_d - mj[..., None])
        w_inter = jnp.exp(inter - mj)
        num = jnp.einsum('bhjs,bhsv->bhjv', s, vc) + w_inter[..., None] * jnp.einsum('bhjd,bhvd->bhjv', qc, C)
        den = jnp.sum(s, axis=-1) + w_inter * jnp.einsum('bhjd,bhd->bhj', qc, n)
        h = num / jnp.maximum(jnp.abs(den), jnp.exp(-mj))[..., None]
        b_last = b[..., -1]
        g = b_last[..., None] - b + ic
        m_new = jnp.maximum(b_last + m, jnp.max(g, axis=-1))
        decay = jnp.exp(b_last + m - m_new)
        wg = jnp.exp(g - m_new[..., None])
        C_new = decay[..., None, None] * C + jnp.einsum('bhsv,bhsd->bhvd', vc * wg[..., None], kc)
        n_new = decay[..., None] * n + jnp.einsum('bhs,bhsd->bhd', wg, kc)
        return (C_new, n_new, m_new), h

    state, h = lax.scan(step, state, (chunks(q), chunks(k), chunks(v), chunks(logi), chunks(logf)))
    h = jnp.moveaxis(h, 0, 2).reshape(B, H, L, -1)
    return h, state

def mlstm_mixer(u, in_w, conv_w, conv_b, q_w, k_w, v_w, gate_w, gate_b, norm_g, skip, out_w,
                init_f, init_b, need_out=True):
    f32 = jnp.float32
    B, L, _ = u.shape
    xm, o_pre = jnp.split(u @ in_w, 2, axis=-1)
    xc = jax.nn.silu(conv_centred(xm, conv_w, conv_b))
    xc_h = xc.reshape(B, L, M_HEADS, M_DH_IN)
    xm_h = xm.reshape(B, L, M_HEADS, M_DH_IN)
    q = jnp.einsum('blhi,hid->bhld', xc_h, q_w).astype(f32)
    k = (jnp.einsum('blhi,hid->bhld', xc_h, k_w) * (M_DQK ** -0.5)).astype(f32)
    v = jnp.einsum('blhi,hid->bhld', xm_h, v_w).astype(f32)
    gates = (jnp.concatenate([xc, xm], axis=-1) @ gate_w + gate_b).astype(f32)
    gates = gates.reshape(B, L, 4, M_HEADS).transpose(2, 0, 3, 1)
    h_f, st_f = mlstm_scan(q, k, v, gates[0], jax.nn.log_sigmoid(gates[1]), init_f)
    rev = lambda a: jnp.flip(a, axis=2)
    h_b, st_b = mlstm_scan(rev(q), rev(k), rev(v), rev(gates[2]), rev(jax.nn.log_sigmoid(gates[3])), init_b)
    if not need_out:
        return None, st_f, st_b
    h = h_f + rev(h_b)
    mu = jnp.mean(h, axis=-1, keepdims=True)
    var = jnp.mean(jnp.square(h - mu), axis=-1, keepdims=True)
    h = (h - mu) * lax.rsqrt(var + EPS)
    h = h.transpose(0, 2, 1, 3).reshape(B, L, M_INNER).astype(u.dtype)
    y = (h * norm_g + skip * xc) * jax.nn.sigmoid(o_pre)
    return y @ out_w, st_f, st_b

def hyena_filters(L, w1, b1, freq, w2, b2, w3, decay):
    f32 = jnp.float32
    pos = jnp.arange(L, dtype=f32)
    t = pos / max(L - 1, 1)
    bands = jnp.arange(1, H_BANDS + 1, dtype=f32)
    ang = (2.0 * math.pi / L) * pos[:, None] * bands[None, :]
    feat = jnp.concatenate([t[:, None], jnp.cos(ang), jnp.sin(ang)], axis=-1)
    fr = freq.astype(f32)
    z = jnp.sin(fr * (feat @ w1.astype(f32) + b1.astype(f32)))
    z = jnp.sin(fr * (z @ w2.astype(f32) + b2.astype(f32)))
    z = z @ w3.astype(f32)
    tau = jnp.abs(pos - L // 2) / (L / 2)
    filt = z * jnp.exp(-tau[:, None] * decay.astype(f32)[None, :])
    return filt * lax.rsqrt(jnp.sum(filt * filt, axis=0, keepdims=True) + EPS)

def fft_long_conv(u, filt, bias):
    f32 = jnp.float32
    L = u.shape[1]
    n = 2 * L
    uf = u.astype(f32)
    spec = jnp.fft.rfft(uf, n=n, axis=1) * jnp.fft.rfft(filt, n=n, axis=0)[None]
    y = jnp.fft.irfft(spec, n=n, axis=1)[:, L // 2:L // 2 + L]
    return (y + uf * bias.astype(f32)).astype(u.dtype)

def hyena_mixer(u, in_w, in_b, sc_w, sc_b, f_w1, f_b1, f_freq, f_w2, f_b2, f_w3, decay, fbias, out_w, out_b):
    B, L, D = u.shape
    z = conv_centred(u @ in_w + in_b, sc_w, sc_b)
    x1, x2, v = jnp.split(z, 3, axis=-1)
    filt = hyena_filters(L, f_w1, f_b1, f_freq, f_w2, f_b2, f_w3, decay)
    y = x1 * fft_long_conv(v, filt[:, :D], fbias[:D])
    y = x2 * fft_long_conv(y, filt[:, D:], fbias[D:])
    return y @ out_w + out_b

def moe_ffn(xt, rg_w, rg_b, re_w, re_b, w13, w2):
    f32 = jnp.float32
    T, D = xt.shape
    g_prob = jax.nn.softmax((xt @ rg_w + rg_b).astype(f32), axis=-1)
    g_w, g_idx = lax.top_k(g_prob, 1)
    e_logits = (xt @ re_w + re_b).astype(f32).reshape(T, N_GROUPS, EXP_PER_GROUP)
    e_logits = jnp.take_along_axis(e_logits, g_idx[:, :, None], axis=1)[:, 0]
    e_w, e_idx = lax.top_k(jax.nn.softmax(e_logits, axis=-1), TOP_K)
    e_w = e_w / jnp.sum(e_w, axis=-1, keepdims=True)
    weights = (g_w * e_w).reshape(-1)
    experts = (g_idx * EXP_PER_GROUP + e_idx).reshape(-1).astype(jnp.int32)
    A = T * TOP_K
    tok = jnp.arange(A, dtype=jnp.int32) // TOP_K
    order = jnp.argsort(experts)
    s_exp, s_tok, s_w = experts[order], tok[order], weights[order]
    counts = jnp.zeros((N_EXPERTS,), jnp.int32).at[experts].add(1)
    starts = jnp.cumsum(counts) - counts
    padded = (counts + MOE_BLOCK - 1) // MOE_BLOCK * MOE_BLOCK
    p_ends = jnp.cumsum(padded)
    p_starts = p_ends - padded
    dest = p_starts[s_exp] + jnp.arange(A, dtype=jnp.int32) - starts[s_exp]
    n_blocks = -(-A // MOE_BLOCK) + N_EXPERTS
    R = n_blocks * MOE_BLOCK
    row_tok = jnp.zeros((R,), jnp.int32).at[dest].set(s_tok)
    row_w = jnp.zeros((R,), f32).at[dest].set(s_w)
    blk_start = jnp.arange(n_blocks, dtype=jnp.int32) * MOE_BLOCK
    blk_exp = jnp.minimum(jnp.searchsorted(p_ends, blk_start, side='right'), N_EXPERTS - 1)
    xb = xt[row_tok].reshape(n_blocks, MOE_BLOCK, D)

    def expert_block(args):
        xblk, e = args
        gate, up = jnp.split(xblk @ w13[e], 2, axis=-1)
        return (jax.nn.silu(gate) * up) @ w2[e]

    yb = lax.map(expert_block, (xb, blk_exp)).reshape(R, D)
    return jax.ops.segment_sum(yb * row_w[:, None].astype(yb.dtype), row_tok, num_segments=T)

def setup_inputs(seed: int = 0) -> dict:
    key = jax.random.key(seed)
    ks = iter(jax.random.split(key, 64))
    f32 = jnp.float32

    def nrm(shape, scale):
        return scale * jax.random.normal(next(ks), shape, f32)

    D = D_MODEL
    n_a = len(range(0, DEPTH, N_MIXERS))
    n_b = len(range(1, DEPTH, N_MIXERS))
    fgate = jnp.linspace(3.0, 6.0, M_HEADS, dtype=f32)[None]
    decay = jnp.tile(jnp.linspace(H_DECAY_MIN, H_DECAY_MAX, D, dtype=f32), H_ORDER)[None]
    return {
        'x': nrm((BATCH, SEQ, D), 1.0),
        'c': nrm((BATCH, D), 1.0),
        'ctx': nrm((BATCH, CTX_LEN, D), 1.0),
        'c_ctx': nrm((D,), 1.0),
        'ada_w': nrm((DEPTH, D, 6 * D), ADA_SCALE * D ** -0.5),
        'ada_b': nrm((DEPTH, 6 * D), 0.01),
        'norm1_g': 1.0 + nrm((DEPTH, D), 0.02),
        'norm2_g': 1.0 + nrm((DEPTH, D), 0.02),
        'rg_w': nrm((DEPTH, D, N_GROUPS), D ** -0.5),
        'rg_b': nrm((DEPTH, N_GROUPS), 0.01),
        're_w': nrm((DEPTH, D, N_EXPERTS), D ** -0.5),
        're_b': nrm((DEPTH, N_EXPERTS), 0.01),
        'moe_w13': nrm((DEPTH, N_EXPERTS, D, 2 * D_EXPERT), D ** -0.5),
        'moe_w2': nrm((DEPTH, N_EXPERTS, D_EXPERT, D), D_EXPERT ** -0.5),
        'm_in_w': nrm((n_a, D, 2 * M_INNER), D ** -0.5),
        'm_conv_w': nrm((n_a, M_CONV, M_INNER), M_CONV ** -0.5),
        'm_conv_b': nrm((n_a, M_INNER), 0.01),
        'm_q_w': nrm((n_a, M_HEADS, M_DH_IN, M_DQK), M_DH_IN ** -0.5),
        'm_k_w': nrm((n_a, M_HEADS, M_DH_IN, M_DQK), M_DH_IN ** -0.5),
        'm_v_w': nrm((n_a, M_HEADS, M_DH_IN, M_DV), M_DH_IN ** -0.5),
        'm_gate_w': nrm((n_a, 2 * M_INNER, 4 * M_HEADS), 0.1 * (2 * M_INNER) ** -0.5),
        'm_gate_b': jnp.concatenate([nrm((n_a, M_HEADS), 0.1), fgate + nrm((n_a, M_HEADS), 0.1),
                                     nrm((n_a, M_HEADS), 0.1), fgate + nrm((n_a, M_HEADS), 0.1)], axis=-1),
        'm_norm_g': 1.0 + nrm((n_a, M_INNER), 0.02),
        'm_skip': 1.0 + nrm((n_a, M_INNER), 0.02),
        'm_out_w': nrm((n_a, M_INNER, D), M_INNER ** -0.5),
        'h_in_w': nrm((n_b, D, 3 * D), D ** -0.5),
        'h_in_b': nrm((n_b, 3 * D), 0.01),
        'h_sc_w': nrm((n_b, H_SCONV, 3 * D), H_SCONV ** -0.5),
        'h_sc_b': nrm((n_b, 3 * D), 0.01),
        'h_f_w1': nrm((n_b, H_EMB, H_FH), H_EMB ** -0.5),
        'h_f_b1': nrm((n_b, H_FH), 0.1),
        'h_f_freq': 1.0 + nrm((n_b, H_FH), 0.02),
        'h_f_w2': nrm((n_b, H_FH, H_FH), H_FH ** -0.5),
        'h_f_b2': nrm((n_b, H_FH), 0.1),
        'h_f_w3': nrm((n_b, H_FH, H_ORDER * D), H_FH ** -0.5),
        'h_decay': decay + nrm((n_b, H_ORDER * D), 0.05),
        'h_fbias': nrm((n_b, H_ORDER * D), 0.5),
        'h_out_w': nrm((n_b, D, D), D ** -0.5),
        'h_out_b': nrm((n_b, D), 0.01),
        'final_g': 1.0 + nrm((D,), 0.02),
    }

def reference(x, c, ctx, c_ctx, ada_w, ada_b, norm1_g, norm2_g, rg_w, rg_b, re_w, re_b, moe_w13, moe_w2,
              m_in_w, m_conv_w, m_conv_b, m_q_w, m_k_w, m_v_w, m_gate_w, m_gate_b, m_norm_g, m_skip, m_out_w,
              h_in_w, h_in_b, h_sc_w, h_sc_b, h_f_w1, h_f_b1, h_f_freq, h_f_w2, h_f_b2, h_f_w3, h_decay,
              h_fbias, h_out_w, h_out_b, final_g):
    B, S, D = x.shape
    n_ctx = ctx.shape[1]
    hl, hc = x, ctx
    for i in range(DEPTH):
        kind = i % N_MIXERS
        slot = i // N_MIXERS
        col_major = (slot % 2) == 1
        ctx_live = any(j % N_MIXERS == 0 for j in range(i + 1, DEPTH))
        ml = (jax.nn.silu(c) @ ada_w[i] + ada_b[i])[:, None, :]
        mc = (jax.nn.silu(c_ctx) @ ada_w[i] + ada_b[i])[None, None, :]
        sh1, sc1, g1, sh2, sc2, g2 = jnp.split(ml, 6, axis=-1)
        csh1, csc1, cg1, csh2, csc2, cg2 = jnp.split(mc, 6, axis=-1)

        ul = to_scan_order(rmsnorm(hl, norm1_g[i]) * (1.0 + sc1) + sh1, col_major)
        if kind == 0 or ctx_live:
            uc = rmsnorm(hc, norm1_g[i]) * (1.0 + csc1) + csh1
        if kind == 0:
            mp = (m_in_w[slot], m_conv_w[slot], m_conv_b[slot], m_q_w[slot], m_k_w[slot], m_v_w[slot],
                  m_gate_w[slot], m_gate_b[slot], m_norm_g[slot], m_skip[slot], m_out_w[slot])
            yc, st_f, st_b = mlstm_mixer(uc, *mp, zero_state(B), zero_state(B), need_out=ctx_live)
            yl, _, _ = mlstm_mixer(ul, *mp, st_f, st_b)
        else:
            hp = (h_in_w[slot], h_in_b[slot], h_sc_w[slot], h_sc_b[slot], h_f_w1[slot], h_f_b1[slot],
                  h_f_freq[slot], h_f_w2[slot], h_f_b2[slot], h_f_w3[slot], h_decay[slot], h_fbias[slot],
                  h_out_w[slot], h_out_b[slot])
            yl = hyena_mixer(ul, *hp)
            if ctx_live:
                yc = hyena_mixer(uc, *hp)
        hl = hl + g1 * from_scan_order(yl, col_major)
        if ctx_live:
            hc = hc + cg1 * yc

        mo = (rg_w[i], rg_b[i], re_w[i], re_b[i], moe_w13[i], moe_w2[i])
        vl = rmsnorm(hl, norm2_g[i]) * (1.0 + sc2) + sh2
        if ctx_live:
            vc = rmsnorm(hc, norm2_g[i]) * (1.0 + csc2) + csh2
            toks = jnp.concatenate([vc, vl], axis=1).reshape(-1, D)
            out = moe_ffn(toks, *mo).reshape(B, n_ctx + S, D)
            hc = hc + cg2 * out[:, :n_ctx]
            hl = hl + g2 * out[:, n_ctx:]
        else:
            hl = hl + g2 * moe_ffn(vl.reshape(-1, D), *mo).reshape(B, S, D)
    return rmsnorm(hl, final_g)


_drawn_inputs = setup_inputs


def setup_inputs(seed=0):
    import zlib

    import numpy as np

    out = dict(_drawn_inputs(seed))
    spreads = {}
    factors = {'norm2_g': 3.018,
     'rg_b': 6.769,
     're_b': 7.251,
     'm_conv_b': 4.782,
     'm_gate_w': 3.115,
     'm_norm_g': 4.306,
     'm_skip': 8.0,
     'h_out_b': 8.0,
     'final_g': 2.739}
    for name, (base, spread) in spreads.items():
        noise = np.random.default_rng([zlib.crc32(name.encode()), seed]).standard_normal(out[name].shape)
        drawn = base * np.exp(spread * noise) if base else spread * noise
        out[name] = jnp.asarray(drawn.astype(out[name].dtype))
    for name, factor in factors.items():
        out[name] = (out[name] * factor).astype(out[name].dtype)
    return out
```

```python
from contextlib import ExitStack

import numpy as np

import concourse.bass as bass
from concourse import mybir

F32 = mybir.dt.float32
I32 = mybir.dt.int32
ALU = mybir.AluOpType
ACT = mybir.ActivationFunctionType
AXX = mybir.AxisListType.X

P = 128
D = 1024
KD = D // P
SEQ = 512
CTX = 256
TL = SEQ // P
TC = CTX // P
TA = TL + TC
NTOK = SEQ + CTX
EPS = 1e-6
HEADS = 4
INNER = 2048
DH = INNER // HEADS
FT = DH // P
DQK = 256
QT = DQK // P
NE = 32
NGRP = 4
DE = 512
NOV = 7
NBLK = NE + NOV
NC3 = 3 * D
FREQ = 384
HFH = 64
HEMB = 33
WCH = 4096
XMW = 1 + CTX + 1 + SEQ + 1
XCW = XMW - 2
LAT0 = CTX + 1


class Counter:

    def __init__(self, eng, sem):
        self.eng, self.sem, self.base, self.n = eng, sem, 0, 0

    def __call__(self, ins):
        self.n += 1
        ins.then_inc(self.sem, 1)
        self.eng.wait_ge(self.sem, self.base + self.n)

    def enter(self, it, per):
        self.keep = (self.base, self.n)
        self.base, self.n = self.base + self.n + it * per, 0

    def leave(self, times, per):
        assert self.n == per, (self.n, per)
        self.base, self.n = self.keep[0], self.keep[1] + times * per


RSQ_STEPS = 2 + 3 * 4


def rsqrt(v, own, r, x, tmp):
    ri, xi = r.bitcast(I32), x.bitcast(I32)
    own(v.tensor_scalar(ri, xi, 1, None, ALU.arith_shift_right))
    own(v.tensor_scalar(ri, ri, -1, 0x5F3759DF, ALU.mult, ALU.add))
    for i in range(4):
        own(v.tensor_tensor(tmp, r, r, ALU.mult))
        own(v.scalar_tensor_tensor(out=tmp, in0=x, scalar=-0.5, in1=tmp, op0=ALU.mult, op1=ALU.mult))
        own(v.scalar_tensor_tensor(out=x if i == 3 else r, in0=tmp, scalar=1.5, in1=r, op0=ALU.add, op1=ALU.mult))


def build(nc, I, out, dbg=None, stop=99):
    top = ExitStack()
    with top:
        live = [[]]

        def sem(name):
            live[-1].append(nc.alloc_semaphore(name=name))
            return live[-1][-1]

        def retire():
            if done := live.pop():
                nc.clear_and_free_semaphores(done)
                nc.all_engine_barrier()

        def stage():
            live.append([])
            ctx = ExitStack()
            ctx.callback(retire)
            return ctx

        def sbt(ctx, name, shape, dt=F32):
            return ctx.enter_context(nc.sbuf_tensor(name, shape, dt))

        def dram(name, shape, dt=F32):
            return nc.dram_tensor(name, shape, dt, kind="Internal").ap()

        bank = [top.enter_context(nc.psum_tensor(f"bank{i}", [P, 512], F32)) for i in range(8)]
        ident = sbt(top, "ident", [P, P])
        ones = sbt(top, "onesmat", [P, P])
        upper = sbt(top, "upper", [P, P])
        hl = sbt(top, "hl", [P, TL, D])

        d_mod = [dram(f"d_mod{i}", [1, 6 * D]) for i in range(2)]
        d_modc = dram("d_modc", [1, 2 * D])
        d_xm = dram("d_xm", [HEADS * FT, P, XMW])
        d_xc = dram("d_xc", [HEADS * FT, P, XCW])
        d_negm = dram("d_negm", [HEADS, 2 * SEQ])
        d_v = [dram(f"d_v{i}", [SEQ, D]) for i in range(2)]
        d_tab = [dram(f"d_tab{i}", [NBLK * P, 1]) for i in range(2)]
        d_y = [dram(f"d_y{i}", [NBLK * P, D]) for i in range(2)]

        d_filt = dram("d_filt", [SEQ, 2 * D])

        def row_bcast(src_row):
            return src_row.to_broadcast([P, src_row.shape[1]])

        def feat_cols(src_row):
            return src_row.rearrange("o (f p) -> p (o f)", p=P)

        def residual(dve, own, src, ready, gate, tmp):
            v = nc.vector
            for g in range(2 * TL):
                t, n = g // 2, g % 2
                cs = slice(n * 512, (n + 1) * 512)
                dve.wait_ge(ready, g + 1)
                own(v.tensor_tensor(tmp[:, n, :], src[g][:], gate[:, cs], ALU.mult))
                own(v.tensor_tensor(hl[:, t, cs], hl[:, t, cs], tmp[:, n, :], ALU.add))

        def expert_ffn(l):
            with stage() as c:
                w13 = [sbt(c, f"w13_{l}{u}", [P, KD, 2 * DE]) for u in range(2)]
                w2 = [sbt(c, f"w2_{l}{u}", [P, DE // P, D]) for u in range(2)]
                tokc = sbt(c, f"tokc{l}", [P, NBLK], I32)
                sli = sbt(c, f"sli{l}", [P, TL * 2], I32)
                wts = sbt(c, f"wts{l}", [P, 2, TL])
                meta = sbt(c, f"meta{l}", [P, 1 + NOV], I32)
                s_w13 = [sem(f"s_w13_{l}{u}") for u in range(2)]
                s_w2 = [sem(f"s_w2_{l}{u}") for u in range(2)]
                w13v = I["moe_w13"][l].rearrange("e (k p) n -> p e k n", p=P)
                w2v = I["moe_w2"][l].rearrange("e (k p) n -> p e k n", p=P)
                route(l, w13, w2, w13v, w2v, s_w13, s_w2, tokc, sli, wts, meta)
                if dbg is not None and stop == 4.5:
                    dump(nc, dbg, sem, [("o_tokc", tokc[:]), ("o_sli", sli[:]), ("o_wts", wts[:].rearrange("p a b -> p (a b)")), ("o_meta", meta[:])], [("o_v", d_v[0])])
                experts(l, w13, w2, w13v, w2v, s_w13, s_w2, tokc, meta)
            with stage() as c:
                yg = [sbt(c, f"yg{l}{i}", [P, D]) for i in range(2 * TL)]
                g2b = sbt(c, f"g2b{l}", [P, D])
                s_yg = [sem(f"s_yg{l}{i}") for i in range(2 * TL)]
                s_g2 = sem(f"s_g2{l}"); s_dc = sem(f"s_dc{l}"); s_c1 = sem(f"s_c1{l}")
                blk = c.enter_context(nc.Block())

                @blk.sync
                def _(sp):
                    sp.dma_start(g2b[:], row_bcast(d_mod[l][:, 5 * D:6 * D])).then_inc(s_g2, 16)

                @blk.gpsimd
                def _(pool):
                    for i in range(2 * TL):
                        nc.gpsimd.indirect_dma_start(yg[i][:], None, d_y[l], bass.IndirectOffsetOnAxis(sli[:, i:i + 1], 0)).then_inc(s_yg[i], 16)

                @blk.scalar
                def _(act):
                    for t in range(TL):
                        act.wait_ge(s_yg[2 * t], 16)
                        nc.scalar.activation(yg[2 * t][:], yg[2 * t][:], ACT.Copy, scale=wts[:, 0, t:t + 1]).then_inc(s_c1, 1)

                @blk.vector
                def _(dve):
                    v = nc.vector
                    own = Counter(dve, s_dc)
                    dve.wait_ge(s_g2, 16)
                    for t in range(TL):
                        dve.wait_ge(s_c1, t + 1)
                        dve.wait_ge(s_yg[2 * t + 1], 16)
                        y = yg[2 * t][:]
                        own(v.scalar_tensor_tensor(out=y, in0=yg[2 * t + 1][:], scalar=wts[:, 1, t:t + 1], in1=y, op0=ALU.mult, op1=ALU.add))
                        own(v.tensor_tensor(y, y, g2b[:], ALU.mult))
                        own(v.tensor_tensor(hl[:, t, :], hl[:, t, :], y, ALU.add))

        def route(l, w13, w2, w13v, w2v, s_w13, s_w2, tokc, sli, wts, meta):
            with stage() as c:
                def T(name, shape, dt=F32):
                    return sbt(c, f"{name}{l}r", shape, dt)

                A2 = T("A2", [P, D]); n2b = T("n2b", [P, D]); shb = T("shb", [P, D]); junk = T("junk", [P, D])
                vt = T("vt", [P, TL, D]); vT = T("vT", [P, KD, SEQ])
                rw = T("rw", [P, KD, NGRP + NE]); rb = T("rb", [P, NGRP + NE])
                ss = T("ss", [P, TL]); r1 = T("r1", [P, TL]); r2 = T("r2", [P, TL])
                zt = T("zt", [NBLK, P]); tabs = T("tabs", [NBLK, P]); tokid = T("tokid", [P, TL])
                ei = T("ei", [P, TL, NE])
                LG = T("LG", [P, TL, NGRP]); LE = T("LE", [P, TL, NE])
                eg = T("eg", [P, TL, NGRP]); t4 = T("t4", [P, TL, NGRP]); ohg = T("ohg", [P, TL * NGRP, 1])
                t32 = T("t32", [P, TL, NE]); oh = [T(f"oh{i}", [P, TL, NE]) for i in range(2)]; sel = T("sel", [P, TL, NE])
                m = T("m", [P, TL, 1]); m1 = T("m1", [P, TL, 1]); m2 = T("m2", [P, TL, 1]); gs = T("gs", [P, TL, 1]); ex = T("ex", [P, TL, 1])
                cnt = T("cnt", [P, NE]); nov = T("nov", [P, NE]); ov = T("ov", [P, NE]); De = T("De", [P, NE]); one32 = T("one32", [P, NE])
                slot = T("slot", [P, TL, NE]); slf = T("slf", [P, TL, 2, 1]); mf = T("mf", [P, 1 + NOV]); cmp = T("cmp", [P, NE])
                S = {k: sem(f"s_{k}_l{l}") for k in "rows rld sq vtile vst vps vT lps eg1 eg2 ex1 ex2 sel rk sl pl dv zst sc tl tps iot".split()}
                blk = c.enter_context(nc.Block())

                @blk.sync
                def _(sp):
                    for dst, src in ((n2b, I["norm2_g"][l:l + 1, :]), (A2, d_mod[l][:, 4 * D:5 * D]), (shb, d_mod[l][:, 3 * D:4 * D])):
                        sp.dma_start(dst[:], row_bcast(src)).then_inc(S["rows"], 16)
                    sp.dma_start(rw[:, :, 0:NGRP], I["rg_w"][l].rearrange("(k p) n -> p k n", p=P)).then_inc(S["rld"], 16)
                    sp.dma_start(rw[:, :, NGRP:], I["re_w"][l].rearrange("(k p) n -> p k n", p=P)).then_inc(S["rld"], 16)
                    sp.dma_start(rb[:, 0:NGRP], row_bcast(I["rg_b"][l:l + 1, :])).then_inc(S["rld"], 16)
                    sp.dma_start(rb[:, NGRP:], row_bcast(I["re_b"][l:l + 1, :])).then_inc(S["rld"], 16)
                    for u in range(2):
                        sp.dma_start(w13[u][:], w13v[:, u]).then_inc(s_w13[u], 16)
                        sp.dma_start(w2[u][:], w2v[:, u]).then_inc(s_w2[u], 16)

                @blk.gpsimd
                def _(pool):
                    g = nc.gpsimd
                    g.memset(zt[:], 0.0).then_inc(S["pl"], 1)
                    g.iota(tokid[:], [[P, TL]], base=0, channel_multiplier=1, allow_small_or_imprecise_dtypes=True).then_inc(S["iot"], 1)
                    g.iota(ei[:], [[0, TL], [1, NE]], base=0, channel_multiplier=0, allow_small_or_imprecise_dtypes=True).then_inc(S["iot"], 1)
                    pool.wait_ge(S["pl"], 1)
                    pool.dma_start(d_tab[l].rearrange("(b p) o -> b (p o)", p=P), zt[:]).then_inc(S["zst"], 16)
                    for t in range(TL):
                        pool.wait_ge(S["vtile"], t + 1)
                        pool.dma_start(d_v[l][t * P:(t + 1) * P, :], vt[:, t, :]).then_inc(S["vst"], 16)
                    pool.wait_ge(S["zst"], 16)
                    pool.wait_ge(S["iot"], 2)
                    pool.wait_ge(S["sl"], 1)
                    for t in range(TL):
                        for k in range(2):
                            g.indirect_dma_start(d_tab[l], bass.IndirectOffsetOnAxis(sli[:, 2 * t + k:2 * t + k + 1], 0), tokid[:, t:t + 1], None).then_inc(S["sc"], 16)
                    pool.wait_ge(S["sc"], 16 * 2 * TL)
                    pool.dma_start(tabs[:], d_tab[l].rearrange("(b p) o -> b (p o)", p=P)).then_inc(S["tl"], 16)
                    pool.wait_ge(S["vst"], 16 * TL)

                @blk.scalar
                def _(act):
                    a = nc.scalar
                    for t in range(TL):
                        act.wait_ge(S["sq"], t)
                        a.activation(junk[:], hl[:, t, :], ACT.Square, accum_out=ss[:, t:t + 1]).then_inc(S["sq"], 1)
                    for k in range(KD):
                        act.wait_ge(S["vps"], k + 1)
                        a.activation(vT[:, k, :], bank[k % 2][:], ACT.Copy).then_inc(S["vT"], 1)
                    act.wait_ge(S["eg1"], 1)
                    a.activation(eg[:], eg[:], ACT.Exp).then_inc(S["eg2"], 1)
                    act.wait_ge(S["ex1"], 1)
                    a.activation(ex[:], ex[:], ACT.Exp).then_inc(S["ex2"], 1)

                @blk.tensor
                def _(pe):
                    t_ = nc.tensor
                    pe.wait_ge(S["vtile"], TL)
                    for k in range(KD):
                        if k >= 2:
                            pe.wait_ge(S["vT"], k - 1)
                        for t in range(TL):
                            ins = t_.transpose(bank[k % 2][:, t * P:(t + 1) * P], vt[:, t, k * P:(k + 1) * P], ident[:])
                        ins.then_inc(S["vps"], 1)
                    pe.wait_ge(S["vT"], KD)
                    pe.wait_ge(S["rld"], 64)
                    for t in range(TL):
                        for k in range(KD):
                            ins = t_.matmul(bank[2 + t][:, 0:NGRP + NE], vT[:, k, t * P:(t + 1) * P], rw[:, k, :], start=(k == 0), stop=(k == KD - 1))
                        ins.then_inc(S["lps"], 1)
                    pe.wait_ge(S["sel"], 1)
                    for j in range(TL):
                        for i in range(j + 1):
                            t_.matmul(bank[6][:, j * NE:(j + 1) * NE], (upper if i == j else ones)[:], sel[:, i, :], start=(i == 0), stop=(i == j))
                    for i in range(TL):
                        ins = t_.matmul(bank[7][:, 0:NE], ones[:], sel[:, i, :], start=(i == 0), stop=(i == TL - 1))
                    ins.then_inc(S["rk"], 1)
                    pe.wait_ge(S["tl"], 16)
                    t_.transpose(bank[0][:, 0:NBLK], tabs[:], ident[0:NBLK, 0:NBLK]).then_inc(S["tps"], 1)

                @blk.vector
                def _(dve):
                    v = nc.vector
                    own = Counter(dve, S["dv"])
                    dve.wait_ge(S["rows"], 48)
                    own(v.scalar_tensor_tensor(out=A2[:], in0=A2[:], scalar=1.0, in1=n2b[:], op0=ALU.add, op1=ALU.mult))
                    dve.wait_ge(S["sq"], TL)
                    own(v.tensor_scalar(ss[:], ss[:], 1.0 / D, EPS, ALU.mult, ALU.add))
                    rsqrt(v, own, r1[:], ss[:], r2[:])
                    for t in range(TL):
                        own(v.scalar_tensor_tensor(out=vt[:, t, :], in0=hl[:, t, :], scalar=ss[:, t:t + 1], in1=A2[:], op0=ALU.mult, op1=ALU.mult))
                        v.tensor_tensor(vt[:, t, :], vt[:, t, :], shb[:], ALU.add).then_inc(S["vtile"], 1)
                    own(v.memset(one32[:], 1.0))
                    dve.wait_ge(S["iot"], 2)
                    for t in range(TL):
                        dve.wait_ge(S["lps"], t + 1)
                        v.tensor_tensor(LG[:, t, :], bank[2 + t][:, 0:NGRP], rb[:, 0:NGRP], ALU.add)
                        own(v.tensor_tensor(LE[:, t, :], bank[2 + t][:, NGRP:NGRP + NE], rb[:, NGRP:], ALU.add))

                    def first_max(x, n, mx, scratch, hot):
                        own(v.tensor_reduce(mx, x, AXX, ALU.max))
                        own(v.tensor_tensor(scratch, x, mx.to_broadcast([P, TL, n]), ALU.is_equal))
                        own(v.scalar_tensor_tensor(out=scratch, in0=scratch, scalar=-64.0, in1=ei[:, :, 0:n], op0=ALU.mult, op1=ALU.add))
                        own(v.tensor_reduce(m[:], scratch, AXX, ALU.min))
                        own(v.tensor_tensor(hot, scratch, m[:].to_broadcast([P, TL, n]), ALU.is_equal))

                    first_max(LG[:], NGRP, gs[:], t4[:], ohg[:].rearrange("p (t g) o -> p t (g o)", g=NGRP))
                    v.tensor_tensor(eg[:], LG[:], gs[:].to_broadcast([P, TL, NGRP]), ALU.subtract).then_inc(S["eg1"], 1)
                    own(v.tensor_scalar(ohg[:], ohg[:], 1e30, -1e30, ALU.mult, ALU.add))
                    le = LE[:].rearrange("p t (g e) -> p (t g) e", g=NGRP)
                    own(v.tensor_tensor(le, le, ohg[:].to_broadcast([P, TL * NGRP, NE // NGRP]), ALU.add))
                    first_max(LE[:], NE, m1[:], t32[:], oh[0][:])
                    own(v.scalar_tensor_tensor(out=LE[:], in0=oh[0][:], scalar=-3e30, in1=LE[:], op0=ALU.mult, op1=ALU.add))
                    first_max(LE[:], NE, m2[:], t32[:], oh[1][:])
                    v.tensor_tensor(sel[:], oh[0][:], oh[1][:], ALU.add).then_inc(S["sel"], 1)
                    v.tensor_tensor(ex[:], m2[:], m1[:], ALU.subtract).then_inc(S["ex1"], 1)
                    dve.wait_ge(S["eg2"], 1)
                    own(v.tensor_reduce(gs[:], eg[:], AXX, ALU.add))
                    dve.wait_ge(S["ex2"], 1)
                    own(v.scalar_tensor_tensor(out=m[:], in0=ex[:], scalar=1.0, in1=gs[:], op0=ALU.add, op1=ALU.mult))
                    own(v.reciprocal(wts[:, 0, :], m[:].rearrange("p t o -> p (t o)")))
                    own(v.tensor_tensor(wts[:, 1, :], wts[:, 0, :], ex[:].rearrange("p t o -> p (t o)"), ALU.mult))
                    dve.wait_ge(S["rk"], 1)
                    own(v.tensor_copy(cnt[:], bank[7][:, 0:NE]))
                    own(v.tensor_scalar(nov[:], cnt[:], float(P), None, ALU.is_gt))
                    for k in (2, 3):
                        own(v.scalar_tensor_tensor(out=nov[:], in0=cnt[:], scalar=float(k * P), in1=nov[:], op0=ALU.is_gt, op1=ALU.add))
                    own(v.tensor_tensor_scan(out=ov[:], data0=one32[:], data1=nov[:], initial=0.0, op0=ALU.mult, op1=ALU.add))
                    own(v.tensor_tensor(De[:], ov[:], nov[:], ALU.subtract))
                    own(v.tensor_tensor(De[:], De[:], ei[:, 0, :], ALU.subtract))
                    own(v.tensor_scalar(De[:], De[:], float(P), float(P * (NE - 1)), ALU.mult, ALU.add))
                    own(v.tensor_copy(slot[:].rearrange("p t e -> p (t e)"), bank[6][:, 0:TL * NE]))
                    for t in range(TL):
                        own(v.scalar_tensor_tensor(out=t32[:, t, :], in0=slot[:, t, :], scalar=float(P), in1=De[:], op0=ALU.is_ge, op1=ALU.mult))
                    own(v.tensor_tensor(slot[:], slot[:], t32[:], ALU.add))
                    own(v.scalar_tensor_tensor(out=slot[:], in0=ei[:], scalar=float(P), in1=slot[:], op0=ALU.mult, op1=ALU.add))
                    for k in range(2):
                        own(v.tensor_tensor(t32[:], oh[k][:], slot[:], ALU.mult))
                        own(v.tensor_reduce(slf[:, :, k, :], t32[:], AXX, ALU.add))
                    v.tensor_copy(sli[:], slf[:].rearrange("p t k o -> p (t k o)")).then_inc(S["sl"], 1)
                    v.tensor_copy(mf[:, 0:1], ov[:, NE - 1:NE])
                    for o in range(NOV):
                        own(v.tensor_scalar(cmp[:], ov[:], float(o), None, ALU.is_le))
                        own(v.tensor_reduce(mf[:, 1 + o:2 + o], cmp[:], AXX, ALU.add))
                    own(v.tensor_scalar(mf[:], mf[:], float(NE - 1), None, ALU.min))
                    own(v.tensor_copy(meta[:], mf[:]))
                    dve.wait_ge(S["tps"], 1)
                    own(v.tensor_copy(tokc[:], bank[0][:, 0:NBLK]))

        def experts(l, w13, w2, w13v, w2v, s_w13, s_w2, tokc, meta):
            with stage() as c:
                def T(name, shape, dt=F32):
                    return sbt(c, f"{name}{l}e", shape, dt)

                xg = [T(f"xg{u}", [P, D]) for u in range(2)]
                idxb = [T(f"idxb{u}", [P, 1], I32) for u in range(2)]
                pad = T("pad", [P, 2])
                xT = T("xT", [P, KD, P]); sg = T("sg", [P, DE]); hb = T("hb", [P, DE]); hT = T("hT", [P, DE // P, P])
                yb = [T(f"yb{u}", [P, D]) for u in range(2)]
                S = {k: sem(f"s_{k}_l{l}") for k in "xps xTa xTv gp up sg h hps hT yp0 yp1 ya yv ix "
                     "ox ow oxps oxT og osg oh ohps ohT oyp oy oyst oix".split()}
                s_xg = [sem(f"s_xg{l}{u}") for u in range(2)]
                s_yst = [sem(f"s_yst{l}{u}") for u in range(2)]
                yv_ = d_y[l].rearrange("(b p) d -> b p d", p=P)
                b_g, b_u, b_x, b_h, b_y = bank[0], bank[1], (bank[2], bank[3]), bank[4], (bank[5], bank[6])
                blk = c.enter_context(nc.Block())

                def extra(eng, reg, body):
                    with eng.Fori(0, NOV) as o:
                        with eng.If(reg > o):
                            body(o)

                @blk.sync
                def _(sp):
                    with sp.Fori(1, NE // 2) as it:
                        for u in range(2):
                            b = it * 2 + u
                            sp.wait_ge(S["up"], b - 1)
                            sp.dma_start(w13[u][:], w13v[:, bass.ds(b, 1)].rearrange("p o k n -> p (o k) n")).then_inc(s_w13[u], 16)
                            sp.wait_ge(S["yp1"], b - 1)
                            sp.dma_start(w2[u][:], w2v[:, bass.ds(b, 1)].rearrange("p o k n -> p (o k) n")).then_inc(s_w2[u], 16)
                    sp.wait_ge(S["yp1"], NE)
                    total = sp.value_load(meta[0:1, 0:1], min_val=0, max_val=NOV)

                    def body(o):
                        sp.wait_ge(S["oyst"], 16 * o)
                        sp.wait_ge(S["yp1"], NE)
                        e = sp.value_load(meta[0:1, bass.ds(o + 1, 1)], min_val=0, max_val=NE - 1)
                        sp.dma_start(w13[0][:], w13v[:, bass.ds(e, 1)].rearrange("p o k n -> p (o k) n")).then_inc(S["ow"], 16)
                        sp.dma_start(w2[0][:], w2v[:, bass.ds(e, 1)].rearrange("p o k n -> p (o k) n")).then_inc(S["ow"], 16)

                    extra(sp, total, body)

                @blk.gpsimd
                def _(pool):
                    g = nc.gpsimd

                    def gather(u, done):
                        pool.wait_ge(S["ix"], done)
                        g.tensor_tensor(pad[:], ident[:, 0:2], ident[:, 0:2], ALU.add)
                        g.indirect_dma_start(xg[u][:], None, d_v[l], bass.IndirectOffsetOnAxis(idxb[u][:, 0:1], 0)).then_inc(s_xg[u], 16)

                    for u in range(2):
                        g.tensor_copy(idxb[u][:], tokc[:, u:u + 1]).then_inc(S["ix"], 1)
                        gather(u, u + 1)
                    with pool.Fori(1, NE // 2) as it:
                        for u in range(2):
                            b = it * 2 + u
                            pool.wait_ge(s_xg[u], 16 * it)
                            pool.wait_ge(S["xps"], 2 * b - 2)
                            g.tensor_copy(idxb[u][:], tokc[:, bass.ds(b, 1)]).then_inc(S["ix"], 1)
                            gather(u, b + 1)
                    total = pool.value_load(meta[0:1, 0:1], min_val=0, max_val=NOV)

                    def body(o):
                        pool.wait_ge(S["oyst"], 16 * o)
                        pool.wait_ge(S["xps"], 2 * NE)
                        g.tensor_copy(idxb[0][:], tokc[:, bass.ds(o + NE, 1)]).then_inc(S["oix"], 1)
                        pool.wait_ge(S["oix"], o + 1)
                        g.tensor_tensor(pad[:], ident[:, 0:2], ident[:, 0:2], ALU.add)
                        g.indirect_dma_start(xg[0][:], None, d_v[l], bass.IndirectOffsetOnAxis(idxb[0][:, 0:1], 0)).then_inc(S["ox"], 16)

                    extra(pool, total, body)

                @blk.tensor
                def _(pe):
                    t_ = nc.tensor

                    def x_transposes(u, done):
                        for half in range(2):
                            for k in range(KD // 2):
                                kk = half * (KD // 2) + k
                                ins = t_.transpose(b_x[half][:, k * P:(k + 1) * P], xg[u][:, kk * P:(kk + 1) * P], ident[:])
                            ins.then_inc(done, 1)

                    def product1(bnk, w, n):
                        for k in range(KD):
                            ins = t_.matmul(bnk[:], xT[:, k, :], w[:, k, n * DE:(n + 1) * DE], start=(k == 0), stop=(k == KD - 1))
                        return ins

                    def h_transposes(done):
                        for k in range(DE // P):
                            ins = t_.transpose(b_h[:, k * P:(k + 1) * P], hb[:, k * P:(k + 1) * P], ident[:])
                        ins.then_inc(done, 1)

                    def product2(w, n):
                        for k in range(DE // P):
                            ins = t_.matmul(b_y[n][:], hT[:, k, :], w[:, k, n * 512:(n + 1) * 512], start=(k == 0), stop=(k == DE // P - 1))
                        return ins

                    def block(it, u, last=False):
                        b = it * 2 + u
                        pe.wait_ge(S["xTa"], b + 1)
                        pe.wait_ge(S["xTv"], b + 1)
                        pe.wait_ge(s_w13[u], 16 * it + 16)
                        pe.wait_ge(S["sg"], b)
                        product1(b_g, w13[u], 0).then_inc(S["gp"], 1)
                        pe.wait_ge(S["h"], b)
                        product1(b_u, w13[u], 1).then_inc(S["up"], 1)
                        if not last:
                            pe.wait_ge(s_xg[1 - u], 16 * it + 16 + 16 * u)
                            x_transposes(1 - u, S["xps"])
                        pe.wait_ge(S["hT"], b)
                        pe.wait_ge(S["h"], b + 1)
                        h_transposes(S["hps"])
                        pe.wait_ge(s_w2[u], 16 * it + 16)
                        pe.wait_ge(S["hT"], b + 1)
                        pe.wait_ge(S["ya"], b)
                        product2(w2[u], 0).then_inc(S["yp0"], 1)
                        pe.wait_ge(S["yv"], b)
                        product2(w2[u], 1).then_inc(S["yp1"], 1)

                    pe.wait_ge(s_xg[0], 16)
                    x_transposes(0, S["xps"])
                    with pe.Fori(0, NE // 2 - 1) as it:
                        for u in range(2):
                            block(it, u)
                    block(NE // 2 - 1, 0)
                    block(NE // 2 - 1, 1, last=True)
                    total = pe.value_load(meta[0:1, 0:1], min_val=0, max_val=NOV)

                    def body(o):
                        pe.wait_ge(S["ox"], 16 * o + 16)
                        x_transposes(0, S["oxps"])
                        pe.wait_ge(S["oxT"], o + 1)
                        pe.wait_ge(S["ow"], 32 * o + 32)
                        product1(b_g, w13[0], 0)
                        product1(b_u, w13[0], 1).then_inc(S["og"], 1)
                        pe.wait_ge(S["oh"], o + 1)
                        h_transposes(S["ohps"])
                        pe.wait_ge(S["ohT"], o + 1)
                        product2(w2[0], 0)
                        product2(w2[0], 1).then_inc(S["oyp"], 1)

                    pe.wait_ge(S["yv"], NE)
                    pe.wait_ge(S["ya"], NE)
                    extra(pe, total, body)

                @blk.scalar
                def _(act):
                    a = nc.scalar

                    def x_half(done):
                        act.wait_ge(S["xps"], done)
                        a.activation(xT[:, 0:4, :].rearrange("p k n -> p (k n)"), b_x[0][:], ACT.Copy).then_inc(S["xTa"], 1)

                    def block(it, u, last=False):
                        b = it * 2 + u
                        act.wait_ge(S["gp"], b + 1)
                        act.wait_ge(S["h"], b)
                        a.activation(sg[:], b_g[:], ACT.Silu).then_inc(S["sg"], 1)
                        if not last:
                            x_half(2 * b + 3)
                        act.wait_ge(s_yst[u], 16 * it)
                        act.wait_ge(S["yp0"], b + 1)
                        a.activation(yb[u][:, 0:512], b_y[0][:], ACT.Copy).then_inc(S["ya"], 1)
                        act.wait_ge(S["ya"], b + 1)
                        act.wait_ge(S["yv"], b + 1)
                        act.wait_ge(S["xTa"], 1)
                        act.dma_start(yv_[bass.ds(b, 1)].rearrange("o p d -> (o p) d"), yb[u][:]).then_inc(s_yst[u], 16)

                    x_half(1)
                    with act.Fori(0, NE // 2 - 1) as it:
                        for u in range(2):
                            block(it, u)
                    block(NE // 2 - 1, 0)
                    block(NE // 2 - 1, 1, last=True)
                    for u in range(2):
                        act.wait_ge(s_yst[u], 16 * (NE // 2))
                    total = act.value_load(meta[0:1, 0:1], min_val=0, max_val=NOV)

                    def body(o):
                        act.wait_ge(S["og"], o + 1)
                        a.activation(sg[:], b_g[:], ACT.Silu).then_inc(S["osg"], 1)
                        act.wait_ge(S["oy"], o + 1)
                        act.wait_ge(S["xTa"], 1)
                        act.dma_start(yv_[bass.ds(o + NE, 1)].rearrange("o p d -> (o p) d"), yb[0][:]).then_inc(S["oyst"], 16)
                        act.wait_ge(S["oyst"], 16 * o + 16)
                        a.activation(sg[:, 0:2], ident[:, 0:2], ACT.Copy)

                    extra(act, total, body)

                @blk.vector
                def _(dve):
                    v = nc.vector

                    def x_half(done):
                        dve.wait_ge(S["xps"], done)
                        v.tensor_copy(xT[:, 4:8, :].rearrange("p k n -> p (k n)"), b_x[1][:]).then_inc(S["xTv"], 1)

                    def block(it, u, last=False):
                        b = it * 2 + u
                        dve.wait_ge(S["sg"], b + 1)
                        dve.wait_ge(S["up"], b + 1)
                        dve.wait_ge(S["hps"], b)
                        v.tensor_tensor(hb[:], sg[:], b_u[:], ALU.mult).then_inc(S["h"], 1)
                        if not last:
                            x_half(2 * b + 4)
                        dve.wait_ge(S["yp1"], b)
                        dve.wait_ge(S["hps"], b + 1)
                        v.tensor_copy(hT[:].rearrange("p k n -> p (k n)"), b_h[:]).then_inc(S["hT"], 1)
                        dve.wait_ge(s_yst[u], 16 * it)
                        dve.wait_ge(S["yp1"], b + 1)
                        v.tensor_copy(yb[u][:, 512:1024], b_y[1][:]).then_inc(S["yv"], 1)

                    x_half(2)
                    with dve.Fori(0, NE // 2 - 1) as it:
                        for u in range(2):
                            block(it, u)
                    block(NE // 2 - 1, 0)
                    block(NE // 2 - 1, 1, last=True)
                    total = dve.value_load(meta[0:1, 0:1], min_val=0, max_val=NOV)

                    def body(o):
                        dve.wait_ge(S["oxps"], 2 * o + 2)
                        for half in range(2):
                            ins = v.tensor_copy(xT[:, 4 * half:4 * half + 4, :].rearrange("p k n -> p (k n)"), b_x[half][:])
                        ins.then_inc(S["oxT"], 1)
                        dve.wait_ge(S["osg"], o + 1)
                        v.tensor_tensor(hb[:], sg[:], b_u[:], ALU.mult).then_inc(S["oh"], 1)
                        dve.wait_ge(S["ohps"], o + 1)
                        v.tensor_copy(hT[:].rearrange("p k n -> p (k n)"), b_h[:]).then_inc(S["ohT"], 1)
                        dve.wait_ge(S["oyp"], o + 1)
                        for n in range(2):
                            ins = v.tensor_copy(yb[0][:, n * 512:(n + 1) * 512], b_y[n][:])
                        ins.then_inc(S["oy"], 1)

                    dve.wait_ge(s_yst[0], 16 * (NE // 2))
                    extra(dve, total, body)

        def filters():
            with stage() as c:
                def T(name, shape, dt=F32):
                    return sbt(c, f"{name}f", shape, dt)

                ft = T("ft", [HEMB, SEQ]); w1 = T("w1", [HEMB, HFH]); w2 = T("w2", [HFH, HFH]); w3 = T("w3", [HFH, 2 * D])
                pc = T("pc", [HFH, 3]); z = [T(f"z{i}", [HFH, SEQ]) for i in range(2)]; kx = T("kx", [HFH, SEQ])
                ntau = T("ntau", [P, TL]); dec = T("dec", [P, 2 * D]); E = T("E", [P, 2, 512])
                fl = T("fl", [P, TL, 2 * D]); sq = T("sq", [P, 2, 512]); nrm = T("nrm", [P, 512]); r1 = T("r1", [P, 512]); r2 = T("r2", [P, 512])
                S = {k: sem(f"s_{k}_fl") for k in "ld ps d x zz E g sq sp st fin".split()}
                blk = c.enter_context(nc.Block())
                TWO_PI_HI = 6.28125
                TWO_PI_LO = 2 * np.pi - TWO_PI_HI
                MAGIC = 1.5 * 2.0 ** 23

                @blk.sync
                def _(sp):
                    sp.dma_start(ft[:], I["feat_t"]).then_inc(S["ld"], 16)
                    sp.dma_start(ntau[:], I["neg_tau"]).then_inc(S["ld"], 16)
                    sp.dma_start(w1[:], I["h_f_w1"][0]).then_inc(S["ld"], 16)
                    sp.dma_start(w2[:], I["h_f_w2"][0]).then_inc(S["ld"], 16)
                    sp.dma_start(w3[:], I["h_f_w3"][0]).then_inc(S["ld"], 16)
                    for i, k in enumerate(("h_f_b1", "h_f_b2", "h_f_freq")):
                        sp.dma_start(pc[:, i:i + 1], I[k].rearrange("o p -> p o"), allow_slow_non_contiguous=True).then_inc(S["ld"], 16)
                    sp.dma_start(dec[:], row_bcast(I["h_decay"][0:1, :])).then_inc(S["ld"], 16)
                    for n in range(4):
                        sp.wait_ge(S["fin"], n + 1)
                        sp.dma_start(d_filt.rearrange("(t p) n -> p t n", p=P)[:, :, n * 512:(n + 1) * 512], fl[:, :, n * 512:(n + 1) * 512]).then_inc(S["st"], 16)
                    sp.wait_ge(S["st"], 64)

                @blk.tensor
                def _(pe):
                    t_ = nc.tensor
                    pe.wait_ge(S["ld"], 16 * 9)
                    t_.matmul(bank[0][0:HFH, :], w1[:], ft[:], start=True, stop=True).then_inc(S["ps"], 1)
                    pe.wait_ge(S["zz"], 1)
                    t_.matmul(bank[0][0:HFH, :], w2[:], z[0][:], start=True, stop=True).then_inc(S["ps"], 1)
                    pe.wait_ge(S["zz"], 2)
                    for n in range(4):
                        for t in range(TL):
                            i = n * TL + t
                            if i >= 2:
                                pe.wait_ge(S["g"], i - 1)
                            t_.matmul(bank[1 + i % 2][:], z[1][:, t * P:(t + 1) * P], w3[:, n * 512:(n + 1) * 512], start=True, stop=True).then_inc(S["ps"], 1)
                            if i >= 1:
                                j = i - 1
                                pe.wait_ge(S["sq"], j + 1)
                                t_.matmul(bank[3 + j // TL][:], ones[:], sq[:, j % 2, :], start=(j % TL == 0), stop=(j % TL == TL - 1)).then_inc(S["sp"], 1)
                    pe.wait_ge(S["sq"], 16)
                    t_.matmul(bank[6][:], ones[:], sq[:, 1, :], start=False, stop=True).then_inc(S["sp"], 1)

                @blk.scalar
                def _(act):
                    a = nc.scalar
                    for i in range(2):
                        act.wait_ge(S["x"], i + 1)
                        a.activation(z[i][:], z[i][:], ACT.Sin).then_inc(S["zz"], 1)
                    for i in range(16):
                        n, t = i // TL, i % TL
                        if i >= 2:
                            act.wait_ge(S["g"], i - 1)
                        a.activation(E[:, i % 2, :], dec[:, n * 512:(n + 1) * 512], ACT.Exp, scale=ntau[:, t:t + 1]).then_inc(S["E"], 1)
                        act.wait_ge(S["g"], i + 1)
                        if i >= 2:
                            act.wait_ge(S["sp"], i - 1)
                        a.activation(sq[:, i % 2, :], fl[:, t, n * 512:(n + 1) * 512], ACT.Square).then_inc(S["sq"], 1)

                @blk.vector
                def _(dve):
                    v = nc.vector
                    own = Counter(dve, S["d"])
                    dve.wait_ge(S["ld"], 16 * 9)
                    for i in range(2):
                        dve.wait_ge(S["ps"], i + 1)
                        own(v.tensor_scalar(z[i][:], bank[0][0:HFH, :], pc[:, i:i + 1], pc[:, 2:3], ALU.add, ALU.mult))
                        own(v.tensor_scalar(kx[:], z[i][:], 1 / (2 * np.pi), MAGIC, ALU.mult, ALU.add))
                        own(v.tensor_scalar(kx[:], kx[:], -MAGIC, None, ALU.add))
                        own(v.scalar_tensor_tensor(out=z[i][:], in0=kx[:], scalar=-TWO_PI_HI, in1=z[i][:], op0=ALU.mult, op1=ALU.add))
                        own(v.scalar_tensor_tensor(out=z[i][:], in0=kx[:], scalar=-TWO_PI_LO, in1=z[i][:], op0=ALU.mult, op1=ALU.add))
                        v.tensor_scalar(z[i][:], z[i][:], 3.1415925, -3.1415925, ALU.min, ALU.max).then_inc(S["x"], 1)
                    for n in range(4):
                        for t in range(TL):
                            i = n * TL + t
                            dve.wait_ge(S["ps"], 2 + i + 1)
                            dve.wait_ge(S["E"], i + 1)
                            v.tensor_tensor(fl[:, t, n * 512:(n + 1) * 512], bank[1 + i % 2][:], E[:, i % 2, :], ALU.mult).then_inc(S["g"], 1)
                    for n in range(4):
                        dve.wait_ge(S["sp"], TL * (n + 1))
                        own(v.tensor_scalar(nrm[:], bank[3 + n][:], EPS, None, ALU.add))
                        rsqrt(v, own, r1[:], nrm[:], r2[:])
                        dve.wait_ge(S["sq"], TL * (n + 1))
                        for t in range(TL):
                            ins = v.tensor_tensor(fl[:, t, n * 512:(n + 1) * 512], fl[:, t, n * 512:(n + 1) * 512], nrm[:], ALU.mult)
                        ins.then_inc(S["fin"], 1)
                        dve.wait_ge(S["fin"], n + 1)

        def hyena():
            filters()
            with stage() as c:
                def T(name, shape, dt=F32):
                    return sbt(c, f"{name}h", shape, dt)

                zt = T("zt", [P, TL, NC3])
                hyena_inputs(zt)
                hyena_convs(zt)

        def hyena_inputs(ztok):
            with stage() as c:
                def T(name, shape, dt=F32):
                    return sbt(c, f"{name}i", shape, dt)

                xh = T("xh", [P, TL, D]); uh = T("uh", [P, KD, SEQ]); junk = T("junk", [P, D])
                win = [T(f"win{u}", [P, KD, 512]) for u in range(2)]
                zb = [T(f"zb{u}", [P, SEQ + 2]) for u in range(2)]
                zc = [T(f"zc{u}", [P, SEQ]) for u in range(2)]
                mA = T("mA", [P, KD]); mB = T("mB", [P, KD]); n1 = T("n1", [P, KD])
                ib = T("ib", [P, NC3 // P]); cw = T("cw", [P, 3, NC3 // P]); cb = T("cb", [P, NC3 // P])
                ss = T("ss", [P, TL]); r1 = T("r1", [P, TL]); r2 = T("r2", [P, TL])
                S = {k: sem(f"s_{k}_hi") for k in "ld sq d mod xh xT uh used zps zb cv zt tps pad".split()}
                s_w = [sem(f"s_w_hi{u}") for u in range(2)]
                wv = I["h_in_w"][0].rearrange("(k p) n -> p k n", p=P)
                PER = 4 * 2
                blk = c.enter_context(nc.Block())

                @blk.sync
                def _(sp):
                    for dst, src in ((mB[:], d_mod[1][:, 0:D]), (mA[:], d_mod[1][:, D:2 * D]), (n1[:], I["norm1_g"][1:2, :]), (ib[:], I["h_in_b"][0:1, :]),
                                     (cb[:], I["h_sc_b"][0:1, :]), *((cw[:, k, :], I["h_sc_w"][0, k:k + 1, :]) for k in range(3))):
                        sp.dma_start(dst, feat_cols(src), allow_slow_non_contiguous=True).then_inc(S["ld"], 16)
                    for u in range(2):
                        sp.dma_start(win[u][:], wv[:, :, u * 512:(u + 1) * 512]).then_inc(s_w[u], 16)
                    with sp.Fori(1, 3) as it:
                        for u in range(2):
                            sp.wait_ge(S["used"], 2 * it + u - 1)
                            sp.dma_start(win[u][:], wv[:, :, bass.ds(it * 1024 + u * 512, 512)]).then_inc(s_w[u], 16)

                @blk.gpsimd
                def _(pool):
                    for u in range(2):
                        nc.gpsimd.memset(zb[u][:], 0.0).then_inc(S["zb"], 1)

                @blk.scalar
                def _(act):
                    a = nc.scalar
                    for t in range(TL):
                        act.wait_ge(S["sq"], t)
                        a.activation(junk[:], hl[:, t, :], ACT.Square, accum_out=ss[:, t:t + 1]).then_inc(S["sq"], 1)
                    act.wait_ge(S["mod"], 1)
                    for k in range(KD):
                        act.wait_ge(S["xT"], k + 1)
                        a.activation(uh[:, k, :], bank[k % 2][:], ACT.Identity, bias=mB[:, k:k + 1], scale=mA[:, k:k + 1]).then_inc(S["uh"], 1)
                    act.wait_ge(S["zb"], 2)
                    act.wait_ge(S["ld"], 16 * 8)

                    def back(n, b):
                        act.wait_ge(S["tps"], 2 + n + 1)
                        a.activation(ztok[:, :, bass.ds(n * P, P)], bank[2 + b][:].rearrange("p (t c) -> p t c", t=TL), ACT.Copy).then_inc(S["zt"], 1)

                    with act.Fori(0, 6) as q:
                        for f in range(4):
                            n = q * 4 + f
                            act.wait_ge(S["zps"], n + 1)
                            act.wait_ge(S["cv"], n + 1)
                            a.activation(zb[f % 2][:, 1:SEQ + 1], bank[f % 2][:], ACT.Identity, bias=ib[:, bass.ds(n, 1)]).then_inc(S["zb"], 1)
                            if f >= 1:
                                back(n - 1, (f - 1) % 2)
                        back(q * 4 + 3, 1)

                @blk.vector
                def _(dve):
                    v = nc.vector
                    own = Counter(dve, S["d"])
                    dve.wait_ge(S["ld"], 16 * 8)
                    own(v.scalar_tensor_tensor(out=mA[:], in0=mA[:], scalar=1.0, in1=n1[:], op0=ALU.add, op1=ALU.mult))
                    dve.wait_ge(S["sq"], TL)
                    v.tensor_copy(n1[:], mA[:]).then_inc(S["mod"], 1)
                    own(v.tensor_scalar(ss[:], ss[:], 1.0 / D, EPS, ALU.mult, ALU.add))
                    rsqrt(v, own, r1[:], ss[:], r2[:])
                    for t in range(TL):
                        v.tensor_scalar(xh[:, t, :], hl[:, t, :], ss[:, t:t + 1], None, ALU.mult).then_inc(S["xh"], 1)
                    own(v.memset(junk[:, 0:2], 0.0))
                    v.memset(r1[:], 0.0).then_inc(S["cv"], 2)
                    v.memset(r2[:], 0.0).then_inc(S["tps"], 2)
                    v.memset(junk[:, 2:4], 0.0).then_inc(S["zt"], 2)
                    with dve.Fori(0, 6) as q:
                        own.enter(q, PER)
                        for f in range(4):
                            n = q * 4 + f
                            b = f % 2
                            dve.wait_ge(S["zb"], 2 + n + 1)
                            dve.wait_ge(S["tps"], n + 1)
                            own(v.tensor_scalar(zc[b][:], zb[b][:, 0:SEQ], cw[:, 0, bass.ds(n, 1)], cb[:, bass.ds(n, 1)], ALU.mult, ALU.add))
                            own(v.scalar_tensor_tensor(out=zc[b][:], in0=zb[b][:, 1:SEQ + 1], scalar=cw[:, 1, bass.ds(n, 1)], in1=zc[b][:], op0=ALU.mult, op1=ALU.add))
                            v.scalar_tensor_tensor(out=zc[b][:], in0=zb[b][:, 2:SEQ + 2], scalar=cw[:, 2, bass.ds(n, 1)], in1=zc[b][:], op0=ALU.mult, op1=ALU.add).then_inc(S["cv"], 1)
                        own.leave(6, PER)

                @blk.tensor
                def _(pe):
                    t_ = nc.tensor
                    pe.wait_ge(S["xh"], TL)
                    for k in range(KD):
                        if k >= 2:
                            pe.wait_ge(S["uh"], k - 1)
                        for t in range(TL):
                            ins = t_.transpose(bank[k % 2][:, t * P:(t + 1) * P], xh[:, t, k * P:(k + 1) * P], ident[:])
                        ins.then_inc(S["xT"], 1)
                    pe.wait_ge(S["uh"], KD)

                    def back(n, b):
                        pe.wait_ge(S["cv"], 2 + n + 1)
                        pe.wait_ge(S["zt"], n + 1)
                        for t in range(TL):
                            ins = t_.transpose(bank[2 + b][:, t * P:(t + 1) * P], zc[b][:, t * P:(t + 1) * P], ident[:])
                        ins.then_inc(S["tps"], 1)

                    with pe.Fori(0, 3) as it:
                        for u in range(2):
                            q = it * 2 + u
                            pe.wait_ge(s_w[u], 16 * it + 16)
                            for f in range(4):
                                n = q * 4 + f
                                pe.wait_ge(S["zb"], n + 1)
                                for k in range(KD):
                                    ins = t_.matmul(bank[f % 2][:], win[u][:, k, f * P:(f + 1) * P], uh[:, k, :], start=(k == 0), stop=(k == KD - 1))
                                ins.then_inc(S["zps"], 1)
                                if f >= 1:
                                    back(n - 1, (f - 1) % 2)
                            pe.wait_ge(S["zps"], 4 * q + 4)
                            t_.matmul(bank[7][0:1, 0:1], ones[:, 0:1], ones[:, 0:1], start=True, stop=True).then_inc(S["used"], 1)
                            back(q * 4 + 3, 1)

        def hyena_convs(ztok):
            with stage() as c:
                def T(name, shape, dt=F32):
                    return sbt(c, f"{name}v", shape, dt)

                dft = T("dft", [P, TL, 2 * FREQ]); idft = T("idft", [P, 2 * FREQ // P, SEQ])
                fl = T("fl", [P, TL, D]); Fs = [T(f"Fs{i}", [P, 6, D]) for i in range(2)]; Pr = T("Pr", [P, 6, D])
                bias = T("bias", [P, 2 * D]); ta = T("ta", [P, 2, 512]); tb = T("tb", [P, 2, 512])
                S = {k: sem(f"s_{k}_hc") for k in "ld fld fps fs vps d m R yps y I".split()}
                NF = 6
                blk = c.enter_context(nc.Block())

                @blk.sync
                def _(sp):
                    sp.dma_start(dft[:], I["dft"].rearrange("(t p) f -> p t f", p=P)).then_inc(S["ld"], 16)
                    fv = d_filt.rearrange("(t p) n -> p t n", p=P)
                    sp.dma_start(fl[:], fv[:, :, 0:D]).then_inc(S["fld"], 16)
                    sp.dma_start(idft[:], I["idft"].rearrange("(f p) t -> p f t", p=P)).then_inc(S["ld"], 16)
                    sp.dma_start(bias[:], row_bcast(I["h_fbias"][0:1, :])).then_inc(S["ld"], 16)
                    sp.wait_ge(S["fps"], 12)
                    sp.dma_start(fl[:], fv[:, :, D:2 * D]).then_inc(S["fld"], 16)

                @blk.tensor
                def _(pe):
                    t_ = nc.tensor
                    pe.wait_ge(S["ld"], 48)

                    def filter_spectrum(o):
                        pe.wait_ge(S["fld"], 16 * o + 16)
                        for g in range(12):
                            f, n = g // 2, g % 2
                            i = 12 * o + g
                            if i >= 2:
                                pe.wait_ge(S["fs"], i - 1)
                            for t in range(TL):
                                ins = t_.matmul(bank[g % 2][:], dft[:, t, f * P:(f + 1) * P], fl[:, t, n * 512:(n + 1) * 512], start=(t == 0), stop=(t == TL - 1))
                            ins.then_inc(S["fps"], 1)

                    def value_spectrum(o):
                        for g in range(6):
                            i, n = g // 2, g % 2
                            j = 6 * o + g
                            if j >= 2:
                                pe.wait_ge(S["m"], j - 1)
                            for part in range(2):
                                f = part * 3 + i
                                for t in range(TL):
                                    ins = t_.matmul(bank[2 + 2 * (g % 2) + part][:], dft[:, t, f * P:(f + 1) * P], ztok[:, t, 2 * D + n * 512:2 * D + (n + 1) * 512], start=(t == 0), stop=(t == TL - 1))
                            ins.then_inc(S["vps"], 1)

                    def inverse(o):
                        for g in range(8):
                            t, n = g // 2, g % 2
                            j = 8 * o + g
                            if j >= 2:
                                pe.wait_ge(S["y"], j - 1)
                            for f in range(NF):
                                ins = t_.matmul(bank[6 + g % 2][:], idft[:, f, t * P:(t + 1) * P], Pr[:, f, n * 512:(n + 1) * 512], start=(f == 0), stop=(f == NF - 1))
                            ins.then_inc(S["yps"], 1)

                    filter_spectrum(0)
                    value_spectrum(0)
                    filter_spectrum(1)
                    pe.wait_ge(S["R"], 6)
                    inverse(0)
                    pe.wait_ge(S["y"], 8)
                    value_spectrum(1)
                    pe.wait_ge(S["R"], 12)
                    inverse(1)

                @blk.scalar
                def _(act):
                    for o in range(2):
                        for g in range(12):
                            f, n = g // 2, g % 2
                            act.wait_ge(S["fps"], 12 * o + g + 1)
                            nc.scalar.activation(Fs[o][:, f, n * 512:(n + 1) * 512], bank[g % 2][:], ACT.Copy).then_inc(S["fs"], 1)

                @blk.gpsimd
                def _(pool):
                    g_ = nc.gpsimd
                    for o in range(2):
                        for g in range(6):
                            i, n = g // 2, g % 2
                            cs = slice(n * 512, (n + 1) * 512)
                            pool.wait_ge(S["m"], 6 * o + g + 1)
                            if o == 1:
                                pool.wait_ge(S["yps"], 8)
                            g_.tensor_tensor(Pr[:, i, cs], ta[:, 0, :], ta[:, 1, :], ALU.subtract)
                            g_.tensor_tensor(Pr[:, 3 + i, cs], tb[:, 0, :], tb[:, 1, :], ALU.add).then_inc(S["R"], 1)

                @blk.vector
                def _(dve):
                    v = nc.vector
                    own = Counter(dve, S["d"])
                    dve.wait_ge(S["ld"], 48)
                    for o in range(2):
                        for g in range(6):
                            i, n = g // 2, g % 2
                            cs = slice(n * 512, (n + 1) * 512)
                            dve.wait_ge(S["vps"], 6 * o + g + 1)
                            dve.wait_ge(S["fs"], 12 * o + 12)
                            dve.wait_ge(S["R"], 6 * o + g)
                            A1, B1 = bank[2 + 2 * (g % 2)], bank[3 + 2 * (g % 2)]
                            v.tensor_tensor(ta[:, 0, :], A1[:], Fs[o][:, i, cs], ALU.mult)
                            v.tensor_tensor(tb[:, 0, :], A1[:], Fs[o][:, 3 + i, cs], ALU.mult)
                            v.tensor_tensor(ta[:, 1, :], B1[:], Fs[o][:, 3 + i, cs], ALU.mult)
                            v.tensor_tensor(tb[:, 1, :], B1[:], Fs[o][:, i, cs], ALU.mult).then_inc(S["m"], 1)
                            dve.wait_ge(S["m"], 6 * o + g + 1)
                        dve.wait_ge(S["R"], 6 * o + 6)
                        for g in range(8):
                            t, n = g // 2, g % 2
                            val = ztok[:, t, 2 * D + n * 512:2 * D + (n + 1) * 512]
                            own(v.tensor_tensor(ta[:, 0, :], val, bias[:, o * D + n * 512:o * D + (n + 1) * 512], ALU.mult))
                            dve.wait_ge(S["yps"], 8 * o + g + 1)
                            own(v.tensor_tensor(ta[:, 0, :], ta[:, 0, :], bank[6 + g % 2][:], ALU.add))
                            v.tensor_tensor(val, ta[:, 0, :], ztok[:, t, o * D + n * 512:o * D + (n + 1) * 512], ALU.mult).then_inc(S["y"], 1)
                            dve.wait_ge(S["y"], 8 * o + g + 1)
            with stage() as c:
                def T(name, shape, dt=F32):
                    return sbt(c, f"{name}q", shape, dt)

                yh = T("yh", [P, KD, SEQ]); ow = T("ow", [P, KD, D]); ob = T("ob", [P, D]); g1 = T("g1", [P, D]); tmp = T("tmp", [P, 2, 512])
                S = {k: sem(f"s_{k}_ho") for k in "ow ld tps yh o d".split()}
                blk = c.enter_context(nc.Block())

                @blk.sync
                def _(sp):
                    sp.dma_start(ob[:], row_bcast(I["h_out_b"][0:1, :])).then_inc(S["ld"], 16)
                    sp.dma_start(g1[:], row_bcast(d_mod[1][:, 2 * D:3 * D])).then_inc(S["ld"], 16)
                    sp.dma_start(ow[:], I["h_out_w"][0].rearrange("(k p) n -> p k n", p=P)).then_inc(S["ow"], 16)

                @blk.tensor
                def _(pe):
                    t_ = nc.tensor
                    for k in range(KD):
                        if k >= 2:
                            pe.wait_ge(S["yh"], k - 1)
                        for t in range(TL):
                            ins = t_.transpose(bank[k % 2][:, t * P:(t + 1) * P], ztok[:, t, 2 * D + k * P:2 * D + (k + 1) * P], ident[:])
                        ins.then_inc(S["tps"], 1)
                    pe.wait_ge(S["ow"], 16)
                    pe.wait_ge(S["yh"], KD)
                    for t in range(TL):
                        for n in range(2):
                            for k in range(KD):
                                ins = t_.matmul(bank[2 * t + n][:], yh[:, k, t * P:(t + 1) * P], ow[:, k, n * 512:(n + 1) * 512], start=(k == 0), stop=(k == KD - 1))
                            ins.then_inc(S["o"], 1)

                @blk.scalar
                def _(act):
                    for k in range(KD):
                        act.wait_ge(S["tps"], k + 1)
                        nc.scalar.activation(yh[:, k, :], bank[k % 2][:], ACT.Copy).then_inc(S["yh"], 1)

                @blk.vector
                def _(dve):
                    v = nc.vector
                    own = Counter(dve, S["d"])
                    dve.wait_ge(S["ld"], 32)
                    own(v.tensor_tensor(ob[:], ob[:], g1[:], ALU.mult))
                    for t in range(TL):
                        own(v.tensor_tensor(hl[:, t, :], hl[:, t, :], ob[:], ALU.add))
                    residual(dve, own, bank, S["o"], g1, tmp)

        c12 = top.enter_context(ExitStack())
        uT = sbt(c12, "uT", [P, KD, NTOK])
        gacc = sbt(c12, "gacc", [P, TA, 16])
        with stage() as c1:
            ctxt = sbt(c1, "ctxt", [P, TC, D])
            xh = sbt(c1, "xh", [P, D])
            junk = sbt(c1, "junk1", [P, D])
            cv = sbt(c1, "cv", [P, 2, KD])
            acc = sbt(c1, "acc", [P, 2 * 6 * D])
            accc = sbt(c1, "accc", [P, 2 * D])
            ptmp = sbt(c1, "ptmp", [P, 2 * D])
            adab = [sbt(c1, f"adab{i}", [P, 2, 2048]) for i in range(2)]
            win = [sbt(c1, f"win{i}", [P, KD, 512]) for i in range(2)]
            srow = [sbt(c1, f"srow{i}", [1, 512]) for i in range(2)]
            ss = sbt(c1, "ss", [P, TA])
            sq = sbt(c1, "sq", [P, TA])
            sq2 = sbt(c1, "sq2", [P, TA])
            mA = sbt(c1, "mA", [P, 2, KD])
            mB = sbt(c1, "mB", [P, 2, KD])
            g1c = sbt(c1, "g1c", [P, KD])
            xmb = [sbt(c1, f"xmb{i}", [P, XMW]) for i in range(2)]
            xcb = [sbt(c1, f"xcb{i}", [P, XCW]) for i in range(2)]
            cvt = sbt(c1, "cvt", [P, XCW])
            gw = sbt(c1, "gw", [P, 2, 16, 16])
            cw = sbt(c1, "cw", [P, 3, 16])
            cb = sbt(c1, "cb", [P, 16])
            s_const = sem("s_const"); s_cvld = sem("s_cvld"); s_accb = sem("s_accb"); s_tok = sem("s_tok"); s_csil = sem("s_csil")
            s_ada = [sem(f"s_ada{i}") for i in range(2)]; s_adaused = sem("s_adaused"); s_adausedc = sem("s_adausedc")
            s_acc0 = sem("s_acc0"); s_acc0c = sem("s_acc0c"); s_rowps = sem("s_rowps"); s_rowsb = sem("s_rowsb"); s_rowst = [sem(f"s_rowst{i}") for i in range(2)]
            s_modld = sem("s_modld"); s_modAB = sem("s_modAB")
            s_ss = sem("s_ss");  s_xh = sem("s_xh"); s_xT = sem("s_xT"); s_uT = sem("s_uT"); s_uTc = sem("s_uTc")
            s_win = [sem(f"s_win{i}") for i in range(2)]; s_winused = sem("s_winused")
            s_xmps = sem("s_xmps"); s_xm = sem("s_xm"); s_cvt = sem("s_cvt"); s_xc = sem("s_xc")
            s_gused = sem("s_gused"); s_gps = sem("s_gps"); s_gacc = sem("s_gacc")
            s_xmst = [sem(f"s_xmst{i}") for i in range(2)]; s_pads = sem("s_pads")
            s_dve1 = sem("s_dve1"); s_pool1 = sem("s_pool1"); s_acc1 = sem("s_acc1"); s_tab0 = sem("s_tab0")
            ada = [I["ada_w"][l].rearrange("(p t) n -> p t n", t=KD) for l in range(2)]
            grp = [(0, 0), (0, 1), (0, 2), (1, 0), (1, 1), (1, 2)]
            blk = c1.enter_context(nc.Block())

            @blk.sync
            def _(sp):
                sp.dma_start(cv[:, 0, :], I["c"].rearrange("o (p t) -> p (o t)", t=KD)).then_inc(s_cvld, 16)
                sp.dma_start(cv[:, 1, :], I["c_ctx"].rearrange("(p t) -> p t", t=KD)).then_inc(s_cvld, 16)
                sp.wait_ge(s_pads, 1)
                for l in range(2):
                    sp.dma_start(acc[0:1, l * 6 * D:(l + 1) * 6 * D], I["ada_b"][l:l + 1, :]).then_inc(s_accb, 16)
                sp.dma_start(accc[0:1, :], I["ada_b"][0:1, 0:2 * D]).then_inc(s_accb, 16)
                for t in range(4):
                    if t >= 2:
                        sp.wait_ge(s_adaused, t - 1)
                        sp.wait_ge(s_adausedc, t - 1)
                    sp.dma_start(adab[t % 2][:], ada[0][:, 2 * t:2 * t + 2, 0:2048]).then_inc(s_ada[t % 2], 16)
                sp.dma_start(hl[:], I["x"][0].rearrange("(t p) d -> p t d", p=P)).then_inc(s_tok, 16)
                sp.dma_start(ctxt[:], I["ctx"][0].rearrange("(t p) d -> p t d", p=P)).then_inc(s_tok, 16)
                for u in range(2):
                    sp.dma_start(win[u][:], I["m_in_w"][0].rearrange("(k p) n -> p k n", p=P)[:, :, u * 512:(u + 1) * 512]).then_inc(s_win[u], 16)
                for i in range(2):
                    sp.wait_ge(s_rowst[i], 16 * 4)
                for i, row in enumerate((d_mod[0], d_modc)):
                    sp.dma_start(mB[:, i, :], feat_cols(row[:, 0:D]), allow_slow_non_contiguous=True).then_inc(s_modld, 16)
                    sp.dma_start(mA[:, i, :], feat_cols(row[:, D:2 * D]), allow_slow_non_contiguous=True).then_inc(s_modld, 16)
                with sp.Fori(0, HEADS // 2) as hh:
                    for u in range(2):
                        for j in range(5):
                            n = 4 + j + u * 5
                            l, g = grp[j + 1]
                            sp.wait_ge(s_adaused, hh * 10 + (n - 1))
                            sp.wait_ge(s_adausedc, 4)
                            sp.dma_start(adab[n % 2][:], ada[l][:, bass.ds(hh * 4 + 2 * u, 2), g * 2048:(g + 1) * 2048]).then_inc(s_ada[n % 2], 16)
                        with sp.If(hh < 1):
                            sp.wait_ge(s_winused, hh * 2 + u + 1)
                            sp.wait_ge(s_adausedc, 4)
                            sp.dma_start(win[u][:], I["m_in_w"][0].rearrange("(k p) n -> p k n", p=P)[:, :, bass.ds(hh * 1024 + (2 + u) * 512, 512)]).then_inc(s_win[u], 16)

            @blk.gpsimd
            def _(pool):
                own = Counter(pool, s_pool1)
                g = nc.gpsimd
                g.memset(acc[:], 0.0)
                g.memset(accc[:], 0.0).then_inc(s_pads, 1)
                own(g.memset(ident[:], 0.0))
                g.affine_select(out=ident[:], in_=ident[:], compare_op=ALU.not_equal, fill=1.0, base=0, pattern=[[-1, P]], channel_multiplier=1).then_inc(s_const, 1)
                g.memset(ones[:], 1.0).then_inc(s_const, 1)
                own(g.memset(upper[:], 0.0))
                g.affine_select(out=upper[:], in_=upper[:], compare_op=ALU.is_ge, fill=1.0, base=0, pattern=[[-1, P]], channel_multiplier=1).then_inc(s_const, 1)
                for u in range(2):
                    g.memset(xmb[u][:], 0.0).then_inc(s_xm, 1)
                g.memset(cvt[:, 0:1], 0.0).then_inc(s_gused, 2)
                g.memset(gacc[:], 0.0).then_inc(s_const, 1)
                pool.wait_ge(s_csil, 1)
                pool.wait_ge(s_accb, 48)
                for t in range(4):
                    pool.wait_ge(s_ada[t % 2], 16 * (t // 2 + 1))
                    for j in range(2):
                        own(g.tensor_scalar(ptmp[:], adab[t % 2][:, j, :], cv[:, 1, 2 * t + j:2 * t + j + 1], None, ALU.mult))
                        ins = g.tensor_tensor(accc[:], accc[:], ptmp[:], ALU.add)
                        if j == 0:
                            own(ins)
                        else:
                            ins.then_inc(s_adausedc, 1)
                            pool.wait_ge(s_adausedc, t + 1)
                for n in range(28):
                    pool.wait_ge(s_rowsb, n + 1)
                    if n < 4:
                        dst = d_mod[0][:, n * 512:(n + 1) * 512]
                    elif n < 8:
                        dst = d_modc[:, (n - 4) * 512:(n - 3) * 512]
                    else:
                        c0 = 2048 + (n - 8) * 512
                        dst = d_mod[c0 // (6 * D)][:, c0 % (6 * D):c0 % (6 * D) + 512]
                    pool.dma_start(dst, srow[n % 2][:]).then_inc(s_rowst[n % 2], 16)
                for i in range(2):
                    pool.wait_ge(s_rowst[i], 16 * 14)

            @blk.scalar
            def _(act):
                a = nc.scalar
                act.dma_start(g1c[:], feat_cols(I["norm1_g"][0:1, :]), allow_slow_non_contiguous=True).then_inc(s_modld, 16)
                for k in range(3):
                    act.dma_start(cw[:, k, :], I["m_conv_w"][0, k:k + 1, :].rearrange("o (f p) -> p (o f)", p=P), allow_slow_non_contiguous=True).then_inc(s_tab0, 16)
                act.dma_start(cb[:], I["m_conv_b"][0:1, :].rearrange("o (f p) -> p (o f)", p=P), allow_slow_non_contiguous=True).then_inc(s_tab0, 16)
                act.dma_start(gw[:], I["m_gate_w"][0].rearrange("(h f p) n -> p h f n", h=2, p=P)).then_inc(s_tab0, 16)
                act.wait_ge(s_cvld, 32)
                a.activation(cv[:], cv[:], ACT.Silu).then_inc(s_csil, 1)
                act.wait_ge(s_tok, 32)
                for t in range(TA):
                    src = hl[:, t, :] if t < TL else ctxt[:, t - TL, :]
                    act.wait_ge(s_ss, t)
                    a.activation(junk[:], src, ACT.Square, accum_out=ss[:, t:t + 1]).then_inc(s_ss, 1)
                act.wait_ge(s_modAB, 1)
                for k in range(KD):
                    act.wait_ge(s_xT, k + 1)
                    a.activation(uT[:, k, 0:CTX], bank[2 * (k % 2)][:, 0:CTX], ACT.Identity, bias=mB[:, 1, k:k + 1], scale=mA[:, 1, k:k + 1]).then_inc(s_uTc, 1)
                act.wait_ge(s_xm, 2)
                with act.Fori(0, HEADS) as h:
                    for f in range(FT):
                        n = f
                        act.wait_ge(s_xmps, h * FT + n + 1)
                        act.wait_ge(s_gused, h * FT + n + 1)
                        act.wait_ge(s_xmst[f % 2], h * 64 + 32 * (f // 2))
                        a.activation(xmb[f % 2][:, 1:1 + CTX], bank[2 * (f % 2) + 1][:, 0:CTX], ACT.Copy)
                        a.activation(xmb[f % 2][:, 2 + CTX:2 + CTX + SEQ], bank[2 * (f % 2)][:], ACT.Copy).then_inc(s_xm, 1)
                        act.wait_ge(s_xm, 2 + h * FT + n + 1)
                        act.dma_start(d_xm[bass.ds(h * FT + f, 1), :, :].rearrange("o p w -> (o p) w"), xmb[f % 2][:]).then_inc(s_xmst[f % 2], 16)
                        act.wait_ge(s_cvt, h * FT + n + 1)
                        a.activation(xcb[f % 2][:], cvt[:], ACT.Silu).then_inc(s_xc, 1)
                        act.wait_ge(s_xc, h * FT + n + 1)
                        act.dma_start(d_xc[bass.ds(h * FT + f, 1), :, :].rearrange("o p w -> (o p) w"), xcb[f % 2][:]).then_inc(s_xmst[f % 2], 16)
                for u in range(2):
                    act.wait_ge(s_xmst[u], 32 * HEADS * FT // 2)

            @blk.vector
            def _(dve):
                v = nc.vector
                own = Counter(dve, s_dve1)
                dve.wait_ge(s_csil, 1)
                dve.wait_ge(s_accb, 48)
                for t in range(4):
                    dve.wait_ge(s_ada[t % 2], 16 * (t // 2 + 1))
                    for j in range(2):
                        ins = v.scalar_tensor_tensor(out=acc[:, 0:2048], in0=adab[t % 2][:, j, :], scalar=cv[:, 0, 2 * t + j:2 * t + j + 1], in1=acc[:, 0:2048], op0=ALU.mult, op1=ALU.add)
                        if j == 0:
                            own(ins)
                        else:
                            ins.then_inc(s_adaused, 1)
                            dve.wait_ge(s_adaused, t + 1)
                for n in range(8):
                    dve.wait_ge(s_rowps, n + 1)
                    dve.wait_ge(s_rowst[n % 2], 16 * (n // 2))
                    v.tensor_copy(srow[n % 2][:], bank[4 + n % 2][0:1, :]).then_inc(s_rowsb, 1)
                dve.wait_ge(s_ss, TA)
                own(v.tensor_scalar(ss[:], ss[:], 1.0 / D, EPS, ALU.mult, ALU.add))
                dve.wait_ge(s_modld, 16 * 5)
                own(v.tensor_scalar(mA[:], mA[:], 1.0, None, ALU.add))
                for i in range(2):
                    ins = v.tensor_tensor(mA[:, i, :], mA[:, i, :], g1c[:], ALU.mult)
                ins.then_inc(s_modAB, 1)
                rsqrt(v, own, sq[:], ss[:], sq2[:])
                for t in range(TA):
                    src = hl[:, t, :] if t < TL else ctxt[:, t - TL, :]
                    v.tensor_scalar(src, src, ss[:, t:t + 1], None, ALU.mult).then_inc(s_xh, 1)
                dve.wait_ge(s_modAB, 1)
                for k in range(KD):
                    dve.wait_ge(s_xT, k + 1)
                    v.tensor_scalar(uT[:, k, CTX:NTOK], bank[2 * (k % 2) + 1][:], mA[:, 0, k:k + 1], mB[:, 0, k:k + 1], ALU.mult, ALU.add).then_inc(s_uT, 1)
                dve.wait_ge(s_tab0, 80)
                dve.wait_ge(s_const, 4)
                PER = 8 + 5
                with dve.Fori(0, HEADS // 2) as hh:
                    own.enter(hh, 2 * PER)
                    for u in range(2):
                        h = hh * 2 + u
                        for f in range(FT):
                            dve.wait_ge(s_xm, 2 + h * FT + f + 1)
                            dve.wait_ge(s_xc, h * FT + f)
                            ft = hh * (2 * FT) + u * FT + f
                            own(v.tensor_scalar(cvt[:], xmb[f % 2][:, 0:XCW], cw[:, 0, bass.ds(ft, 1)], cb[:, bass.ds(ft, 1)], ALU.mult, ALU.add))
                            own(v.scalar_tensor_tensor(out=cvt[:], in0=xmb[f % 2][:, 1:1 + XCW], scalar=cw[:, 1, bass.ds(ft, 1)], in1=cvt[:], op0=ALU.mult, op1=ALU.add))
                            v.scalar_tensor_tensor(out=cvt[:], in0=xmb[f % 2][:, 2:2 + XCW], scalar=cw[:, 2, bass.ds(ft, 1)], in1=cvt[:], op0=ALU.mult, op1=ALU.add).then_inc(s_cvt, 1)
                        for j in range(5):
                            n = 4 + j + u * 5
                            dve.wait_ge(s_ada[n % 2], hh * 80 + 16 * (n // 2 + 1))
                            col = (j + 1) * 2048
                            own(v.scalar_tensor_tensor(out=acc[:, col:col + 2048], in0=adab[n % 2][:, 0, :], scalar=cv[:, 0, bass.ds(hh * 4 + 2 * u, 1)], in1=acc[:, col:col + 2048], op0=ALU.mult, op1=ALU.add))
                            v.scalar_tensor_tensor(out=acc[:, col:col + 2048], in0=adab[n % 2][:, 1, :], scalar=cv[:, 0, bass.ds(hh * 4 + 2 * u + 1, 1)], in1=acc[:, col:col + 2048], op0=ALU.mult, op1=ALU.add).then_inc(s_adaused, 1)
                            dve.wait_ge(s_adaused, hh * 10 + n + 1)
                        dve.wait_ge(s_gps, h + 1)
                        v.tensor_tensor(gacc[:].rearrange("p t n -> p (t n)"), gacc[:].rearrange("p t n -> p (t n)"), bank[6][:, 0:TA * 16], ALU.add).then_inc(s_gacc, 1)
                        dve.wait_ge(s_gacc, h + 1)
                    own.leave(2, 2 * PER)
                for n in range(20):
                    dve.wait_ge(s_rowps, 8 + n + 1)
                    dve.wait_ge(s_rowst[n % 2], 16 * (4 + n // 2))
                    v.tensor_copy(srow[n % 2][:], bank[4 + n % 2][0:1, :]).then_inc(s_rowsb, 1)

            @blk.tensor
            def _(pe):
                t_ = nc.tensor
                pe.wait_ge(s_const, 4)
                pe.wait_ge(s_adaused, 4)
                pe.wait_ge(s_adausedc, 4)
                for n in range(8):
                    if n >= 2:
                        pe.wait_ge(s_rowsb, n - 1)
                    src = acc[:, n * 512:(n + 1) * 512] if n < 4 else accc[:, (n - 4) * 512:(n - 3) * 512]
                    t_.matmul(bank[4 + n % 2][0:1, :], ones[:, 0:1], src, start=True, stop=True).then_inc(s_rowps, 1)
                pe.wait_ge(s_xh, TA)
                for k in range(KD):
                    if k >= 2:
                        pe.wait_ge(s_uT, k - 1)
                        pe.wait_ge(s_uTc, k - 1)
                    for t in range(TC):
                        t_.transpose(bank[2 * (k % 2)][:, t * P:(t + 1) * P], ctxt[:, t, k * P:(k + 1) * P], ident[:])
                    for t in range(TL):
                        ins = t_.transpose(bank[2 * (k % 2) + 1][:, t * P:(t + 1) * P], hl[:, t, k * P:(k + 1) * P], ident[:])
                    ins.then_inc(s_xT, 1)
                pe.wait_ge(s_uT, KD)
                pe.wait_ge(s_uTc, KD)
                pe.wait_ge(s_tab0, 80)

                def gates(h, f):
                    pe.wait_ge(s_xc, h * FT + f + 1)
                    if f == 0:
                        pe.wait_ge(s_gacc, h)
                    for half in range(2):
                        for t in range(TA):
                            if half == 0:
                                c0 = t * P if t < TC else LAT0 + (t - TC) * P
                                lhs = xcb[f % 2][:, c0:c0 + P]
                            else:
                                c0 = 1 + t * P if t < TC else 2 + CTX + (t - TC) * P
                                lhs = xmb[f % 2][:, c0:c0 + P]
                            ins = t_.matmul(bank[6][:, t * 16:(t + 1) * 16], lhs, gw[:, half, bass.ds(h * FT + f, 1), :].rearrange("p o n -> p (o n)"),
                                            start=(f == 0 and half == 0 and t == 0), stop=(f == FT - 1 and half == 1 and t == TA - 1), skip_group_check=True)
                    ins.then_inc(s_gused, 1)

                with pe.Fori(0, HEADS // 2) as hh:
                    for u in range(2):
                        h = hh * 2 + u
                        pe.wait_ge(s_win[u], hh * 16 + 16)
                        for f in range(FT):
                            pe.wait_ge(s_xm, h * FT + f + 1)
                            for k in range(KD):
                                w = win[u][:, k, f * P:(f + 1) * P]
                                t_.matmul(bank[2 * (f % 2)][:], w, uT[:, k, CTX:NTOK], start=(k == 0), stop=(k == KD - 1))
                                ins = t_.matmul(bank[2 * (f % 2) + 1][:, 0:CTX], w, uT[:, k, 0:CTX], start=(k == 0), stop=(k == KD - 1))
                            ins.then_inc(s_xmps, 1)
                            if f >= 1:
                                gates(h, f - 1)
                        pe.wait_ge(s_xmps, h * FT + FT)
                        t_.matmul(bank[7][0:1, 0:1], ones[:, 0:1], ones[:, 0:1], start=True, stop=True).then_inc(s_winused, 1)
                        gates(h, FT - 1)
                        pe.wait_ge(s_gused, 2 + h * FT + FT)
                        t_.matmul(bank[7][0:1, 0:1], ones[:, 0:1], ones[:, 0:1], start=True, stop=True).then_inc(s_gps, 1)
                pe.wait_ge(s_adaused, 24)
                for n in range(20):
                    pe.wait_ge(s_rowsb, 8 + n - 1)
                    t_.matmul(bank[4 + n % 2][0:1, :], ones[:, 0:1], acc[:, 2048 + n * 512:2048 + (n + 1) * 512], start=True, stop=True).then_inc(s_rowps, 1)

        if dbg is not None and stop == 1:
            return dump(nc, dbg, sem, [("o_gacc", gacc[:].rearrange("p t n -> p (t n)")), ("o_uT", uT[:].rearrange("p k n -> p (k n)"))],
                        [("o_mod0", d_mod[0]), ("o_mod1", d_mod[1]), ("o_xc", d_xc.rearrange("a p w -> (a p) w"))])
        yT = sbt(c12, "yT", [P, HEADS * FT, SEQ])
        acol = sbt(c12, "acol", [P, 2, TA, HEADS])
        ecol = sbt(c12, "ecol", [P, 2, TL, HEADS])
        with stage() as c2:
            gb = sbt(c2, "gb", [HEADS, 4])
            R = sbt(c2, "R", [HEADS, 4, NTOK])
            lt = sbt(c2, "lt", [HEADS, 2, NTOK])
            B = sbt(c2, "Bsum", [HEADS, 2, NTOK])
            A = sbt(c2, "Arow", [HEADS, 2, NTOK])
            M = sbt(c2, "Mrow", [HEADS, 2, NTOK])
            AN = sbt(c2, "AN", [HEADS, 2, NTOK])
            EN = sbt(c2, "EN", [HEADS, 2, SEQ])
            NM = sbt(c2, "NM", [HEADS, 2, SEQ])
            s_gb = sem("s_gb"); s_rps = sem("s_rps"); s_lf = sem("s_lf"); s_ln = sem("s_ln"); s_d2 = sem("s_d2")
            s_em = sem("s_em"); s_en = sem("s_en"); s_rows = sem("s_rows"); s_cps = sem("s_cps"); s_nmst = sem("s_nmst")
            s_a2 = sem("s_a2"); s_nmr = sem("s_nmr")
            blk = c2.enter_context(nc.Block())

            @blk.sync
            def _(sp):
                sp.dma_start(gb[:], I["m_gate_b"][0:1, :].rearrange("o (g h) -> (o h) g", g=4), allow_slow_non_contiguous=True).then_inc(s_gb, 16)
                sp.wait_ge(s_nmr, 1)
                sp.dma_start(d_negm, NM[:].rearrange("h d t -> h (d t)")).then_inc(s_nmst, 16)
                sp.wait_ge(s_nmst, 16)

            @blk.tensor
            def _(pe):
                t_ = nc.tensor
                for g in range(4):
                    for t in range(TC):
                        t_.matmul(bank[4 + g][0:HEADS, t * P:(t + 1) * P], gacc[:, t, g * 4:g * 4 + 4], ident[:], start=True, stop=True)
                    for t in range(TL):
                        ins = t_.matmul(bank[g][0:HEADS, t * P:(t + 1) * P], gacc[:, TC + t, g * 4:g * 4 + 4], ident[:], start=True, stop=True)
                    ins.then_inc(s_rps, 1)
                pe.wait_ge(s_rows, 1)
                pe.wait_ge(s_en, 1)
                for d in range(2):
                    for t in range(TA):
                        t_.transpose(bank[0][:, (d * TA + t) * HEADS:(d * TA + t + 1) * HEADS], AN[:, d, t * P:(t + 1) * P], ident[0:HEADS, 0:HEADS])
                    for t in range(TL):
                        ins = t_.transpose(bank[1][:, (d * TL + t) * HEADS:(d * TL + t + 1) * HEADS], EN[:, d, t * P:(t + 1) * P], ident[0:HEADS, 0:HEADS])
                ins.then_inc(s_cps, 1)

            @blk.scalar
            def _(act):
                a = nc.scalar
                act.wait_ge(s_lf, 1)
                a.activation(lt[:], lt[:], ACT.Exp).then_inc(s_a2, 1)
                act.wait_ge(s_a2, 1)
                a.activation(lt[:], lt[:], ACT.Ln, bias=1.0).then_inc(s_ln, 1)
                act.wait_ge(s_em, 1)
                a.activation(EN[:], EN[:], ACT.Exp, scale=-1.0).then_inc(s_en, 1)

            @blk.vector
            def _(dve):
                v = nc.vector
                own = Counter(dve, s_d2)
                dve.wait_ge(s_gb, 16)
                own(v.memset(A[:], 1.0))
                for g in range(4):
                    dve.wait_ge(s_rps, g + 1)
                    for lo, n, src in ((0, CTX, bank[4 + g]), (CTX, SEQ, bank[g])):
                        row = src[0:HEADS, 0:n] if g < 2 else src[0:HEADS, n - 1::-1]
                        own(v.tensor_scalar(R[:, g, lo:lo + n], row, gb[:, g:g + 1], None, ALU.add))
                for d in range(2):
                    ins = v.scalar_tensor_tensor(out=lt[:, d, :], in0=R[:, 2 * d + 1, :], scalar=-1.0, in1=R[:, 2 * d + 1, :], op0=ALU.mult, op1=ALU.min)
                ins.then_inc(s_lf, 1)
                dve.wait_ge(s_ln, 1)
                for d in range(2):
                    own(v.scalar_tensor_tensor(out=lt[:, d, :], in0=R[:, 2 * d + 1, :], scalar=0.0, in1=lt[:, d, :], op0=ALU.min, op1=ALU.subtract))
                for d in range(2):
                    own(v.tensor_tensor_scan(out=B[:, d, :], data0=A[:, d, :], data1=lt[:, d, :], initial=0.0, op0=ALU.mult, op1=ALU.add))
                for d in range(2):
                    own(v.tensor_tensor(A[:, d, :], R[:, 2 * d, :], B[:, d, :], ALU.subtract))
                    own(v.tensor_tensor_scan(out=M[:, d, :], data0=A[:, d, :], data1=A[:, d, :], initial=0.0, op0=ALU.max, op1=ALU.max))
                    own(v.tensor_tensor(B[:, d, :], B[:, d, :], M[:, d, :], ALU.add))

                def lat(T, d):
                    return T[:, d, CTX:NTOK] if d == 0 else T[:, d, NTOK - 1:CTX - 1:-1]

                for d in range(2):
                    ins = v.tensor_scalar(NM[:, d, :], lat(M, d), -1.0, None, ALU.mult)
                ins.then_inc(s_nmr, 1)
                for d in range(2):
                    ins = v.tensor_copy(EN[:, d, :], lat(B, d))
                ins.then_inc(s_em, 1)
                for d in range(2):
                    v.tensor_copy(AN[:, d, CTX:NTOK], lat(A, d))
                    ins = v.tensor_copy(AN[:, d, 0:CTX], A[:, d, 0:CTX] if d == 0 else A[:, d, CTX - 1::-1])
                ins.then_inc(s_rows, 1)
                dve.wait_ge(s_cps, 1)
                v.tensor_copy(acol[:].rearrange("p a b c -> p (a b c)"), bank[0][:, 0:2 * TA * HEADS])
                v.tensor_copy(ecol[:].rearrange("p a b c -> p (a b c)"), bank[1][:, 0:2 * TL * HEADS])
        if dbg is not None and stop == 2:
            return dump(nc, dbg, sem, [("o_acol", acol[:].rearrange("p a b c -> p (a b c)")), ("o_ecol", ecol[:].rearrange("p a b c -> p (a b c)"))], [("o_negm", d_negm)])

        with stage() as c3:
            xch = sbt(c3, "xch", [P, FT, XCW])
            xmh = sbt(c3, "xmh", [P, FT, XMW])
            qT = sbt(c3, "qT", [P, QT, SEQ])
            kT = sbt(c3, "kT", [P, QT, NTOK])
            vv = sbt(c3, "vv", [P, TA, DH])
            og = sbt(c3, "og", [P, FT, SEQ])
            PW = sbt(c3, "PW", [P, 2, TA, SEQ])
            rowb = sbt(c3, "rowb", [P, 2, SEQ])
            hh_ = sbt(c3, "hh", [P, TL, DH])
            wo = sbt(c3, "wo", [P, KD, DH])
            qw = sbt(c3, "qw", [P, FT, DQK])
            kw = sbt(c3, "kw", [P, FT, DQK])
            vw = sbt(c3, "vw", [P, FT, DH])
            ngc = sbt(c3, "ngc", [P, HEADS * FT])
            skc = sbt(c3, "skc", [P, HEADS * FT])
            lower = sbt(c3, "lower", [P, P])
            upin = sbt(c3, "upin", [P, P])
            dcol = sbt(c3, "dcol", [P, 8])
            pad = sbt(c3, "pad", [P, 2])
            padp = sbt(c3, "padp", [P, 2])
            ah = sbt(c3, "ah", [P, 2, TA])
            st6 = sbt(c3, "st6", [P, TL, 6])
            mv = sbt(c3, "mv", [P, TL, 2])
            var = sbt(c3, "var", [P, TL])
            r1 = sbt(c3, "r1", [P, TL])
            r2 = sbt(c3, "r2", [P, TL])
            s_hld = sem("s_hld"); s_rld = sem("s_rld"); s_nsk = sem("s_nsk"); s_mask = sem("s_mask")
            s_pj = sem("s_pj"); s_pvA = sem("s_pvA"); s_pvV = sem("s_pvV"); s_og = sem("s_og"); s_pre = sem("s_pre")
            s_exp = sem("s_exp"); s_msk = sem("s_msk"); s_P = sem("s_P"); s_nd = sem("s_nd"); s_ndfree = sem("s_ndfree")
            s_hn = sem("s_hn"); s_y = sem("s_y"); s_d3 = sem("s_d3"); s_ah = sem("s_ah"); s_po3 = sem("s_po3")
            GROUPS = [("o", f) for f in range(FT)] + [("q", i) for i in range(QT)] + [("k", i) for i in range(2 * QT)] + \
                     [("v", t) for t in range(TA)] + [("s", t) for t in range(TA)] + [("h", f) for f in range(FT)]
            NG = len(GROUPS)
            owner, cA, cV = [], 0, 0
            for kind, _i in GROUPS:
                if kind in "ov":
                    cA += 1
                    owner.append(("A", cA))
                else:
                    cV += 1
                    owner.append(("V", cV))
            NA, NV = cA, cV
            NPRJ = FT + 3 * QT + TA
            first = [NG - 4 + (b - NG) % 4 for b in range(4)]
            blk = c3.enter_context(nc.Block())

            def cols(d, si):
                if si < TC:
                    return 0, SEQ
                j = si - TC
                return (j * P, SEQ) if d == 0 else (0, (j + 1) * P)

            @blk.sync
            def _(sp):
                for dst, src in ((ngc, "m_norm_g"), (skc, "m_skip")):
                    sp.dma_start(dst[:], feat_cols(I[src][0:1, :]), allow_slow_non_contiguous=True).then_inc(s_nsk, 16)

                def load(h):
                    sp.dma_start(xch[:], d_xc[bass.ds(h * FT, FT)].rearrange("f p w -> p f w")).then_inc(s_hld, 16)
                    sp.dma_start(wo[:], I["m_in_w"][0].rearrange("(k p) n -> p k n", p=P)[:, :, bass.ds(h * DH + INNER, DH)]).then_inc(s_hld, 16)
                    for dst, src in ((qw, "m_q_w"), (kw, "m_k_w"), (vw, "m_v_w")):
                        sp.dma_start(dst[:], I[src][0][bass.ds(h, 1)].rearrange("o (f p) n -> p (o f) n", p=P)).then_inc(s_hld, 16)
                    sp.dma_start(xmh[:], d_xm[bass.ds(h * FT, FT)].rearrange("f p w -> p f w")).then_inc(s_hld, 16)

                def load_rows(h):
                    sp.dma_start(rowb[:].rearrange("p d t -> p (d t)"), d_negm[bass.ds(h, 1), :].to_broadcast([P, 2 * SEQ])).then_inc(s_rld, 16)

                load(0)
                load_rows(0)
                with sp.Fori(1, HEADS) as h:
                    sp.wait_ge(s_pj, NG * h - (NG - NPRJ))
                    sp.wait_ge(s_og, FT * h + 1)
                    load(h)
                    sp.wait_ge(s_pre, 2 * TA * h)
                    load_rows(h)

            @blk.gpsimd
            def _(pool):
                g = nc.gpsimd
                own = Counter(pool, s_po3)
                own(g.memset(lower[:], 0.0))
                own(g.memset(upin[:], 1.0))
                g.affine_select(out=lower[:], in_=lower[:], compare_op=ALU.is_gt, fill=1.0, base=0, pattern=[[1, P]], channel_multiplier=-1).then_inc(s_mask, 1)
                g.affine_select(out=upin[:], in_=upin[:], compare_op=ALU.is_ge, fill=0.0, base=0, pattern=[[1, P]], channel_multiplier=-1).then_inc(s_mask, 1)
                pool.wait_ge(s_mask, 2)
                with pool.Fori(0, HEADS) as h:
                    pool.wait_ge(s_rld, 16 * h + 16)
                    pool.wait_ge(s_nd, 2 * TL * h)
                    g.tensor_copy(ah[:], acol[:, :, :, bass.ds(h, 1)].rearrange("p d t o -> p d (t o)")).then_inc(s_ah, 1)
                    pool.wait_ge(s_ah, h + 1)
                    g.tensor_tensor(padp[:], ident[:, 0:2], ident[:, 0:2], ALU.add)
                    for si in range(TA):
                        for d in range(2):
                            lo, hi = cols(d, si)
                            g.tensor_scalar(PW[:, d, si, lo:hi], rowb[:, d, lo:hi], ah[:, d, si:si + 1], 0.0, ALU.add, ALU.min).then_inc(s_pre, 1)
                    for j in range(TL):
                        for d in range(2):
                            pool.wait_ge(s_exp, h * 2 * TA + 2 * (TC + j) + d + 1)
                            dg = PW[:, d, TC + j, j * P:(j + 1) * P]
                            g.tensor_tensor(dg, dg, (upin if d == 0 else lower)[:], ALU.mult).then_inc(s_msk, 1)

            @blk.scalar
            def _(act):
                a = nc.scalar
                with act.Fori(0, HEADS) as h:
                    for f in range(FT):
                        act.wait_ge(s_pj, NG * h + f + 1)
                        act.wait_ge(s_y, FT * h)
                        a.activation(og[:, f, :], bank[f % 4][:], ACT.Sigmoid).then_inc(s_pvA, 1)
                    for si in range(TA):
                        for d in range(2):
                            lo, hi = cols(d, si)
                            act.wait_ge(s_pre, h * 2 * TA + 2 * si + d + 1)
                            a.activation(PW[:, d, si, lo:hi], PW[:, d, si, lo:hi], ACT.Exp).then_inc(s_exp, 1)
                    for t in range(TA):
                        n = NPRJ - TA + t
                        act.wait_ge(s_pj, NG * h + n + 1)
                        act.wait_ge(s_nd, 2 * TL * h)
                        a.activation(vv[:, t, :], bank[n % 4][:], ACT.Copy).then_inc(s_pvA, 1)

            @blk.vector
            def _(dve):
                v = nc.vector
                own = Counter(dve, s_d3)
                dve.wait_ge(s_nsk, 32)
                dve.wait_ge(s_mask, 2)
                v.memset(dcol[:], 0.0).then_inc(s_ndfree, 2)
                v.memset(st6[:], 0.0).then_inc(s_og, 1)
                v.memset(pad[:], 0.0).then_inc(s_pvV, NV)
                PER = 2 * TL * 3 + TL + 2 + RSQ_STEPS + TL
                with dve.Fori(0, HEADS) as h:
                    own.enter(h, PER)
                    ch = FT * h
                    for f in range(FT):
                        dve.wait_ge(s_pvA, NA * h + f + 1)
                        fc = bass.ds(ch + f, 1)
                        yt = yT[:, fc, :].rearrange("p o n -> p (o n)")
                        v.scalar_tensor_tensor(out=yt, in0=xch[:, f, LAT0:XCW], scalar=skc[:, fc], in1=og[:, f, :], op0=ALU.mult, op1=ALU.mult)
                        v.tensor_scalar(og[:, f, :], og[:, f, :], ngc[:, fc], None, ALU.mult).then_inc(s_og, 1)
                    for i in range(QT):
                        n = FT + i
                        dve.wait_ge(s_pj, NG * h + n + 1)
                        v.tensor_copy(qT[:, i, :], bank[n % 4][:]).then_inc(s_pvV, 1)
                    for i in range(2 * QT):
                        n = FT + QT + i
                        dve.wait_ge(s_pj, NG * h + n + 1)
                        dst = kT[:, i // 2, CTX:NTOK] if i % 2 == 0 else kT[:, i // 2, 0:CTX]
                        v.tensor_scalar(dst, bank[n % 4][:, 0:SEQ if i % 2 == 0 else CTX], DQK ** -0.5, None, ALU.mult).then_inc(s_pvV, 1)
                    for si in range(TA):
                        n = NPRJ + si
                        dve.wait_ge(s_pj, NG * h + n + 1)
                        dve.wait_ge(s_exp, h * 2 * TA + 2 * si + 2)
                        if si >= TC:
                            dve.wait_ge(s_msk, h * 2 * TL + 2 * (si - TC) + 2)
                        for d in range(2):
                            lo, hi = cols(d, si)
                            ins = v.tensor_tensor(PW[:, d, si, lo:hi], PW[:, d, si, lo:hi], bank[n % 4][:, lo:hi], ALU.mult)
                        ins.then_inc(s_pvV, 1)
                    for g in range(2 * TL):
                        t, d = g // 2, g % 2
                        dve.wait_ge(s_nd, h * 2 * TL + g + 1)
                        den = bank[6 + g % 2][:, 0:1]
                        x = dcol[:, g:g + 1]
                        own(v.tensor_scalar(x, den, 0.0, ecol[:, d, t, bass.ds(h, 1)], ALU.add, ALU.max))
                        own(v.scalar_tensor_tensor(out=x, in0=den, scalar=-1.0, in1=x, op0=ALU.mult, op1=ALU.max))
                        own(v.reciprocal(x, x))
                        if d == 0:
                            v.tensor_scalar(hh_[:, t, :], bank[4 + g % 2][:], x, None, ALU.mult).then_inc(s_ndfree, 1)
                        else:
                            dve.wait_ge(s_ndfree, 2 + h * 2 * TL + g)
                            v.scalar_tensor_tensor(out=hh_[:, t, :], in0=bank[4 + g % 2][:], scalar=x, in1=hh_[:, t, :], op0=ALU.mult, op1=ALU.add).then_inc(s_ndfree, 1)
                            dve.wait_ge(s_ndfree, 2 + h * 2 * TL + g + 1)
                            own(v.bn_stats(st6[:, t, :], hh_[:, t, :]))
                    v.memset(pad[:], 0.0)
                    for t in range(TL - 1):
                        v.bn_aggr(mv[:, t, :], st6[:, t, :])
                    own(v.bn_aggr(mv[:, TL - 1, :], st6[:, TL - 1, :]))
                    own(v.tensor_scalar(var[:], mv[:, :, 1:2].rearrange("p t o -> p (t o)"), EPS, None, ALU.add))
                    rsqrt(v, own, r1[:], var[:], r2[:])
                    for t in range(TL):
                        own(v.tensor_scalar(hh_[:, t, :], hh_[:, t, :], mv[:, t, 0:1], var[:, t:t + 1], ALU.subtract, ALU.mult))
                    v.memset(pad[:], 0.0).then_inc(s_hn, 1)
                    for f in range(FT):
                        n = NPRJ + TA + f
                        dve.wait_ge(s_pj, NG * h + n + 1)
                        fc = bass.ds(ch + f, 1)
                        yt = yT[:, fc, :].rearrange("p o n -> p (o n)")
                        v.tensor_tensor(og[:, f, :], og[:, f, :], bank[n % 4][:], ALU.mult).then_inc(s_pvV, 1)
                        dve.wait_ge(s_pvV, NV + NV * h + owner[n][1])
                        v.tensor_tensor(yt, yt, og[:, f, :], ALU.add).then_inc(s_y, 1)
                    own.leave(HEADS, PER)

            @blk.tensor
            def _(pe):
                t_ = nc.tensor
                with pe.Fori(0, HEADS) as h:
                    pe.wait_ge(s_hld, (h + 1) * 96)

                    def begin(n):
                        if n < 4:
                            who, c = owner[first[n]]
                            pe.wait_ge(s_pvV, NV * h + c)
                        else:
                            who, c = owner[n - 4]
                            if who == "A":
                                pe.wait_ge(s_pvA, NA * h + c)
                            else:
                                pe.wait_ge(s_pvV, NV + NV * h + c)
                        return bank[n % 4]

                    for n, (kind, i) in enumerate(GROUPS):
                        if kind == "s" and i == 0:
                            pe.wait_ge(s_pvV, NV + NV * h + 3 * QT)
                        if kind == "h" and i == 0:
                            pe.wait_ge(s_pvA, NA * h + NA)
                            pe.wait_ge(s_pvV, NV + NV * h + 3 * QT + TA)
                            for g in range(2 * TL):
                                t, d = g // 2, g % 2
                                pe.wait_ge(s_ndfree, h * 2 * TL + g + 1)
                                sis = list(range(TC)) + [TC + j for j in range(TL) if (j <= t if d == 0 else j >= t)]
                                for m, si in enumerate(sis):
                                    w = PW[:, d, si, t * P:(t + 1) * P]
                                    t_.matmul(bank[4 + g % 2][:], w, vv[:, si, :], start=(m == 0), stop=(m == len(sis) - 1))
                                    ins = t_.matmul(bank[6 + g % 2][:, 0:1], w, ones[:, 0:1], start=(m == 0), stop=(m == len(sis) - 1))
                                ins.then_inc(s_nd, 1)
                            pe.wait_ge(s_hn, h + 1)
                        b = begin(n)
                        if kind == "o":
                            for k in range(KD):
                                ins = t_.matmul(b[:], wo[:, k, i * P:(i + 1) * P], uT[:, k, CTX:NTOK], start=(k == 0), stop=(k == KD - 1))
                        elif kind in "qk":
                            w = qw if kind == "q" else kw
                            c = i if kind == "q" else i // 2
                            ctx_part = kind == "k" and i % 2 == 1
                            for f in range(FT):
                                x = xch[:, f, 0:CTX] if ctx_part else xch[:, f, LAT0:XCW]
                                ins = t_.matmul(b[:, 0:CTX] if ctx_part else b[:], w[:, f, c * P:(c + 1) * P], x, start=(f == 0), stop=(f == FT - 1))
                        elif kind == "v":
                            c0 = 1 + i * P if i < TC else 2 + i * P
                            for f in range(FT):
                                ins = t_.matmul(b[:], xmh[:, f, c0:c0 + P], vw[:, f, :], start=(f == 0), stop=(f == FT - 1))
                        elif kind == "s":
                            for c in range(QT):
                                ins = t_.matmul(b[:], kT[:, c, i * P:(i + 1) * P], qT[:, c, :], start=(c == 0), stop=(c == QT - 1))
                        else:
                            for t in range(TL):
                                ins = t_.transpose(b[:, t * P:(t + 1) * P], hh_[:, t, i * P:(i + 1) * P], ident[:])
                        ins.then_inc(s_pj, 1)
        if dbg is not None and stop == 3:
            return dump(nc, dbg, sem, [("o_yT", yT[:].rearrange("p a b -> p (a b)"))], [])
        with stage() as c4:
            ow = [sbt(c4, f"ow{i}", [P, FT, D]) for i in range(HEADS)]
            g1b = sbt(c4, "g1b", [P, D])
            zero4 = sbt(c4, "zero4", [P, D])
            s_z4 = sem("s_z4"); s_zr = sem("s_zr")
            tmp4 = sbt(c4, "tmp4", [P, 2, 512])
            s_x4 = sem("s_x4"); s_ow = [sem(f"s_ow{i}") for i in range(HEADS)]; s_o4 = sem("s_o4"); s_d4 = sem("s_d4")
            blk = c4.enter_context(nc.Block())

            @blk.gpsimd
            def _(pool):
                nc.gpsimd.memset(zero4[:], 0.0).then_inc(s_zr, 1)

            @blk.sync
            def _(sp):
                sp.wait_ge(s_zr, 1)
                for i in range(HEADS):
                    if i == 0:
                        for l in range(2):
                            for o in range(NOV):
                                sp.dma_start(d_y[l][(NE + o) * P:(NE + o + 1) * P, :], zero4[:]).then_inc(s_z4, 16)
                    sp.dma_start(ow[i][:], I["m_out_w"][0, i * DH:(i + 1) * DH, :].rearrange("(f p) n -> p f n", p=P)).then_inc(s_ow[i], 16)
                    if i == 0:
                        sp.dma_start(hl[:], I["x"][0].rearrange("(t p) d -> p t d", p=P)).then_inc(s_x4, 16)
                        sp.dma_start(g1b[:], row_bcast(d_mod[0][:, 2 * D:3 * D])).then_inc(s_x4, 16)
                sp.wait_ge(s_z4, 16 * 2 * NOV)

            @blk.tensor
            def _(pe):
                for i in range(HEADS):
                    pe.wait_ge(s_ow[i], 16)
                    for t in range(TL):
                        for n in range(2):
                            for f in range(FT):
                                ins = nc.tensor.matmul(bank[2 * t + n][:], yT[:, i * FT + f, t * P:(t + 1) * P], ow[i][:, f, n * 512:(n + 1) * 512],
                                                       start=(i == 0 and f == 0), stop=(i == HEADS - 1 and f == FT - 1))
                            if i == HEADS - 1:
                                ins.then_inc(s_o4, 1)

            @blk.vector
            def _(dve):
                v = nc.vector
                own = Counter(dve, s_d4)
                dve.wait_ge(s_x4, 32)
                residual(dve, own, bank, s_o4, g1b, tmp4)
        c12.close()
        if dbg is not None and stop == 4:
            return dump(nc, dbg, sem, [("o_hl", hl[:].rearrange("p t d -> p (t d)"))], [])
        expert_ffn(0)
        if dbg is not None and stop == 5:
            return dump(nc, dbg, sem, [("o_hl", hl[:].rearrange("p t d -> p (t d)"))], [])
        hyena()
        if dbg is not None and stop == 6:
            return dump(nc, dbg, sem, [("o_hl", hl[:].rearrange("p t d -> p (t d)"))], [])
        expert_ffn(1)
        if dbg is not None and stop == 7:
            return dump(nc, dbg, sem, [("o_hl", hl[:].rearrange("p t d -> p (t d)"))], [])

        with stage() as c:
            fg = sbt(c, "fg", [P, D]); junk = sbt(c, "junkf", [P, D])
            ss = sbt(c, "ssz", [P, TL]); r1 = sbt(c, "r1z", [P, TL]); r2 = sbt(c, "r2z", [P, TL])
            s_fg = sem("s_fg"); s_sqf = sem("s_sqf"); s_df = sem("s_df"); s_of = sem("s_of"); s_out = sem("s_out")
            blk = c.enter_context(nc.Block())

            @blk.sync
            def _(sp):
                sp.dma_start(fg[:], row_bcast(I["final_g"].rearrange("(o n) -> o n", o=1))).then_inc(s_fg, 16)
                for t in range(TL):
                    sp.wait_ge(s_of, t + 1)
                    sp.dma_start(out[0, t * P:(t + 1) * P, :], hl[:, t, :]).then_inc(s_out, 16)
                sp.wait_ge(s_out, 16 * TL)

            @blk.scalar
            def _(act):
                for t in range(TL):
                    act.wait_ge(s_sqf, t)
                    nc.scalar.activation(junk[:], hl[:, t, :], ACT.Square, accum_out=ss[:, t:t + 1]).then_inc(s_sqf, 1)

            @blk.vector
            def _(dve):
                v = nc.vector
                own = Counter(dve, s_df)
                dve.wait_ge(s_sqf, TL)
                own(v.tensor_scalar(ss[:], ss[:], 1.0 / D, EPS, ALU.mult, ALU.add))
                rsqrt(v, own, r1[:], ss[:], r2[:])
                dve.wait_ge(s_fg, 16)
                for t in range(TL):
                    v.scalar_tensor_tensor(out=hl[:, t, :], in0=hl[:, t, :], scalar=ss[:, t:t + 1], in1=fg[:], op0=ALU.mult, op1=ALU.mult).then_inc(s_of, 1)


def dump(nc, dbg, sem, sb, dr):
    s = sem("s_dump")
    with ExitStack() as c:
        blk = c.enter_context(nc.Block())

        @blk.sync
        def _(sp):
            n = 0
            for name, ap in sb + dr:
                sp.dma_start(dbg[name], ap).then_inc(s, 16)
                n += 16
            sp.wait_ge(s, n)


def constants():
    t = np.arange(SEQ, dtype=np.float64)
    f = np.arange(FREQ, dtype=np.float64)
    n = 2 * FREQ
    ang = np.pi * np.outer(t, 2 * f + 1) / n
    dft = np.concatenate([np.cos(ang), np.sin(ang)], axis=1)
    m = t + SEQ // 2
    ang = np.pi * np.outer(2 * f + 1, m) / n
    idft = np.concatenate([np.cos(ang), np.sin(ang)], axis=0) * (2.0 / n)
    bands = np.arange(1, 17)
    a = (2.0 * np.pi / SEQ) * np.outer(bands, t)
    feat = np.concatenate([t[None] / (SEQ - 1), np.cos(a), np.sin(a)], axis=0)
    tau = np.abs(t - SEQ // 2) / (SEQ / 2)
    neg_tau = -tau.reshape(TL, P).T
    return {k: np.ascontiguousarray(x, dtype=np.float32) for k, x in
            {"dft": dft, "idft": idft, "feat_t": feat, "neg_tau": neg_tau}.items()}


NAMES = ["x", "c", "ctx", "c_ctx", "ada_w", "ada_b", "norm1_g", "norm2_g", "rg_w", "rg_b", "re_w", "re_b",
         "moe_w13", "moe_w2", "m_in_w", "m_conv_w", "m_conv_b", "m_q_w", "m_k_w", "m_v_w", "m_gate_w",
         "m_gate_b", "m_norm_g", "m_skip", "m_out_w", "h_in_w", "h_in_b", "h_sc_w", "h_sc_b", "h_f_w1",
         "h_f_b1", "h_f_freq", "h_f_w2", "h_f_b2", "h_f_w3", "h_decay", "h_fbias", "h_out_w", "h_out_b",
         "final_g"]


def kernel(**inputs):
    import concourse.bacc as bacc
    from concourse.bass_utils import run_bass_kernel_spmd

    nc = bacc.Bacc("TRN2", target_bir_lowering=False, num_devices=1)
    arrays, aps = {}, {}
    for name, a in [(n, inputs[n]) for n in NAMES] + list(constants().items()):
        a = np.ascontiguousarray(a)
        arrays["in_" + name] = a
        aps[name] = nc.dram_tensor("in_" + name, a.shape, mybir.dt.from_np(a.dtype), kind="ExternalInput").ap()
    out = nc.dram_tensor("out_latents", (1, SEQ, D), F32, kind="ExternalOutput").ap()
    build(nc, aps, out)
    r = run_bass_kernel_spmd(nc, [arrays], core_ids=[0])
    return r.results[0]["out_latents"]
```

```python
from contextlib import ExitStack

import numpy as np

import concourse.bass as bass
from concourse import mybir

F32 = mybir.dt.float32
I32 = mybir.dt.int32
ALU = mybir.AluOpType
ACT = mybir.ActivationFunctionType
AXX = mybir.AxisListType.X

P = 128
D = 1024
KD = D // P
SEQ = 512
CTX = 256
TL = SEQ // P
TC = CTX // P
TA = TL + TC
NTOK = SEQ + CTX
EPS = 1e-6
HEADS = 4
INNER = 2048
DH = INNER // HEADS
FT = DH // P
DQK = 256
QT = DQK // P
NE = 32
NGRP = 4
DE = 512
NO_ROW = 4096
NOV = 7
NBLK = NE + NOV
NC3 = 3 * D
FREQ = 384
HFH = 64
HEMB = 33
WCH = 4096
XMW = 1 + CTX + 1 + SEQ + 1
XCW = XMW - 2
LAT0 = CTX + 1


class Counter:

    def __init__(self, eng, sem):
        self.eng, self.sem, self.base, self.n = eng, sem, 0, 0

    def __call__(self, ins):
        self.n += 1
        ins.then_inc(self.sem, 1)
        self.eng.wait_ge(self.sem, self.base + self.n)

    def enter(self, it, per):
        self.keep = (self.base, self.n)
        self.base, self.n = self.base + self.n + it * per, 0

    def leave(self, times, per):
        assert self.n == per, (self.n, per)
        self.base, self.n = self.keep[0], self.keep[1] + times * per


def at_least(eng, sem, value):
    if not isinstance(value, int) or value > 0:
        eng.wait_ge(sem, value)


RSQ_STEPS = 2 + 3 * 4


def rsqrt(v, own, r, x, tmp):
    ri, xi = r.bitcast(I32), x.bitcast(I32)
    own(v.tensor_scalar(ri, xi, 1, None, ALU.arith_shift_right))
    own(v.tensor_scalar(ri, ri, -1, 0x5F3759DF, ALU.mult, ALU.add))
    for i in range(4):
        own(v.tensor_tensor(tmp, r, r, ALU.mult))
        own(v.scalar_tensor_tensor(out=tmp, in0=x, scalar=-0.5, in1=tmp, op0=ALU.mult, op1=ALU.mult))
        own(v.scalar_tensor_tensor(out=x if i == 3 else r, in0=tmp, scalar=1.5, in1=r, op0=ALU.add, op1=ALU.mult))


def build(nc, I, out, dbg=None, stop=99):
    top = ExitStack()
    with top:
        live = [[]]

        def sem(name):
            live[-1].append(nc.alloc_semaphore(name=name))
            return live[-1][-1]

        def retire():
            if done := live.pop():
                nc.clear_and_free_semaphores(done)
                nc.all_engine_barrier()

        def stage():
            live.append([])
            ctx = ExitStack()
            ctx.callback(retire)
            return ctx

        def sbt(ctx, name, shape, dt=F32):
            return ctx.enter_context(nc.sbuf_tensor(name, shape, dt))

        def dram(name, shape, dt=F32):
            return nc.dram_tensor(name, shape, dt, kind="Internal").ap()

        bank = [top.enter_context(nc.psum_tensor(f"bank{i}", [P, 512], F32)) for i in range(8)]
        ident = sbt(top, "ident", [P, P])
        ones = sbt(top, "onesmat", [P, P])
        upper = sbt(top, "upper", [P, P])
        hl = sbt(top, "hl", [P, TL, D])

        d_mod = [dram(f"d_mod{i}", [1, 6 * D]) for i in range(2)]
        d_modc = dram("d_modc", [1, 2 * D])
        d_xm = dram("d_xm", [HEADS * FT, P, XMW])
        d_xc = dram("d_xc", [HEADS * FT, P, XCW])
        d_negm = dram("d_negm", [HEADS, 2 * SEQ])
        d_v = [dram(f"d_v{i}", [SEQ, D]) for i in range(2)]
        d_tab = [dram(f"d_tab{i}", [NBLK * P, 1]) for i in range(2)]
        d_y = [dram(f"d_y{i}", [2 * SEQ, D]) for i in range(2)]

        d_filt = dram("d_filt", [SEQ, 2 * D])

        def row_bcast(src_row):
            return src_row.to_broadcast([P, src_row.shape[1]])

        def feat_cols(src_row):
            return src_row.rearrange("o (f p) -> p (o f)", p=P)

        def residual(dve, own, src, ready, gate, tmp):
            v = nc.vector
            for g in range(2 * TL):
                t, n = g // 2, g % 2
                cs = slice(n * 512, (n + 1) * 512)
                dve.wait_ge(ready, g + 1)
                own(v.tensor_tensor(tmp[:, n, :], src[g][:], gate[:, cs], ALU.mult))
                own(v.tensor_tensor(hl[:, t, cs], hl[:, t, cs], tmp[:, n, :], ALU.add))

        def expert_ffn(l):
            with stage() as c:
                w13 = [sbt(c, f"w13_{l}{u}", [P, KD, 2 * DE]) for u in range(2)]
                w2 = [sbt(c, f"w2_{l}{u}", [P, DE // P, D]) for u in range(2)]
                tokc = sbt(c, f"tokc{l}", [P, NBLK], I32)
                dst = sbt(c, f"dst{l}", [P, NBLK], I32)
                wts = sbt(c, f"wts{l}", [P, 2, TL])
                meta = sbt(c, f"meta{l}", [P, 1 + NOV], I32)
                s_w13 = [sem(f"s_w13_{l}{u}") for u in range(2)]
                s_w2 = [sem(f"s_w2_{l}{u}") for u in range(2)]
                w13v = I["moe_w13"][l].rearrange("e (k p) n -> p e k n", p=P)
                w2v = I["moe_w2"][l].rearrange("e (k p) n -> p e k n", p=P)
                route(l, w13, w2, w13v, w2v, s_w13, s_w2, tokc, dst, wts, meta)
                if dbg is not None and stop == 4.5:
                    dump(nc, dbg, sem, [("o_tokc", tokc[:]), ("o_wts", wts[:].rearrange("p a b -> p (a b)")), ("o_meta", meta[:])], [("o_v", d_v[0])])
                experts(l, w13, w2, w13v, w2v, s_w13, s_w2, tokc, dst, meta)
            with stage() as c:
                yg = [sbt(c, f"yg{l}{i}", [P, 2, D]) for i in range(TL)]
                g2b = sbt(c, f"g2b{l}", [P, D])
                s_yg = [sem(f"s_yg{l}{i}") for i in range(TL)]
                s_g2 = sem(f"s_g2{l}"); s_dc = sem(f"s_dc{l}"); s_c1 = sem(f"s_c1{l}")
                blk = c.enter_context(nc.Block())

                @blk.sync
                def _(sp):
                    for t in range(TL):
                        sp.dma_start(yg[t][:], d_y[l].rearrange("(t p k) d -> t p k d", p=P, k=2)[t]).then_inc(s_yg[t], 16)
                        if t == 0:
                            sp.dma_start(g2b[:], row_bcast(d_mod[l][:, 5 * D:6 * D])).then_inc(s_g2, 16)

                @blk.scalar
                def _(act):
                    for t in range(TL):
                        act.wait_ge(s_yg[t], 16)
                        nc.scalar.activation(yg[t][:, 0, :], yg[t][:, 0, :], ACT.Copy, scale=wts[:, 0, t:t + 1]).then_inc(s_c1, 1)

                @blk.vector
                def _(dve):
                    v = nc.vector
                    own = Counter(dve, s_dc)
                    dve.wait_ge(s_g2, 16)
                    for t in range(TL):
                        dve.wait_ge(s_c1, t + 1)
                        y = yg[t][:, 0, :]
                        own(v.scalar_tensor_tensor(out=y, in0=yg[t][:, 1, :], scalar=wts[:, 1, t:t + 1], in1=y, op0=ALU.mult, op1=ALU.add))
                        own(v.tensor_tensor(y, y, g2b[:], ALU.mult))
                        own(v.tensor_tensor(hl[:, t, :], hl[:, t, :], y, ALU.add))

        def route(l, w13, w2, w13v, w2v, s_w13, s_w2, tokc, dst, wts, meta):
            with stage() as c:
                def T(name, shape, dt=F32):
                    return sbt(c, f"{name}{l}r", shape, dt)

                A2 = T("A2", [P, D]); n2b = T("n2b", [P, D]); shb = T("shb", [P, D]); junk = T("junk", [P, D])
                vt = T("vt", [P, TL, D]); vT = T("vT", [P, KD, SEQ])
                rw = T("rw", [P, KD, NGRP + NE]); rb = T("rb", [P, NGRP + NE])
                ss = T("ss", [P, TL]); r1 = T("r1", [P, TL]); r2 = T("r2", [P, TL])
                zt = T("zt", [NBLK, P]); tabs = T("tabs", [NBLK, P]); tokid = T("tokid", [P, 2 * TL])
                sli = T("sli", [P, TL * 2], I32)
                ei = T("ei", [P, TL, NE])
                LG = T("LG", [P, TL, NGRP]); LE = T("LE", [P, TL, NE])
                eg = T("eg", [P, TL, NGRP]); t4 = T("t4", [P, TL, NGRP]); ohg = T("ohg", [P, TL * NGRP, 1])
                t32 = T("t32", [P, TL, NE]); oh = [T(f"oh{i}", [P, TL, NE]) for i in range(2)]; sel = T("sel", [P, TL, NE])
                m = T("m", [P, TL, 1]); m1 = T("m1", [P, TL, 1]); m2 = T("m2", [P, TL, 1]); gs = T("gs", [P, TL, 1]); ex = T("ex", [P, TL, 1])
                cnt = T("cnt", [P, NE]); nov = T("nov", [P, NE]); ov = T("ov", [P, NE]); De = T("De", [P, NE]); one32 = T("one32", [P, NE])
                slot = T("slot", [P, TL, NE]); slf = T("slf", [P, TL, 2, 1]); mf = T("mf", [P, 1 + NOV]); cmp = T("cmp", [P, NE])
                S = {k: sem(f"s_{k}_l{l}") for k in "rows rld sq vtile vst vps vT lps eg1 eg2 ex1 ex2 sel rk sl pl dv zst sc tl tps iot".split()}
                blk = c.enter_context(nc.Block())

                @blk.sync
                def _(sp):
                    for dst, src in ((n2b, I["norm2_g"][l:l + 1, :]), (A2, d_mod[l][:, 4 * D:5 * D]), (shb, d_mod[l][:, 3 * D:4 * D])):
                        sp.dma_start(dst[:], row_bcast(src)).then_inc(S["rows"], 16)
                    sp.dma_start(rw[:, :, 0:NGRP], I["rg_w"][l].rearrange("(k p) n -> p k n", p=P)).then_inc(S["rld"], 16)
                    sp.dma_start(rw[:, :, NGRP:], I["re_w"][l].rearrange("(k p) n -> p k n", p=P)).then_inc(S["rld"], 16)
                    sp.dma_start(rb[:, 0:NGRP], row_bcast(I["rg_b"][l:l + 1, :])).then_inc(S["rld"], 16)
                    sp.dma_start(rb[:, NGRP:], row_bcast(I["re_b"][l:l + 1, :])).then_inc(S["rld"], 16)
                    for u in range(2):
                        sp.dma_start(w13[u][:], w13v[:, u]).then_inc(s_w13[u], 16)
                        sp.dma_start(w2[u][:], w2v[:, u]).then_inc(s_w2[u], 16)

                @blk.gpsimd
                def _(pool):
                    g = nc.gpsimd
                    g.memset(zt[:], float(NO_ROW)).then_inc(S["pl"], 1)
                    g.iota(tokid[:], [[2 * P, TL], [1, 2]], base=0, channel_multiplier=2, allow_small_or_imprecise_dtypes=True).then_inc(S["iot"], 1)
                    g.iota(ei[:], [[0, TL], [1, NE]], base=0, channel_multiplier=0, allow_small_or_imprecise_dtypes=True).then_inc(S["iot"], 1)
                    pool.wait_ge(S["pl"], 1)
                    pool.dma_start(d_tab[l].rearrange("(b p) o -> b (p o)", p=P), zt[:]).then_inc(S["zst"], 16)
                    for t in range(TL):
                        pool.wait_ge(S["vtile"], t + 1)
                        pool.dma_start(d_v[l][t * P:(t + 1) * P, :], vt[:, t, :]).then_inc(S["vst"], 16)
                    pool.wait_ge(S["zst"], 16)
                    pool.wait_ge(S["iot"], 2)
                    pool.wait_ge(S["sl"], 1)
                    for t in range(TL):
                        for k in range(2):
                            g.indirect_dma_start(d_tab[l], bass.IndirectOffsetOnAxis(sli[:, 2 * t + k:2 * t + k + 1], 0), tokid[:, 2 * t + k:2 * t + k + 1], None).then_inc(S["sc"], 16)
                    pool.wait_ge(S["sc"], 16 * 2 * TL)
                    pool.dma_start(tabs[:], d_tab[l].rearrange("(b p) o -> b (p o)", p=P)).then_inc(S["tl"], 16)
                    pool.wait_ge(S["vst"], 16 * TL)

                @blk.scalar
                def _(act):
                    a = nc.scalar
                    for t in range(TL):
                        act.wait_ge(S["sq"], t)
                        a.activation(junk[:], hl[:, t, :], ACT.Square, accum_out=ss[:, t:t + 1]).then_inc(S["sq"], 1)
                    for k in range(KD):
                        act.wait_ge(S["vps"], k + 1)
                        a.activation(vT[:, k, :], bank[k % 2][:], ACT.Copy).then_inc(S["vT"], 1)
                    act.wait_ge(S["eg1"], 1)
                    a.activation(eg[:], eg[:], ACT.Exp).then_inc(S["eg2"], 1)
                    act.wait_ge(S["ex1"], 1)
                    a.activation(ex[:], ex[:], ACT.Exp).then_inc(S["ex2"], 1)

                @blk.tensor
                def _(pe):
                    t_ = nc.tensor
                    pe.wait_ge(S["vtile"], TL)
                    for k in range(KD):
                        if k >= 2:
                            pe.wait_ge(S["vT"], k - 1)
                        for t in range(TL):
                            ins = t_.transpose(bank[k % 2][:, t * P:(t + 1) * P], vt[:, t, k * P:(k + 1) * P], ident[:])
                        ins.then_inc(S["vps"], 1)
                    pe.wait_ge(S["vT"], KD)
                    pe.wait_ge(S["rld"], 64)
                    for t in range(TL):
                        for k in range(KD):
                            ins = t_.matmul(bank[2 + t][:, 0:NGRP + NE], vT[:, k, t * P:(t + 1) * P], rw[:, k, :], start=(k == 0), stop=(k == KD - 1))
                        ins.then_inc(S["lps"], 1)
                    pe.wait_ge(S["sel"], 1)
                    for j in range(TL):
                        for i in range(j + 1):
                            t_.matmul(bank[6][:, j * NE:(j + 1) * NE], (upper if i == j else ones)[:], sel[:, i, :], start=(i == 0), stop=(i == j))
                    for i in range(TL):
                        ins = t_.matmul(bank[7][:, 0:NE], ones[:], sel[:, i, :], start=(i == 0), stop=(i == TL - 1))
                    ins.then_inc(S["rk"], 1)
                    pe.wait_ge(S["tl"], 16)
                    t_.transpose(bank[0][:, 0:NBLK], tabs[:], ident[0:NBLK, 0:NBLK]).then_inc(S["tps"], 1)

                @blk.vector
                def _(dve):
                    v = nc.vector
                    own = Counter(dve, S["dv"])
                    dve.wait_ge(S["rows"], 48)
                    own(v.scalar_tensor_tensor(out=A2[:], in0=A2[:], scalar=1.0, in1=n2b[:], op0=ALU.add, op1=ALU.mult))
                    dve.wait_ge(S["sq"], TL)
                    own(v.tensor_scalar(ss[:], ss[:], 1.0 / D, EPS, ALU.mult, ALU.add))
                    rsqrt(v, own, r1[:], ss[:], r2[:])
                    for t in range(TL):
                        own(v.scalar_tensor_tensor(out=vt[:, t, :], in0=hl[:, t, :], scalar=ss[:, t:t + 1], in1=A2[:], op0=ALU.mult, op1=ALU.mult))
                        v.tensor_tensor(vt[:, t, :], vt[:, t, :], shb[:], ALU.add).then_inc(S["vtile"], 1)
                    own(v.memset(one32[:], 1.0))
                    dve.wait_ge(S["iot"], 2)
                    for t in range(TL):
                        dve.wait_ge(S["lps"], t + 1)
                        v.tensor_tensor(LG[:, t, :], bank[2 + t][:, 0:NGRP], rb[:, 0:NGRP], ALU.add)
                        own(v.tensor_tensor(LE[:, t, :], bank[2 + t][:, NGRP:NGRP + NE], rb[:, NGRP:], ALU.add))

                    def first_max(x, n, mx, scratch, hot):
                        own(v.tensor_reduce(mx, x, AXX, ALU.max))
                        own(v.tensor_tensor(scratch, x, mx.to_broadcast([P, TL, n]), ALU.is_equal))
                        own(v.scalar_tensor_tensor(out=scratch, in0=scratch, scalar=-64.0, in1=ei[:, :, 0:n], op0=ALU.mult, op1=ALU.add))
                        own(v.tensor_reduce(m[:], scratch, AXX, ALU.min))
                        own(v.tensor_tensor(hot, scratch, m[:].to_broadcast([P, TL, n]), ALU.is_equal))

                    first_max(LG[:], NGRP, gs[:], t4[:], ohg[:].rearrange("p (t g) o -> p t (g o)", g=NGRP))
                    v.tensor_tensor(eg[:], LG[:], gs[:].to_broadcast([P, TL, NGRP]), ALU.subtract).then_inc(S["eg1"], 1)
                    own(v.tensor_scalar(ohg[:], ohg[:], 1e30, -1e30, ALU.mult, ALU.add))
                    le = LE[:].rearrange("p t (g e) -> p (t g) e", g=NGRP)
                    own(v.tensor_tensor(le, le, ohg[:].to_broadcast([P, TL * NGRP, NE // NGRP]), ALU.add))
                    first_max(LE[:], NE, m1[:], t32[:], oh[0][:])
                    own(v.scalar_tensor_tensor(out=LE[:], in0=oh[0][:], scalar=-3e30, in1=LE[:], op0=ALU.mult, op1=ALU.add))
                    first_max(LE[:], NE, m2[:], t32[:], oh[1][:])
                    v.tensor_tensor(sel[:], oh[0][:], oh[1][:], ALU.add).then_inc(S["sel"], 1)
                    v.tensor_tensor(ex[:], m2[:], m1[:], ALU.subtract).then_inc(S["ex1"], 1)
                    dve.wait_ge(S["eg2"], 1)
                    own(v.tensor_reduce(gs[:], eg[:], AXX, ALU.add))
                    dve.wait_ge(S["ex2"], 1)
                    own(v.scalar_tensor_tensor(out=m[:], in0=ex[:], scalar=1.0, in1=gs[:], op0=ALU.add, op1=ALU.mult))
                    own(v.reciprocal(wts[:, 0, :], m[:].rearrange("p t o -> p (t o)")))
                    own(v.tensor_tensor(wts[:, 1, :], wts[:, 0, :], ex[:].rearrange("p t o -> p (t o)"), ALU.mult))
                    dve.wait_ge(S["rk"], 1)
                    own(v.tensor_copy(cnt[:], bank[7][:, 0:NE]))
                    own(v.tensor_scalar(nov[:], cnt[:], float(P), None, ALU.is_gt))
                    for k in (2, 3):
                        own(v.scalar_tensor_tensor(out=nov[:], in0=cnt[:], scalar=float(k * P), in1=nov[:], op0=ALU.is_gt, op1=ALU.add))
                    own(v.tensor_tensor_scan(out=ov[:], data0=one32[:], data1=nov[:], initial=0.0, op0=ALU.mult, op1=ALU.add))
                    own(v.tensor_tensor(De[:], ov[:], nov[:], ALU.subtract))
                    own(v.tensor_tensor(De[:], De[:], ei[:, 0, :], ALU.subtract))
                    own(v.tensor_scalar(De[:], De[:], float(P), float(P * (NE - 1)), ALU.mult, ALU.add))
                    own(v.tensor_copy(slot[:].rearrange("p t e -> p (t e)"), bank[6][:, 0:TL * NE]))
                    for t in range(TL):
                        own(v.scalar_tensor_tensor(out=t32[:, t, :], in0=slot[:, t, :], scalar=float(P), in1=De[:], op0=ALU.is_ge, op1=ALU.mult))
                    own(v.tensor_tensor(slot[:], slot[:], t32[:], ALU.add))
                    own(v.scalar_tensor_tensor(out=slot[:], in0=ei[:], scalar=float(P), in1=slot[:], op0=ALU.mult, op1=ALU.add))
                    for k in range(2):
                        own(v.tensor_tensor(t32[:], oh[k][:], slot[:], ALU.mult))
                        own(v.tensor_reduce(slf[:, :, k, :], t32[:], AXX, ALU.add))
                    v.tensor_copy(sli[:], slf[:].rearrange("p t k o -> p (t k o)")).then_inc(S["sl"], 1)
                    v.tensor_copy(mf[:, 0:1], ov[:, NE - 1:NE])
                    for o in range(NOV):
                        own(v.tensor_scalar(cmp[:], ov[:], float(o), None, ALU.is_le))
                        own(v.tensor_reduce(mf[:, 1 + o:2 + o], cmp[:], AXX, ALU.add))
                    own(v.tensor_scalar(mf[:], mf[:], float(NE - 1), None, ALU.min))
                    own(v.tensor_copy(meta[:], mf[:]))
                    dve.wait_ge(S["tps"], 1)
                    own(v.tensor_copy(dst[:], bank[0][:, 0:NBLK]))
                    own(v.tensor_scalar(tokc[:], dst[:], 1, None, ALU.arith_shift_right))

        def experts(l, w13, w2, w13v, w2v, s_w13, s_w2, tokc, dst, meta):
            with stage() as c:
                def T(name, shape, dt=F32):
                    return sbt(c, f"{name}{l}e", shape, dt)

                xg = [T(f"xg{u}", [P, D]) for u in range(2)]
                gix = [T(f"gix{u}", [P, 1], I32) for u in range(2)]
                six = [T(f"six{u}", [P, 1], I32) for u in range(2)]
                pad = T("pad", [P, 2]); cpad = T("cpad", [P, 2])
                xT = T("xT", [P, KD, P]); sg = T("sg", [P, DE]); hb = T("hb", [P, DE]); hT = T("hT", [P, DE // P, P])
                yb = [T(f"yb{u}", [P, D]) for u in range(2)]
                S = {k: sem(f"s_{k}_l{l}") for k in "xps xTa xTv gp up sg h hps hT yp0 yp1 ya yv ix sx xz "
                     "ox ow oxps oxT og osg oh ohps ohT oyp oy oyst oix osx oblk".split()}
                s_xg = [sem(f"s_xg{l}{u}") for u in range(2)]
                s_yst = [sem(f"s_yst{l}{u}") for u in range(2)]
                b_g, b_u, b_x, b_h, b_y = bank[0], bank[1], (bank[2], bank[3]), bank[4], (bank[5], bank[6])
                blk = c.enter_context(nc.Block())

                def extra(eng, reg, body):
                    with eng.Fori(0, NOV) as o:
                        with eng.If(reg > o):
                            body(o)

                @blk.sync
                def _(sp):
                    with sp.Fori(1, NE // 2) as it:
                        for u in range(2):
                            b = it * 2 + u
                            sp.wait_ge(S["up"], b - 1)
                            sp.dma_start(w13[u][:], w13v[:, bass.ds(b, 1)].rearrange("p o k n -> p (o k) n")).then_inc(s_w13[u], 16)
                            sp.wait_ge(S["yp1"], b - 1)
                            sp.dma_start(w2[u][:], w2v[:, bass.ds(b, 1)].rearrange("p o k n -> p (o k) n")).then_inc(s_w2[u], 16)
                    sp.wait_ge(S["yp1"], NE)
                    total = sp.value_load(meta[0:1, 0:1], min_val=0, max_val=NOV)

                    def body(o):
                        sp.wait_ge(S["oblk"], o + 1)
                        sp.wait_ge(S["yp1"], NE)
                        e = sp.value_load(meta[0:1, bass.ds(o + 1, 1)], min_val=0, max_val=NE - 1)
                        sp.dma_start(w13[0][:], w13v[:, bass.ds(e, 1)].rearrange("p o k n -> p (o k) n")).then_inc(S["ow"], 16)
                        sp.dma_start(w2[0][:], w2v[:, bass.ds(e, 1)].rearrange("p o k n -> p (o k) n")).then_inc(S["ow"], 16)

                    extra(sp, total, body)

                @blk.gpsimd
                def _(pool):
                    g = nc.gpsimd

                    def gather(u, col, copied, count, done):
                        g.tensor_copy(gix[u][:], col).then_inc(copied, 1)
                        pool.wait_ge(copied, count)
                        g.tensor_tensor(pad[:], ident[:, 0:2], ident[:, 0:2], ALU.add)
                        g.indirect_dma_start(xg[u][:], None, d_v[l], bass.IndirectOffsetOnAxis(gix[u][:, 0:1], 0),
                                             bounds_check=SEQ - 1, oob_is_err=False).then_inc(done, 16)

                    def scatter(u, col, copied, count, done):
                        g.tensor_copy(six[u][:], col).then_inc(copied, 1)
                        pool.wait_ge(copied, count)
                        g.tensor_tensor(pad[:], ident[:, 0:2], ident[:, 0:2], ALU.add)
                        g.indirect_dma_start(d_y[l], bass.IndirectOffsetOnAxis(six[u][:, 0:1], 0), yb[u][:], None,
                                             bounds_check=2 * SEQ - 1, oob_is_err=False).then_inc(done, 16)

                    for u in range(2):
                        g.memset(xg[u][:], 0.0).then_inc(S["xz"], 1)
                    pool.wait_ge(S["xz"], 2)
                    for u in range(2):
                        gather(u, tokc[:, u:u + 1], S["ix"], u + 1, s_xg[u])

                    def block(it, u, last=False):
                        b = it * 2 + u
                        if not last:
                            pool.wait_ge(s_xg[u], 16 * it + 16)
                            pool.wait_ge(S["xps"], 2 * b + 2)
                            gather(u, tokc[:, bass.ds(b + 2, 1)], S["ix"], b + 3, s_xg[u])
                        at_least(pool, s_yst[u], 16 * it)
                        pool.wait_ge(S["ya"], b + 1)
                        pool.wait_ge(S["yv"], b + 1)
                        scatter(u, dst[:, bass.ds(b, 1)], S["sx"], b + 1, s_yst[u])

                    for u in range(2):
                        block(0, u)
                    with pool.Fori(1, NE // 2 - 1) as it:
                        for u in range(2):
                            block(it, u)
                    for u in range(2):
                        block(NE // 2 - 1, u, last=True)
                    for u in range(2):
                        pool.wait_ge(s_yst[u], 16 * (NE // 2))
                    total = pool.value_load(meta[0:1, 0:1], min_val=0, max_val=NOV)
                    g.tensor_tensor(cpad[:], ident[:, 0:2], ident[:, 0:2], ALU.add).then_inc(S["oblk"], 1)

                    def body(o):
                        pool.wait_ge(S["oblk"], o + 1)
                        gather(0, tokc[:, bass.ds(o + NE, 1)], S["oix"], o + 1, S["ox"])
                        pool.wait_ge(S["oy"], o + 1)
                        scatter(0, dst[:, bass.ds(o + NE, 1)], S["osx"], o + 1, S["oyst"])
                        pool.wait_ge(S["oyst"], 16 * o + 16)
                        g.tensor_tensor(cpad[:], ident[:, 0:2], ident[:, 0:2], ALU.add).then_inc(S["oblk"], 1)

                    extra(pool, total, body)

                @blk.tensor
                def _(pe):
                    t_ = nc.tensor

                    def x_transposes(u, done):
                        for half in range(2):
                            for k in range(KD // 2):
                                kk = half * (KD // 2) + k
                                ins = t_.transpose(b_x[half][:, k * P:(k + 1) * P], xg[u][:, kk * P:(kk + 1) * P], ident[:])
                            ins.then_inc(done, 1)

                    def product1(bnk, w, n):
                        for k in range(KD):
                            ins = t_.matmul(bnk[:], xT[:, k, :], w[:, k, n * DE:(n + 1) * DE], start=(k == 0), stop=(k == KD - 1))
                        return ins

                    def h_transposes(done):
                        for k in range(DE // P):
                            ins = t_.transpose(b_h[:, k * P:(k + 1) * P], hb[:, k * P:(k + 1) * P], ident[:])
                        ins.then_inc(done, 1)

                    def product2(w, n):
                        for k in range(DE // P):
                            ins = t_.matmul(b_y[n][:], hT[:, k, :], w[:, k, n * 512:(n + 1) * 512], start=(k == 0), stop=(k == DE // P - 1))
                        return ins

                    def block(it, u, last=False):
                        b = it * 2 + u
                        pe.wait_ge(S["xTa"], b + 1)
                        pe.wait_ge(S["xTv"], b + 1)
                        pe.wait_ge(s_w13[u], 16 * it + 16)
                        at_least(pe, S["sg"], b)
                        product1(b_g, w13[u], 0).then_inc(S["gp"], 1)
                        at_least(pe, S["h"], b)
                        product1(b_u, w13[u], 1).then_inc(S["up"], 1)
                        if not last:
                            pe.wait_ge(s_xg[1 - u], 16 * it + 16 + 16 * u)
                            x_transposes(1 - u, S["xps"])
                        at_least(pe, S["hT"], b)
                        pe.wait_ge(S["h"], b + 1)
                        h_transposes(S["hps"])
                        pe.wait_ge(s_w2[u], 16 * it + 16)
                        pe.wait_ge(S["hT"], b + 1)
                        at_least(pe, S["ya"], b)
                        product2(w2[u], 0).then_inc(S["yp0"], 1)
                        at_least(pe, S["yv"], b)
                        product2(w2[u], 1).then_inc(S["yp1"], 1)

                    pe.wait_ge(s_xg[0], 16)
                    x_transposes(0, S["xps"])
                    for u in range(2):
                        block(0, u)
                    with pe.Fori(1, NE // 2 - 1) as it:
                        for u in range(2):
                            block(it, u)
                    block(NE // 2 - 1, 0)
                    block(NE // 2 - 1, 1, last=True)
                    total = pe.value_load(meta[0:1, 0:1], min_val=0, max_val=NOV)

                    def body(o):
                        pe.wait_ge(S["ox"], 16 * o + 16)
                        x_transposes(0, S["oxps"])
                        pe.wait_ge(S["oxT"], o + 1)
                        pe.wait_ge(S["ow"], 32 * o + 32)
                        product1(b_g, w13[0], 0)
                        product1(b_u, w13[0], 1).then_inc(S["og"], 1)
                        pe.wait_ge(S["oh"], o + 1)
                        h_transposes(S["ohps"])
                        pe.wait_ge(S["ohT"], o + 1)
                        product2(w2[0], 0)
                        product2(w2[0], 1).then_inc(S["oyp"], 1)

                    pe.wait_ge(S["yv"], NE)
                    pe.wait_ge(S["ya"], NE)
                    extra(pe, total, body)

                @blk.scalar
                def _(act):
                    a = nc.scalar

                    def x_half(done):
                        act.wait_ge(S["xps"], done)
                        a.activation(xT[:, 0:4, :].rearrange("p k n -> p (k n)"), b_x[0][:], ACT.Copy).then_inc(S["xTa"], 1)

                    def block(it, u, last=False):
                        b = it * 2 + u
                        act.wait_ge(S["gp"], b + 1)
                        at_least(act, S["h"], b)
                        a.activation(sg[:], b_g[:], ACT.Silu).then_inc(S["sg"], 1)
                        if not last:
                            x_half(2 * b + 3)
                        at_least(act, s_yst[u], 16 * it)
                        act.wait_ge(S["yp0"], b + 1)
                        a.activation(yb[u][:, 0:512], b_y[0][:], ACT.Copy).then_inc(S["ya"], 1)

                    x_half(1)
                    for u in range(2):
                        block(0, u)
                    with act.Fori(1, NE // 2 - 1) as it:
                        for u in range(2):
                            block(it, u)
                    block(NE // 2 - 1, 0)
                    block(NE // 2 - 1, 1, last=True)
                    total = act.value_load(meta[0:1, 0:1], min_val=0, max_val=NOV)

                    def body(o):
                        act.wait_ge(S["og"], o + 1)
                        a.activation(sg[:], b_g[:], ACT.Silu).then_inc(S["osg"], 1)

                    extra(act, total, body)

                @blk.vector
                def _(dve):
                    v = nc.vector

                    def x_half(done):
                        dve.wait_ge(S["xps"], done)
                        v.tensor_copy(xT[:, 4:8, :].rearrange("p k n -> p (k n)"), b_x[1][:]).then_inc(S["xTv"], 1)

                    def block(it, u, last=False):
                        b = it * 2 + u
                        dve.wait_ge(S["sg"], b + 1)
                        dve.wait_ge(S["up"], b + 1)
                        at_least(dve, S["hps"], b)
                        v.tensor_tensor(hb[:], sg[:], b_u[:], ALU.mult).then_inc(S["h"], 1)
                        if not last:
                            x_half(2 * b + 4)
                        at_least(dve, S["yp1"], b)
                        dve.wait_ge(S["hps"], b + 1)
                        v.tensor_copy(hT[:].rearrange("p k n -> p (k n)"), b_h[:]).then_inc(S["hT"], 1)
                        at_least(dve, s_yst[u], 16 * it)
                        dve.wait_ge(S["yp1"], b + 1)
                        v.tensor_copy(yb[u][:, 512:1024], b_y[1][:]).then_inc(S["yv"], 1)

                    x_half(2)
                    for u in range(2):
                        block(0, u)
                    with dve.Fori(1, NE // 2 - 1) as it:
                        for u in range(2):
                            block(it, u)
                    block(NE // 2 - 1, 0)
                    block(NE // 2 - 1, 1, last=True)
                    total = dve.value_load(meta[0:1, 0:1], min_val=0, max_val=NOV)

                    def body(o):
                        dve.wait_ge(S["oxps"], 2 * o + 2)
                        for half in range(2):
                            ins = v.tensor_copy(xT[:, 4 * half:4 * half + 4, :].rearrange("p k n -> p (k n)"), b_x[half][:])
                        ins.then_inc(S["oxT"], 1)
                        dve.wait_ge(S["osg"], o + 1)
                        v.tensor_tensor(hb[:], sg[:], b_u[:], ALU.mult).then_inc(S["oh"], 1)
                        dve.wait_ge(S["ohps"], o + 1)
                        v.tensor_copy(hT[:].rearrange("p k n -> p (k n)"), b_h[:]).then_inc(S["ohT"], 1)
                        dve.wait_ge(S["oyp"], o + 1)
                        for n in range(2):
                            ins = v.tensor_copy(yb[0][:, n * 512:(n + 1) * 512], b_y[n][:])
                        ins.then_inc(S["oy"], 1)

                    for u in range(2):
                        dve.wait_ge(s_yst[u], 16 * (NE // 2))
                    extra(dve, total, body)

        def filters():
            with stage() as c:
                def T(name, shape, dt=F32):
                    return sbt(c, f"{name}f", shape, dt)

                ft = T("ft", [HEMB, SEQ]); w1 = T("w1", [HEMB, HFH]); w2 = T("w2", [HFH, HFH]); w3 = T("w3", [HFH, 2 * D])
                pc = T("pc", [HFH, 3]); z = [T(f"z{i}", [HFH, SEQ]) for i in range(2)]; kx = T("kx", [HFH, SEQ])
                ntau = T("ntau", [P, TL]); dec = T("dec", [P, 2 * D]); E = T("E", [P, 2, 512])
                fl = T("fl", [P, TL, 2 * D]); sq = T("sq", [P, 2, 512]); NF = 2 * D // P
                nrm = T("nrm", [P, NF]); r1 = T("r1", [P, NF]); r2 = T("r2", [P, NF]); dg = T("dg", [P, 4, 512])
                S = {k: sem(f"s_{k}_fl") for k in "ld ps d x zz E g sq sp dg bc st fin".split()}
                blk = c.enter_context(nc.Block())
                TWO_PI_HI = 6.28125
                TWO_PI_LO = 2 * np.pi - TWO_PI_HI
                MAGIC = 1.5 * 2.0 ** 23

                @blk.sync
                def _(sp):
                    sp.dma_start(ft[:], I["feat_t"]).then_inc(S["ld"], 16)
                    sp.dma_start(ntau[:], I["neg_tau"]).then_inc(S["ld"], 16)
                    sp.dma_start(w1[:], I["h_f_w1"][0]).then_inc(S["ld"], 16)
                    sp.dma_start(w2[:], I["h_f_w2"][0]).then_inc(S["ld"], 16)
                    sp.dma_start(w3[:], I["h_f_w3"][0]).then_inc(S["ld"], 16)
                    for i, k in enumerate(("h_f_b1", "h_f_b2", "h_f_freq")):
                        sp.dma_start(pc[:, i:i + 1], I[k].rearrange("o p -> p o"), allow_slow_non_contiguous=True).then_inc(S["ld"], 16)
                    sp.dma_start(dec[:], row_bcast(I["h_decay"][0:1, :])).then_inc(S["ld"], 16)
                    for n in range(4):
                        sp.wait_ge(S["fin"], n + 1)
                        sp.dma_start(d_filt.rearrange("(t p) n -> p t n", p=P)[:, :, n * 512:(n + 1) * 512], fl[:, :, n * 512:(n + 1) * 512]).then_inc(S["st"], 16)
                    sp.wait_ge(S["st"], 64)

                @blk.tensor
                def _(pe):
                    t_ = nc.tensor

                    def norms(i):
                        n = i // TL
                        pe.wait_ge(S["sq"], i + 1)
                        for q in range(4):
                            c = n * 4 + q
                            ins = t_.matmul(bank[3][:, c:c + 1], sq[:, i % 2, q * P:(q + 1) * P], ones[:, 0:1],
                                            start=(i == 0 and q == 0), stop=(i == 4 * TL - 1 and q == 3), skip_group_check=True)
                        ins.then_inc(S["sp"], 1)

                    pe.wait_ge(S["ld"], 16 * 9)
                    t_.matmul(bank[0][0:HFH, :], w1[:], ft[:], start=True, stop=True).then_inc(S["ps"], 1)
                    pe.wait_ge(S["zz"], 1)
                    t_.matmul(bank[0][0:HFH, :], w2[:], z[0][:], start=True, stop=True).then_inc(S["ps"], 1)
                    pe.wait_ge(S["zz"], 2)
                    for n in range(4):
                        for t in range(TL):
                            i = n * TL + t
                            if i >= 2:
                                pe.wait_ge(S["g"], i - 1)
                            t_.matmul(bank[1 + i % 2][:], z[1][:, t * P:(t + 1) * P], w3[:, n * 512:(n + 1) * 512], start=True, stop=True).then_inc(S["ps"], 1)
                            if i >= 1:
                                norms(i - 1)
                    norms(4 * TL - 1)
                    for n in range(4):
                        pe.wait_ge(S["dg"], n + 1)
                        t_.matmul(bank[4 + n][:], ones[:], dg[:, n, :], start=True, stop=True).then_inc(S["bc"], 1)

                @blk.scalar
                def _(act):
                    a = nc.scalar
                    for i in range(2):
                        act.wait_ge(S["x"], i + 1)
                        a.activation(z[i][:], z[i][:], ACT.Sin).then_inc(S["zz"], 1)
                    for i in range(16):
                        n, t = i // TL, i % TL
                        if i >= 2:
                            act.wait_ge(S["g"], i - 1)
                        a.activation(E[:, i % 2, :], dec[:, n * 512:(n + 1) * 512], ACT.Exp, scale=ntau[:, t:t + 1]).then_inc(S["E"], 1)
                        act.wait_ge(S["g"], i + 1)
                        if i >= 2:
                            act.wait_ge(S["sp"], i - 1)
                        a.activation(sq[:, i % 2, :], fl[:, t, n * 512:(n + 1) * 512], ACT.Square).then_inc(S["sq"], 1)

                @blk.vector
                def _(dve):
                    v = nc.vector
                    own = Counter(dve, S["d"])
                    dve.wait_ge(S["ld"], 16 * 9)
                    for i in range(2):
                        dve.wait_ge(S["ps"], i + 1)
                        own(v.tensor_scalar(z[i][:], bank[0][0:HFH, :], pc[:, i:i + 1], pc[:, 2:3], ALU.add, ALU.mult))
                        own(v.tensor_scalar(kx[:], z[i][:], 1 / (2 * np.pi), MAGIC, ALU.mult, ALU.add))
                        own(v.tensor_scalar(kx[:], kx[:], -MAGIC, None, ALU.add))
                        own(v.scalar_tensor_tensor(out=z[i][:], in0=kx[:], scalar=-TWO_PI_HI, in1=z[i][:], op0=ALU.mult, op1=ALU.add))
                        own(v.scalar_tensor_tensor(out=z[i][:], in0=kx[:], scalar=-TWO_PI_LO, in1=z[i][:], op0=ALU.mult, op1=ALU.add))
                        v.tensor_scalar(z[i][:], z[i][:], 3.1415925, -3.1415925, ALU.min, ALU.max).then_inc(S["x"], 1)
                    for n in range(4):
                        for t in range(TL):
                            i = n * TL + t
                            dve.wait_ge(S["ps"], 2 + i + 1)
                            dve.wait_ge(S["E"], i + 1)
                            v.tensor_tensor(fl[:, t, n * 512:(n + 1) * 512], bank[1 + i % 2][:], E[:, i % 2, :], ALU.mult).then_inc(S["g"], 1)
                    dve.wait_ge(S["sp"], 4 * TL)
                    own(v.tensor_scalar(nrm[:], bank[3][:, 0:NF], EPS, None, ALU.add))
                    rsqrt(v, own, r1[:], nrm[:], r2[:])
                    for n in range(4):
                        for q in range(4):
                            ins = v.tensor_scalar(dg[:, n, q * P:(q + 1) * P], ident[:], nrm[:, n * 4 + q:n * 4 + q + 1], None, ALU.mult)
                        ins.then_inc(S["dg"], 1)
                    for n in range(4):
                        dve.wait_ge(S["bc"], n + 1)
                        dve.wait_ge(S["sq"], 4 * TL)
                        for t in range(TL):
                            ins = v.tensor_tensor(fl[:, t, n * 512:(n + 1) * 512], fl[:, t, n * 512:(n + 1) * 512], bank[4 + n][:], ALU.mult)
                        ins.then_inc(S["fin"], 1)
                        dve.wait_ge(S["fin"], n + 1)

        def hyena():
            filters()
            with stage() as c:
                def T(name, shape, dt=F32):
                    return sbt(c, f"{name}h", shape, dt)

                zt = T("zt", [P, TL, NC3])
                hyena_inputs(zt)
                hyena_convs(zt)

        def hyena_inputs(ztok):
            with stage() as c:
                def T(name, shape, dt=F32):
                    return sbt(c, f"{name}i", shape, dt)

                xh = T("xh", [P, TL, D]); uh = T("uh", [P, KD, SEQ]); junk = T("junk", [P, D])
                win = [T(f"win{u}", [P, KD, 512]) for u in range(2)]
                zb = [T(f"zb{u}", [P, SEQ + 2]) for u in range(2)]
                zc = [T(f"zc{u}", [P, SEQ]) for u in range(2)]
                mA = T("mA", [P, KD]); mB = T("mB", [P, KD]); n1 = T("n1", [P, KD])
                ib = T("ib", [P, NC3 // P]); cw = T("cw", [P, 3, NC3 // P]); cb = T("cb", [P, NC3 // P])
                ss = T("ss", [P, TL]); r1 = T("r1", [P, TL]); r2 = T("r2", [P, TL])
                S = {k: sem(f"s_{k}_hi") for k in "ld sq d mod xh xT uh used zps zb cv zt tps pad".split()}
                s_w = [sem(f"s_w_hi{u}") for u in range(2)]
                wv = I["h_in_w"][0].rearrange("(k p) n -> p k n", p=P)
                PER = 4 * 2
                blk = c.enter_context(nc.Block())

                @blk.sync
                def _(sp):
                    for dst, src in ((mB[:], d_mod[1][:, 0:D]), (mA[:], d_mod[1][:, D:2 * D]), (n1[:], I["norm1_g"][1:2, :]), (ib[:], I["h_in_b"][0:1, :]),
                                     (cb[:], I["h_sc_b"][0:1, :]), *((cw[:, k, :], I["h_sc_w"][0, k:k + 1, :]) for k in range(3))):
                        sp.dma_start(dst, feat_cols(src), allow_slow_non_contiguous=True).then_inc(S["ld"], 16)
                    for u in range(2):
                        sp.dma_start(win[u][:], wv[:, :, u * 512:(u + 1) * 512]).then_inc(s_w[u], 16)
                    with sp.Fori(1, 3) as it:
                        for u in range(2):
                            sp.wait_ge(S["used"], 2 * it + u - 1)
                            sp.dma_start(win[u][:], wv[:, :, bass.ds(it * 1024 + u * 512, 512)]).then_inc(s_w[u], 16)

                @blk.gpsimd
                def _(pool):
                    for u in range(2):
                        nc.gpsimd.memset(zb[u][:], 0.0).then_inc(S["zb"], 1)

                @blk.scalar
                def _(act):
                    a = nc.scalar
                    for t in range(TL):
                        act.wait_ge(S["sq"], t)
                        a.activation(junk[:], hl[:, t, :], ACT.Square, accum_out=ss[:, t:t + 1]).then_inc(S["sq"], 1)
                    act.wait_ge(S["mod"], 1)
                    for k in range(KD):
                        act.wait_ge(S["xT"], k + 1)
                        a.activation(uh[:, k, :], bank[k % 2][:], ACT.Identity, bias=mB[:, k:k + 1], scale=mA[:, k:k + 1]).then_inc(S["uh"], 1)
                    act.wait_ge(S["zb"], 2)
                    act.wait_ge(S["ld"], 16 * 8)

                    def back(n, b):
                        act.wait_ge(S["tps"], 2 + n + 1)
                        a.activation(ztok[:, :, bass.ds(n * P, P)], bank[2 + b][:].rearrange("p (t c) -> p t c", t=TL), ACT.Copy).then_inc(S["zt"], 1)

                    with act.Fori(0, 6) as q:
                        for f in range(4):
                            n = q * 4 + f
                            act.wait_ge(S["zps"], n + 1)
                            act.wait_ge(S["cv"], n + 1)
                            a.activation(zb[f % 2][:, 1:SEQ + 1], bank[f % 2][:], ACT.Identity, bias=ib[:, bass.ds(n, 1)]).then_inc(S["zb"], 1)
                            if f >= 1:
                                back(n - 1, (f - 1) % 2)
                        back(q * 4 + 3, 1)

                @blk.vector
                def _(dve):
                    v = nc.vector
                    own = Counter(dve, S["d"])
                    dve.wait_ge(S["ld"], 16 * 8)
                    own(v.scalar_tensor_tensor(out=mA[:], in0=mA[:], scalar=1.0, in1=n1[:], op0=ALU.add, op1=ALU.mult))
                    dve.wait_ge(S["sq"], TL)
                    v.tensor_copy(n1[:], mA[:]).then_inc(S["mod"], 1)
                    own(v.tensor_scalar(ss[:], ss[:], 1.0 / D, EPS, ALU.mult, ALU.add))
                    rsqrt(v, own, r1[:], ss[:], r2[:])
                    for t in range(TL):
                        v.tensor_scalar(xh[:, t, :], hl[:, t, :], ss[:, t:t + 1], None, ALU.mult).then_inc(S["xh"], 1)
                    own(v.memset(junk[:, 0:2], 0.0))
                    v.memset(r1[:], 0.0).then_inc(S["cv"], 2)
                    v.memset(r2[:], 0.0).then_inc(S["tps"], 2)
                    v.memset(junk[:, 2:4], 0.0).then_inc(S["zt"], 2)
                    with dve.Fori(0, 6) as q:
                        own.enter(q, PER)
                        for f in range(4):
                            n = q * 4 + f
                            b = f % 2
                            dve.wait_ge(S["zb"], 2 + n + 1)
                            dve.wait_ge(S["tps"], n + 1)
                            own(v.tensor_scalar(zc[b][:], zb[b][:, 0:SEQ], cw[:, 0, bass.ds(n, 1)], cb[:, bass.ds(n, 1)], ALU.mult, ALU.add))
                            own(v.scalar_tensor_tensor(out=zc[b][:], in0=zb[b][:, 1:SEQ + 1], scalar=cw[:, 1, bass.ds(n, 1)], in1=zc[b][:], op0=ALU.mult, op1=ALU.add))
                            v.scalar_tensor_tensor(out=zc[b][:], in0=zb[b][:, 2:SEQ + 2], scalar=cw[:, 2, bass.ds(n, 1)], in1=zc[b][:], op0=ALU.mult, op1=ALU.add).then_inc(S["cv"], 1)
                        own.leave(6, PER)

                @blk.tensor
                def _(pe):
                    t_ = nc.tensor
                    pe.wait_ge(S["xh"], TL)
                    for k in range(KD):
                        if k >= 2:
                            pe.wait_ge(S["uh"], k - 1)
                        for t in range(TL):
                            ins = t_.transpose(bank[k % 2][:, t * P:(t + 1) * P], xh[:, t, k * P:(k + 1) * P], ident[:])
                        ins.then_inc(S["xT"], 1)
                    pe.wait_ge(S["uh"], KD)

                    def back(n, b):
                        pe.wait_ge(S["cv"], 2 + n + 1)
                        pe.wait_ge(S["zt"], n + 1)
                        for t in range(TL):
                            ins = t_.transpose(bank[2 + b][:, t * P:(t + 1) * P], zc[b][:, t * P:(t + 1) * P], ident[:])
                        ins.then_inc(S["tps"], 1)

                    with pe.Fori(0, 3) as it:
                        for u in range(2):
                            q = it * 2 + u
                            pe.wait_ge(s_w[u], 16 * it + 16)
                            for f in range(4):
                                n = q * 4 + f
                                pe.wait_ge(S["zb"], n + 1)
                                for k in range(KD):
                                    ins = t_.matmul(bank[f % 2][:], win[u][:, k, f * P:(f + 1) * P], uh[:, k, :], start=(k == 0), stop=(k == KD - 1))
                                ins.then_inc(S["zps"], 1)
                                if f >= 1:
                                    back(n - 1, (f - 1) % 2)
                            pe.wait_ge(S["zps"], 4 * q + 4)
                            t_.matmul(bank[7][0:1, 0:1], ones[:, 0:1], ones[:, 0:1], start=True, stop=True).then_inc(S["used"], 1)
                            back(q * 4 + 3, 1)

        def hyena_convs(ztok):
            with stage() as c:
                def T(name, shape, dt=F32):
                    return sbt(c, f"{name}v", shape, dt)

                dft = T("dft", [P, TL, 2 * FREQ]); idft = T("idft", [P, 2 * FREQ // P, SEQ])
                fl = T("fl", [P, TL, D]); Fs = [T(f"Fs{i}", [P, 6, D]) for i in range(2)]; Pr = T("Pr", [P, 6, D])
                bias = T("bias", [P, 2 * D]); ta = T("ta", [P, 2, 512]); tb = T("tb", [P, 2, 512])
                S = {k: sem(f"s_{k}_hc") for k in "ld fld fps fs vps d m R yps y I".split()}
                NF = 6
                blk = c.enter_context(nc.Block())

                @blk.sync
                def _(sp):
                    sp.dma_start(dft[:], I["dft"].rearrange("(t p) f -> p t f", p=P)).then_inc(S["ld"], 16)
                    fv = d_filt.rearrange("(t p) n -> p t n", p=P)
                    sp.dma_start(fl[:], fv[:, :, 0:D]).then_inc(S["fld"], 16)
                    sp.dma_start(idft[:], I["idft"].rearrange("(f p) t -> p f t", p=P)).then_inc(S["ld"], 16)
                    sp.dma_start(bias[:], row_bcast(I["h_fbias"][0:1, :])).then_inc(S["ld"], 16)
                    sp.wait_ge(S["fps"], 12)
                    sp.dma_start(fl[:], fv[:, :, D:2 * D]).then_inc(S["fld"], 16)

                @blk.tensor
                def _(pe):
                    t_ = nc.tensor
                    pe.wait_ge(S["ld"], 48)

                    def filter_spectrum(o):
                        pe.wait_ge(S["fld"], 16 * o + 16)
                        for g in range(12):
                            f, n = g // 2, g % 2
                            i = 12 * o + g
                            if i >= 2:
                                pe.wait_ge(S["fs"], i - 1)
                            for t in range(TL):
                                ins = t_.matmul(bank[g % 2][:], dft[:, t, f * P:(f + 1) * P], fl[:, t, n * 512:(n + 1) * 512], start=(t == 0), stop=(t == TL - 1))
                            ins.then_inc(S["fps"], 1)

                    def value_spectrum(o):
                        for g in range(6):
                            i, n = g // 2, g % 2
                            j = 6 * o + g
                            if j >= 2:
                                pe.wait_ge(S["m"], j - 1)
                            for part in range(2):
                                f = part * 3 + i
                                for t in range(TL):
                                    ins = t_.matmul(bank[2 + 2 * (g % 2) + part][:], dft[:, t, f * P:(f + 1) * P], ztok[:, t, 2 * D + n * 512:2 * D + (n + 1) * 512], start=(t == 0), stop=(t == TL - 1))
                            ins.then_inc(S["vps"], 1)

                    def inverse(o):
                        for g in range(8):
                            t, n = g // 2, g % 2
                            j = 8 * o + g
                            if j >= 2:
                                pe.wait_ge(S["y"], j - 1)
                            for f in range(NF):
                                ins = t_.matmul(bank[6 + g % 2][:], idft[:, f, t * P:(t + 1) * P], Pr[:, f, n * 512:(n + 1) * 512], start=(f == 0), stop=(f == NF - 1))
                            ins.then_inc(S["yps"], 1)

                    filter_spectrum(0)
                    value_spectrum(0)
                    filter_spectrum(1)
                    pe.wait_ge(S["R"], 6)
                    inverse(0)
                    pe.wait_ge(S["y"], 8)
                    value_spectrum(1)
                    pe.wait_ge(S["R"], 12)
                    inverse(1)

                @blk.scalar
                def _(act):
                    for o in range(2):
                        for g in range(12):
                            f, n = g // 2, g % 2
                            act.wait_ge(S["fps"], 12 * o + g + 1)
                            nc.scalar.activation(Fs[o][:, f, n * 512:(n + 1) * 512], bank[g % 2][:], ACT.Copy).then_inc(S["fs"], 1)

                @blk.gpsimd
                def _(pool):
                    g_ = nc.gpsimd
                    for o in range(2):
                        for g in range(6):
                            i, n = g // 2, g % 2
                            cs = slice(n * 512, (n + 1) * 512)
                            pool.wait_ge(S["m"], 6 * o + g + 1)
                            if o == 1:
                                pool.wait_ge(S["yps"], 8)
                            g_.tensor_tensor(Pr[:, i, cs], ta[:, 0, :], ta[:, 1, :], ALU.subtract)
                            g_.tensor_tensor(Pr[:, 3 + i, cs], tb[:, 0, :], tb[:, 1, :], ALU.add).then_inc(S["R"], 1)

                @blk.vector
                def _(dve):
                    v = nc.vector
                    own = Counter(dve, S["d"])
                    dve.wait_ge(S["ld"], 48)
                    for o in range(2):
                        for g in range(6):
                            i, n = g // 2, g % 2
                            cs = slice(n * 512, (n + 1) * 512)
                            dve.wait_ge(S["vps"], 6 * o + g + 1)
                            dve.wait_ge(S["fs"], 12 * o + 12)
                            dve.wait_ge(S["R"], 6 * o + g)
                            A1, B1 = bank[2 + 2 * (g % 2)], bank[3 + 2 * (g % 2)]
                            v.tensor_tensor(ta[:, 0, :], A1[:], Fs[o][:, i, cs], ALU.mult)
                            v.tensor_tensor(tb[:, 0, :], A1[:], Fs[o][:, 3 + i, cs], ALU.mult)
                            v.tensor_tensor(ta[:, 1, :], B1[:], Fs[o][:, 3 + i, cs], ALU.mult)
                            v.tensor_tensor(tb[:, 1, :], B1[:], Fs[o][:, i, cs], ALU.mult).then_inc(S["m"], 1)
                            dve.wait_ge(S["m"], 6 * o + g + 1)
                        dve.wait_ge(S["R"], 6 * o + 6)
                        for g in range(8):
                            t, n = g // 2, g % 2
                            val = ztok[:, t, 2 * D + n * 512:2 * D + (n + 1) * 512]
                            own(v.tensor_tensor(ta[:, 0, :], val, bias[:, o * D + n * 512:o * D + (n + 1) * 512], ALU.mult))
                            dve.wait_ge(S["yps"], 8 * o + g + 1)
                            own(v.tensor_tensor(ta[:, 0, :], ta[:, 0, :], bank[6 + g % 2][:], ALU.add))
                            v.tensor_tensor(val, ta[:, 0, :], ztok[:, t, o * D + n * 512:o * D + (n + 1) * 512], ALU.mult).then_inc(S["y"], 1)
                            dve.wait_ge(S["y"], 8 * o + g + 1)
            with stage() as c:
                def T(name, shape, dt=F32):
                    return sbt(c, f"{name}q", shape, dt)

                yh = T("yh", [P, KD, SEQ]); ow = T("ow", [P, KD, D]); ob = T("ob", [P, D]); g1 = T("g1", [P, D]); tmp = T("tmp", [P, 2, 512])
                S = {k: sem(f"s_{k}_ho") for k in "ow ld tps yh o d".split()}
                blk = c.enter_context(nc.Block())

                @blk.sync
                def _(sp):
                    sp.dma_start(ob[:], row_bcast(I["h_out_b"][0:1, :])).then_inc(S["ld"], 16)
                    sp.dma_start(g1[:], row_bcast(d_mod[1][:, 2 * D:3 * D])).then_inc(S["ld"], 16)
                    sp.dma_start(ow[:], I["h_out_w"][0].rearrange("(k p) n -> p k n", p=P)).then_inc(S["ow"], 16)

                @blk.tensor
                def _(pe):
                    t_ = nc.tensor
                    for k in range(KD):
                        if k >= 2:
                            pe.wait_ge(S["yh"], k - 1)
                        for t in range(TL):
                            ins = t_.transpose(bank[k % 2][:, t * P:(t + 1) * P], ztok[:, t, 2 * D + k * P:2 * D + (k + 1) * P], ident[:])
                        ins.then_inc(S["tps"], 1)
                    pe.wait_ge(S["ow"], 16)
                    pe.wait_ge(S["yh"], KD)
                    for t in range(TL):
                        for n in range(2):
                            for k in range(KD):
                                ins = t_.matmul(bank[2 * t + n][:], yh[:, k, t * P:(t + 1) * P], ow[:, k, n * 512:(n + 1) * 512], start=(k == 0), stop=(k == KD - 1))
                            ins.then_inc(S["o"], 1)

                @blk.scalar
                def _(act):
                    for k in range(KD):
                        act.wait_ge(S["tps"], k + 1)
                        nc.scalar.activation(yh[:, k, :], bank[k % 2][:], ACT.Copy).then_inc(S["yh"], 1)

                @blk.vector
                def _(dve):
                    v = nc.vector
                    own = Counter(dve, S["d"])
                    dve.wait_ge(S["ld"], 32)
                    own(v.tensor_tensor(ob[:], ob[:], g1[:], ALU.mult))
                    for t in range(TL):
                        own(v.tensor_tensor(hl[:, t, :], hl[:, t, :], ob[:], ALU.add))
                    residual(dve, own, bank, S["o"], g1, tmp)

        c12 = top.enter_context(ExitStack())
        uT = sbt(c12, "uT", [P, KD, NTOK])
        gacc = sbt(c12, "gacc", [P, TA, 16])
        with stage() as c1:
            ctxt = sbt(c1, "ctxt", [P, TC, D])
            xh = sbt(c1, "xh", [P, D])
            junk = sbt(c1, "junk1", [P, D])
            cv = sbt(c1, "cv", [P, 2, KD])
            acc = sbt(c1, "acc", [P, 2 * 6 * D])
            row0 = sbt(c1, "row0", [2, 2 * D])
            bias0 = sbt(c1, "bias0", [2, 2 * D])
            credit = sbt(c1, "credit1", [1, 2]); credg = sbt(c1, "credg", [1, 2]); credx = sbt(c1, "credx", [1, 2])
            credst = [sbt(c1, f"credst{u}", [1, 2]) for u in range(2)]
            adab = [sbt(c1, f"adab{i}", [P, 2, 2048]) for i in range(2)]
            win = [sbt(c1, f"win{i}", [P, KD, 512]) for i in range(2)]
            ss = sbt(c1, "ss", [P, TA])
            sq = sbt(c1, "sq", [P, TA])
            sq2 = sbt(c1, "sq2", [P, TA])
            mA = sbt(c1, "mA", [P, 2, KD])
            mB = sbt(c1, "mB", [P, 2, KD])
            g1c = sbt(c1, "g1c", [P, KD])
            xmb = [sbt(c1, f"xmb{i}", [P, XMW]) for i in range(2)]
            xcb = [sbt(c1, f"xcb{i}", [P, XCW]) for i in range(2)]
            cvt = sbt(c1, "cvt", [P, XCW])
            gw = sbt(c1, "gw", [P, 2, 16, 16])
            cw = sbt(c1, "cw", [P, 3, 16])
            cb = sbt(c1, "cb", [P, 16])
            s_const = sem("s_const"); s_cvld = sem("s_cvld"); s_accb = sem("s_accb"); s_tok = sem("s_tok"); s_csil = sem("s_csil")
            s_ada = [sem(f"s_ada{i}") for i in range(2)]; s_adaused = sem("s_adaused"); s_ada0used = sem("s_ada0used")
            s_bias0 = sem("s_bias0"); s_row0 = sem("s_row0"); s_row0st = sem("s_row0st"); s_rowps = sem("s_rowps"); s_rowsb = sem("s_rowsb"); s_rowst = sem("s_rowst")
            s_modld = sem("s_modld"); s_modAB = sem("s_modAB")
            s_ss = sem("s_ss");  s_xh = sem("s_xh"); s_xT = sem("s_xT"); s_uT = sem("s_uT"); s_uTc = sem("s_uTc")
            s_win = [sem(f"s_win{i}") for i in range(2)]; s_winused = sem("s_winused")
            s_xmps = sem("s_xmps"); s_xm = sem("s_xm"); s_cvt = sem("s_cvt"); s_xc = sem("s_xc")
            s_gused = sem("s_gused"); s_gps = sem("s_gps"); s_gacc = sem("s_gacc")
            s_xmst = [sem(f"s_xmst{i}") for i in range(2)]; s_pads = sem("s_pads")
            s_dve1 = sem("s_dve1"); s_pool1 = sem("s_pool1"); s_acc1 = sem("s_acc1"); s_tab0 = sem("s_tab0")
            ada = [I["ada_w"][l].rearrange("(p t) n -> p t n", t=KD) for l in range(2)]
            grp = [(0, 0), (0, 1), (0, 2), (1, 0), (1, 1), (1, 2)]
            blk = c1.enter_context(nc.Block())

            @blk.sync
            def _(sp):
                sp.dma_start(cv[:, 0, :], I["c"].rearrange("o (p t) -> p (o t)", t=KD)).then_inc(s_cvld, 16)
                sp.dma_start(cv[:, 1, :], I["c_ctx"].rearrange("(p t) -> p t", t=KD)).then_inc(s_cvld, 16)
                for i in range(2):
                    sp.dma_start(bias0[i:i + 1, :], I["ada_b"][0:1, 0:2 * D]).then_inc(s_bias0, 16)
                for t in range(2):
                    sp.dma_start(adab[t][:], ada[0][:, 2 * t:2 * t + 2, 0:2048]).then_inc(s_ada[t], 16)
                sp.dma_start(hl[:], I["x"][0].rearrange("(t p) d -> p t d", p=P)).then_inc(s_tok, 16)
                sp.dma_start(ctxt[:], I["ctx"][0].rearrange("(t p) d -> p t d", p=P)).then_inc(s_tok, 16)
                for t in range(2, 4):
                    sp.wait_ge(s_ada0used, t - 1)
                    sp.dma_start(adab[t % 2][:], ada[0][:, 2 * t:2 * t + 2, 0:2048]).then_inc(s_ada[t % 2], 16)
                for u in range(2):
                    sp.dma_start(win[u][:], I["m_in_w"][0].rearrange("(k p) n -> p k n", p=P)[:, :, u * 512:(u + 1) * 512]).then_inc(s_win[u], 16)
                sp.wait_ge(s_pads, 1)
                for l in range(2):
                    lo = 2 * D if l == 0 else 0
                    sp.dma_start(acc[0:1, l * 6 * D + lo:(l + 1) * 6 * D], I["ada_b"][l:l + 1, lo:6 * D]).then_inc(s_accb, 16)
                sp.wait_ge(s_row0, 4)
                sp.dma_start(d_mod[0][:, 0:2 * D], row0[0:1, :]).then_inc(s_row0st, 16)
                sp.dma_start(d_modc, row0[1:2, :]).then_inc(s_row0st, 16)
                sp.wait_ge(s_row0st, 32)
                for i, row in enumerate((d_mod[0], d_modc)):
                    sp.dma_start(mB[:, i, :], feat_cols(row[:, 0:D]), allow_slow_non_contiguous=True).then_inc(s_modld, 16)
                    sp.dma_start(mA[:, i, :], feat_cols(row[:, D:2 * D]), allow_slow_non_contiguous=True).then_inc(s_modld, 16)
                with sp.Fori(0, HEADS // 2) as hh:
                    for u in range(2):
                        for j in range(5):
                            n = 4 + j + u * 5
                            l, g = grp[j + 1]
                            sp.wait_ge(s_adaused, hh * 10 + (n - 1))
                            sp.dma_start(adab[n % 2][:], ada[l][:, bass.ds(hh * 4 + 2 * u, 2), g * 2048:(g + 1) * 2048]).then_inc(s_ada[n % 2], 16)
                        with sp.If(hh < 1):
                            sp.wait_ge(s_winused, hh * 2 + u + 1)
                            sp.dma_start(win[u][:], I["m_in_w"][0].rearrange("(k p) n -> p k n", p=P)[:, :, bass.ds(hh * 1024 + (2 + u) * 512, 512)]).then_inc(s_win[u], 16)
                sp.wait_ge(s_rowsb, 20)
                sp.dma_start(d_mod[0][:, 2 * D:6 * D], acc[0:1, 2 * D:6 * D]).then_inc(s_rowst, 16)
                sp.dma_start(d_mod[1], acc[0:1, 6 * D:12 * D]).then_inc(s_rowst, 16)
                sp.wait_ge(s_rowst, 32)

            @blk.gpsimd
            def _(pool):
                own = Counter(pool, s_pool1)
                g = nc.gpsimd
                own(g.memset(ident[:], 0.0))
                g.affine_select(out=ident[:], in_=ident[:], compare_op=ALU.not_equal, fill=1.0, base=0, pattern=[[-1, P]], channel_multiplier=1).then_inc(s_const, 1)
                g.memset(ones[:], 1.0).then_inc(s_const, 1)
                own(g.memset(upper[:], 0.0))
                g.affine_select(out=upper[:], in_=upper[:], compare_op=ALU.is_ge, fill=1.0, base=0, pattern=[[-1, P]], channel_multiplier=1).then_inc(s_const, 1)
                for u in range(2):
                    g.memset(xmb[u][:], 0.0).then_inc(s_xm, 1)
                g.memset(cvt[:, 0:1], 0.0).then_inc(s_gused, 2)
                g.memset(gacc[:], 0.0).then_inc(s_const, 1)
                g.memset(acc[:, 2 * D:], 0.0).then_inc(s_pads, 1)

            @blk.scalar
            def _(act):
                a = nc.scalar
                act.dma_start(g1c[:], feat_cols(I["norm1_g"][0:1, :]), allow_slow_non_contiguous=True).then_inc(s_modld, 16)
                for k in range(3):
                    act.dma_start(cw[:, k, :], I["m_conv_w"][0, k:k + 1, :].rearrange("o (f p) -> p (o f)", p=P), allow_slow_non_contiguous=True).then_inc(s_tab0, 16)
                act.dma_start(cb[:], I["m_conv_b"][0:1, :].rearrange("o (f p) -> p (o f)", p=P), allow_slow_non_contiguous=True).then_inc(s_tab0, 16)
                act.dma_start(gw[:], I["m_gate_w"][0].rearrange("(h f p) n -> p h f n", h=2, p=P)).then_inc(s_tab0, 16)
                act.wait_ge(s_cvld, 32)
                a.activation(cv[:], cv[:], ACT.Silu).then_inc(s_csil, 1)
                act.wait_ge(s_tok, 32)
                for t in range(TA):
                    src = hl[:, t, :] if t < TL else ctxt[:, t - TL, :]
                    act.wait_ge(s_ss, t)
                    a.activation(junk[:], src, ACT.Square, accum_out=ss[:, t:t + 1]).then_inc(s_ss, 1)
                act.wait_ge(s_modAB, 1)
                for k in range(KD):
                    act.wait_ge(s_xT, k + 1)
                    a.activation(uT[:, k, 0:CTX], bank[2 * (k % 2)][:, 0:CTX], ACT.Identity, bias=mB[:, 1, k:k + 1], scale=mA[:, 1, k:k + 1]).then_inc(s_uTc, 1)
                act.wait_ge(s_xm, 2)
                act.wait_ge(s_csil, 1)
                a.activation(credx[:], cv[0:1, 0, 0:2], ACT.Copy).then_inc(s_xc, 1)
                for u in range(2):
                    act.dma_start(credst[u][:], I["c"][0:1, 0:2]).then_inc(s_xmst[u], 16)
                with act.Fori(0, HEADS) as h:
                    for f in range(FT):
                        n = f
                        act.wait_ge(s_xmps, h * FT + n + 1)
                        act.wait_ge(s_gused, h * FT + n + 1)
                        act.wait_ge(s_xmst[f % 2], h * 64 + 32 * (f // 2) + 16)
                        a.activation(xmb[f % 2][:, 1:1 + CTX], bank[2 * (f % 2) + 1][:, 0:CTX], ACT.Copy)
                        a.activation(xmb[f % 2][:, 2 + CTX:2 + CTX + SEQ], bank[2 * (f % 2)][:], ACT.Copy).then_inc(s_xm, 1)
                        act.wait_ge(s_xm, 2 + h * FT + n + 1)
                        act.dma_start(d_xm[bass.ds(h * FT + f, 1), :, :].rearrange("o p w -> (o p) w"), xmb[f % 2][:]).then_inc(s_xmst[f % 2], 16)
                        act.wait_ge(s_cvt, h * FT + n + 1)
                        a.activation(xcb[f % 2][:], cvt[:], ACT.Silu).then_inc(s_xc, 1)
                        act.wait_ge(s_xc, h * FT + n + 2)
                        act.dma_start(d_xc[bass.ds(h * FT + f, 1), :, :].rearrange("o p w -> (o p) w"), xcb[f % 2][:]).then_inc(s_xmst[f % 2], 16)
                for u in range(2):
                    act.wait_ge(s_xmst[u], 32 * HEADS * FT // 2 + 16)

            @blk.vector
            def _(dve):
                v = nc.vector
                own = Counter(dve, s_dve1)
                dve.wait_ge(s_ss, TA)
                own(v.tensor_scalar(ss[:], ss[:], 1.0 / D, EPS, ALU.mult, ALU.add))
                rsqrt(v, own, sq[:], ss[:], sq2[:])
                for t in range(TA):
                    src = hl[:, t, :] if t < TL else ctxt[:, t - TL, :]
                    v.tensor_scalar(src, src, ss[:, t:t + 1], None, ALU.mult).then_inc(s_xh, 1)
                dve.wait_ge(s_ada0used, 4)
                dve.wait_ge(s_bias0, 32)
                v.memset(credit[:], 0.0).then_inc(s_adaused, 4)
                for n in range(4):
                    v.tensor_tensor(row0[:, n * 512:(n + 1) * 512], bank[4 + n][0:2, :], bias0[:, n * 512:(n + 1) * 512], ALU.add).then_inc(s_row0, 1)
                dve.wait_ge(s_modld, 16 * 5)
                own(v.tensor_scalar(mA[:], mA[:], 1.0, None, ALU.add))
                for i in range(2):
                    ins = v.tensor_tensor(mA[:, i, :], mA[:, i, :], g1c[:], ALU.mult)
                ins.then_inc(s_modAB, 1)
                dve.wait_ge(s_modAB, 1)
                for k in range(KD):
                    dve.wait_ge(s_xT, k + 1)
                    v.tensor_scalar(uT[:, k, CTX:NTOK], bank[2 * (k % 2) + 1][:], mA[:, 0, k:k + 1], mB[:, 0, k:k + 1], ALU.mult, ALU.add).then_inc(s_uT, 1)
                dve.wait_ge(s_tab0, 80)
                dve.wait_ge(s_const, 4)
                dve.wait_ge(s_accb, 32)
                dve.wait_ge(s_adaused, 4)
                v.memset(credg[:], 0.0).then_inc(s_gacc, 1)
                PER = 8 + 5
                with dve.Fori(0, HEADS // 2) as hh:
                    own.enter(hh, 2 * PER)
                    for u in range(2):
                        h = hh * 2 + u
                        for f in range(FT):
                            dve.wait_ge(s_xm, 2 + h * FT + f + 1)
                            dve.wait_ge(s_xc, h * FT + f + 1)
                            ft = hh * (2 * FT) + u * FT + f
                            own(v.tensor_scalar(cvt[:], xmb[f % 2][:, 0:XCW], cw[:, 0, bass.ds(ft, 1)], cb[:, bass.ds(ft, 1)], ALU.mult, ALU.add))
                            own(v.scalar_tensor_tensor(out=cvt[:], in0=xmb[f % 2][:, 1:1 + XCW], scalar=cw[:, 1, bass.ds(ft, 1)], in1=cvt[:], op0=ALU.mult, op1=ALU.add))
                            v.scalar_tensor_tensor(out=cvt[:], in0=xmb[f % 2][:, 2:2 + XCW], scalar=cw[:, 2, bass.ds(ft, 1)], in1=cvt[:], op0=ALU.mult, op1=ALU.add).then_inc(s_cvt, 1)
                        for j in range(5):
                            n = 4 + j + u * 5
                            dve.wait_ge(s_ada[n % 2], hh * 80 + 16 * (n // 2 + 1))
                            col = (j + 1) * 2048
                            own(v.scalar_tensor_tensor(out=acc[:, col:col + 2048], in0=adab[n % 2][:, 0, :], scalar=cv[:, 0, bass.ds(hh * 4 + 2 * u, 1)], in1=acc[:, col:col + 2048], op0=ALU.mult, op1=ALU.add))
                            v.scalar_tensor_tensor(out=acc[:, col:col + 2048], in0=adab[n % 2][:, 1, :], scalar=cv[:, 0, bass.ds(hh * 4 + 2 * u + 1, 1)], in1=acc[:, col:col + 2048], op0=ALU.mult, op1=ALU.add).then_inc(s_adaused, 1)
                            dve.wait_ge(s_adaused, hh * 10 + n + 1)
                        dve.wait_ge(s_gps, h + 1)
                        v.tensor_tensor(gacc[:].rearrange("p t n -> p (t n)"), gacc[:].rearrange("p t n -> p (t n)"), bank[6][:, 0:TA * 16], ALU.add).then_inc(s_gacc, 1)
                        dve.wait_ge(s_gacc, h + 2)
                    own.leave(2, 2 * PER)
                for n in range(20):
                    dve.wait_ge(s_rowps, n + 1)
                    v.tensor_copy(acc[0:1, 2 * D + n * 512:2 * D + (n + 1) * 512], bank[n % 4][0:1, :]).then_inc(s_rowsb, 1)

            @blk.tensor
            def _(pe):
                t_ = nc.tensor
                pe.wait_ge(s_const, 4)
                pe.wait_ge(s_csil, 1)
                for t in range(4):
                    pe.wait_ge(s_ada[t % 2], 16 * (t // 2 + 1))
                    for j in range(2):
                        for n in range(4):
                            ins = t_.matmul(bank[4 + n][0:2, :], cv[:, :, 2 * t + j:2 * t + j + 1].rearrange("p i o -> p (i o)"),
                                            adab[t % 2][:, j, n * 512:(n + 1) * 512], start=(t == 0 and j == 0), stop=(t == 3 and j == 1))
                    ins.then_inc(s_ada0used, 1)
                pe.wait_ge(s_xh, TA)
                for k in range(KD):
                    if k >= 2:
                        pe.wait_ge(s_uT, k - 1)
                        pe.wait_ge(s_uTc, k - 1)
                    for t in range(TC):
                        t_.transpose(bank[2 * (k % 2)][:, t * P:(t + 1) * P], ctxt[:, t, k * P:(k + 1) * P], ident[:])
                    for t in range(TL):
                        ins = t_.transpose(bank[2 * (k % 2) + 1][:, t * P:(t + 1) * P], hl[:, t, k * P:(k + 1) * P], ident[:])
                    ins.then_inc(s_xT, 1)
                pe.wait_ge(s_uT, KD)
                pe.wait_ge(s_uTc, KD)
                pe.wait_ge(s_tab0, 80)

                def gates(h, f):
                    pe.wait_ge(s_xc, h * FT + f + 2)
                    if f == 0:
                        pe.wait_ge(s_gacc, h + 1)
                    for half in range(2):
                        for t in range(TA):
                            if half == 0:
                                c0 = t * P if t < TC else LAT0 + (t - TC) * P
                                lhs = xcb[f % 2][:, c0:c0 + P]
                            else:
                                c0 = 1 + t * P if t < TC else 2 + CTX + (t - TC) * P
                                lhs = xmb[f % 2][:, c0:c0 + P]
                            ins = t_.matmul(bank[6][:, t * 16:(t + 1) * 16], lhs, gw[:, half, bass.ds(h * FT + f, 1), :].rearrange("p o n -> p (o n)"),
                                            start=(f == 0 and half == 0 and t == 0), stop=(f == FT - 1 and half == 1 and t == TA - 1), skip_group_check=True)
                    ins.then_inc(s_gused, 1)

                with pe.Fori(0, HEADS // 2) as hh:
                    for u in range(2):
                        h = hh * 2 + u
                        pe.wait_ge(s_win[u], hh * 16 + 16)
                        for f in range(FT):
                            pe.wait_ge(s_xm, h * FT + f + 1)
                            for k in range(KD):
                                w = win[u][:, k, f * P:(f + 1) * P]
                                t_.matmul(bank[2 * (f % 2)][:], w, uT[:, k, CTX:NTOK], start=(k == 0), stop=(k == KD - 1))
                                ins = t_.matmul(bank[2 * (f % 2) + 1][:, 0:CTX], w, uT[:, k, 0:CTX], start=(k == 0), stop=(k == KD - 1))
                            ins.then_inc(s_xmps, 1)
                            if f >= 1:
                                gates(h, f - 1)
                        pe.wait_ge(s_xmps, h * FT + FT)
                        t_.matmul(bank[7][0:1, 0:1], ones[:, 0:1], ones[:, 0:1], start=True, stop=True).then_inc(s_winused, 1)
                        gates(h, FT - 1)
                        pe.wait_ge(s_gused, 2 + h * FT + FT)
                        t_.matmul(bank[7][0:1, 0:1], ones[:, 0:1], ones[:, 0:1], start=True, stop=True).then_inc(s_gps, 1)
                pe.wait_ge(s_adaused, 24)
                pe.wait_ge(s_xm, 2 + HEADS * FT)
                for n in range(20):
                    if n >= 4:
                        pe.wait_ge(s_rowsb, n - 3)
                    t_.matmul(bank[n % 4][0:1, :], ones[:, 0:1], acc[:, 2048 + n * 512:2048 + (n + 1) * 512], start=True, stop=True).then_inc(s_rowps, 1)

        if dbg is not None and stop == 1:
            return dump(nc, dbg, sem, [("o_gacc", gacc[:].rearrange("p t n -> p (t n)")), ("o_uT", uT[:].rearrange("p k n -> p (k n)"))],
                        [("o_mod0", d_mod[0]), ("o_mod1", d_mod[1]), ("o_xc", d_xc.rearrange("a p w -> (a p) w"))])
        yT = sbt(c12, "yT", [P, HEADS * FT, SEQ])
        acol = sbt(c12, "acol", [P, 2, TA, HEADS])
        ecol = sbt(c12, "ecol", [P, 2, TL, HEADS])
        with stage() as c2:
            gb = sbt(c2, "gb", [HEADS, 4])
            R = sbt(c2, "R", [HEADS, 4, NTOK])
            lt = sbt(c2, "lt", [HEADS, 2, NTOK])
            B = sbt(c2, "Bsum", [HEADS, 2, NTOK])
            A = sbt(c2, "Arow", [HEADS, 2, NTOK])
            M = sbt(c2, "Mrow", [HEADS, 2, NTOK])
            AN = sbt(c2, "AN", [HEADS, 2, NTOK])
            EN = sbt(c2, "EN", [HEADS, 2, SEQ])
            NM = sbt(c2, "NM", [HEADS, 2, SEQ])
            s_gb = sem("s_gb"); s_rps = sem("s_rps"); s_lf = sem("s_lf"); s_ln = sem("s_ln"); s_d2 = sem("s_d2")
            s_em = sem("s_em"); s_en = sem("s_en"); s_rows = sem("s_rows"); s_cps = sem("s_cps"); s_nmst = sem("s_nmst")
            s_a2 = sem("s_a2"); s_nmr = sem("s_nmr")
            blk = c2.enter_context(nc.Block())

            @blk.sync
            def _(sp):
                sp.dma_start(gb[:], I["m_gate_b"][0:1, :].rearrange("o (g h) -> (o h) g", g=4), allow_slow_non_contiguous=True).then_inc(s_gb, 16)
                sp.wait_ge(s_nmr, 1)
                sp.dma_start(d_negm, NM[:].rearrange("h d t -> h (d t)")).then_inc(s_nmst, 16)
                sp.wait_ge(s_nmst, 16)

            @blk.tensor
            def _(pe):
                t_ = nc.tensor
                for g in range(4):
                    for t in range(TC):
                        t_.matmul(bank[4 + g][0:HEADS, t * P:(t + 1) * P], gacc[:, t, g * 4:g * 4 + 4], ident[:], start=True, stop=True)
                    for t in range(TL):
                        ins = t_.matmul(bank[g][0:HEADS, t * P:(t + 1) * P], gacc[:, TC + t, g * 4:g * 4 + 4], ident[:], start=True, stop=True)
                    ins.then_inc(s_rps, 1)
                pe.wait_ge(s_rows, 1)
                pe.wait_ge(s_en, 1)
                for d in range(2):
                    for t in range(TA):
                        t_.transpose(bank[0][:, (d * TA + t) * HEADS:(d * TA + t + 1) * HEADS], AN[:, d, t * P:(t + 1) * P], ident[0:HEADS, 0:HEADS])
                    for t in range(TL):
                        ins = t_.transpose(bank[1][:, (d * TL + t) * HEADS:(d * TL + t + 1) * HEADS], EN[:, d, t * P:(t + 1) * P], ident[0:HEADS, 0:HEADS])
                ins.then_inc(s_cps, 1)

            @blk.scalar
            def _(act):
                a = nc.scalar
                act.wait_ge(s_lf, 1)
                a.activation(lt[:], lt[:], ACT.Exp).then_inc(s_a2, 1)
                act.wait_ge(s_a2, 1)
                a.activation(lt[:], lt[:], ACT.Ln, bias=1.0).then_inc(s_ln, 1)
                act.wait_ge(s_em, 1)
                a.activation(EN[:], EN[:], ACT.Exp, scale=-1.0).then_inc(s_en, 1)

            @blk.vector
            def _(dve):
                v = nc.vector
                own = Counter(dve, s_d2)
                dve.wait_ge(s_gb, 16)
                own(v.memset(A[:], 1.0))
                for g in range(4):
                    dve.wait_ge(s_rps, g + 1)
                    for lo, n, src in ((0, CTX, bank[4 + g]), (CTX, SEQ, bank[g])):
                        row = src[0:HEADS, 0:n] if g < 2 else src[0:HEADS, n - 1::-1]
                        own(v.tensor_scalar(R[:, g, lo:lo + n], row, gb[:, g:g + 1], None, ALU.add))
                for d in range(2):
                    ins = v.scalar_tensor_tensor(out=lt[:, d, :], in0=R[:, 2 * d + 1, :], scalar=-1.0, in1=R[:, 2 * d + 1, :], op0=ALU.mult, op1=ALU.min)
                ins.then_inc(s_lf, 1)
                dve.wait_ge(s_ln, 1)
                for d in range(2):
                    own(v.scalar_tensor_tensor(out=lt[:, d, :], in0=R[:, 2 * d + 1, :], scalar=0.0, in1=lt[:, d, :], op0=ALU.min, op1=ALU.subtract))
                for d in range(2):
                    own(v.tensor_tensor_scan(out=B[:, d, :], data0=A[:, d, :], data1=lt[:, d, :], initial=0.0, op0=ALU.mult, op1=ALU.add))
                for d in range(2):
                    own(v.tensor_tensor(A[:, d, :], R[:, 2 * d, :], B[:, d, :], ALU.subtract))
                    own(v.tensor_tensor_scan(out=M[:, d, :], data0=A[:, d, :], data1=A[:, d, :], initial=0.0, op0=ALU.max, op1=ALU.max))
                    own(v.tensor_tensor(B[:, d, :], B[:, d, :], M[:, d, :], ALU.add))

                def lat(T, d):
                    return T[:, d, CTX:NTOK] if d == 0 else T[:, d, NTOK - 1:CTX - 1:-1]

                for d in range(2):
                    ins = v.tensor_scalar(NM[:, d, :], lat(M, d), -1.0, None, ALU.mult)
                ins.then_inc(s_nmr, 1)
                for d in range(2):
                    ins = v.tensor_copy(EN[:, d, :], lat(B, d))
                ins.then_inc(s_em, 1)
                for d in range(2):
                    v.tensor_copy(AN[:, d, CTX:NTOK], lat(A, d))
                    ins = v.tensor_copy(AN[:, d, 0:CTX], A[:, d, 0:CTX] if d == 0 else A[:, d, CTX - 1::-1])
                ins.then_inc(s_rows, 1)
                dve.wait_ge(s_cps, 1)
                v.tensor_copy(acol[:].rearrange("p a b c -> p (a b c)"), bank[0][:, 0:2 * TA * HEADS])
                v.tensor_copy(ecol[:].rearrange("p a b c -> p (a b c)"), bank[1][:, 0:2 * TL * HEADS])
        if dbg is not None and stop == 2:
            return dump(nc, dbg, sem, [("o_acol", acol[:].rearrange("p a b c -> p (a b c)")), ("o_ecol", ecol[:].rearrange("p a b c -> p (a b c)"))], [("o_negm", d_negm)])

        with stage() as c3:
            xch = sbt(c3, "xch", [P, FT, XCW])
            xmh = sbt(c3, "xmh", [P, FT, XMW])
            qT = sbt(c3, "qT", [P, QT, SEQ])
            kT = sbt(c3, "kT", [P, QT, NTOK])
            vv = sbt(c3, "vv", [P, TA, DH])
            og = sbt(c3, "og", [P, FT, SEQ])
            PW = sbt(c3, "PW", [P, 2, TA, SEQ])
            rowb = sbt(c3, "rowb", [P, 2, SEQ])
            hh_ = sbt(c3, "hh", [P, TL, DH])
            wo = sbt(c3, "wo", [P, KD, DH])
            qw = sbt(c3, "qw", [P, FT, DQK])
            kw = sbt(c3, "kw", [P, FT, DQK])
            vw = sbt(c3, "vw", [P, FT, DH])
            ngc = sbt(c3, "ngc", [P, HEADS * FT])
            skc = sbt(c3, "skc", [P, HEADS * FT])
            lower = sbt(c3, "lower", [P, P])
            upin = sbt(c3, "upin", [P, P])
            dcol = sbt(c3, "dcol", [P, 8])
            pad = sbt(c3, "pad", [P, 2])
            padp = sbt(c3, "padp", [P, 2])
            ah = sbt(c3, "ah", [P, 2, TA])
            st6 = sbt(c3, "st6", [P, TL, 6])
            credy = sbt(c3, "credy", [1, 2])
            mv = sbt(c3, "mv", [P, TL, 2])
            var = sbt(c3, "var", [P, TL])
            r1 = sbt(c3, "r1", [P, TL])
            r2 = sbt(c3, "r2", [P, TL])
            s_hld = sem("s_hld"); s_rld = sem("s_rld"); s_nsk = sem("s_nsk"); s_mask = sem("s_mask")
            s_pj = sem("s_pj"); s_pvA = sem("s_pvA"); s_pvV = sem("s_pvV"); s_og = sem("s_og"); s_pre = sem("s_pre")
            s_exp = sem("s_exp"); s_msk = sem("s_msk"); s_P = sem("s_P"); s_nd = sem("s_nd"); s_ndfree = sem("s_ndfree")
            s_hn = sem("s_hn"); s_y = sem("s_y"); s_d3 = sem("s_d3"); s_ah = sem("s_ah"); s_po3 = sem("s_po3")
            GROUPS = [("o", f) for f in range(FT)] + [("q", i) for i in range(QT)] + [("k", i) for i in range(2 * QT)] + \
                     [("v", t) for t in range(TA)] + [("s", t) for t in range(TA)] + [("h", f) for f in range(FT)]
            NG = len(GROUPS)
            owner, cA, cV = [], 0, 0
            for kind, _i in GROUPS:
                if kind in "ov":
                    cA += 1
                    owner.append(("A", cA))
                else:
                    cV += 1
                    owner.append(("V", cV))
            NA, NV = cA, cV
            NPRJ = FT + 3 * QT + TA
            first = [NG - 4 + (b - NG) % 4 for b in range(4)]
            blk = c3.enter_context(nc.Block())

            def cols(d, si):
                if si < TC:
                    return 0, SEQ
                j = si - TC
                return (j * P, SEQ) if d == 0 else (0, (j + 1) * P)

            @blk.sync
            def _(sp):
                for dst, src in ((ngc, "m_norm_g"), (skc, "m_skip")):
                    sp.dma_start(dst[:], feat_cols(I[src][0:1, :]), allow_slow_non_contiguous=True).then_inc(s_nsk, 16)

                def load(h):
                    sp.dma_start(xch[:], d_xc[bass.ds(h * FT, FT)].rearrange("f p w -> p f w")).then_inc(s_hld, 16)
                    sp.dma_start(wo[:], I["m_in_w"][0].rearrange("(k p) n -> p k n", p=P)[:, :, bass.ds(h * DH + INNER, DH)]).then_inc(s_hld, 16)
                    for dst, src in ((qw, "m_q_w"), (kw, "m_k_w"), (vw, "m_v_w")):
                        sp.dma_start(dst[:], I[src][0][bass.ds(h, 1)].rearrange("o (f p) n -> p (o f) n", p=P)).then_inc(s_hld, 16)
                    sp.dma_start(xmh[:], d_xm[bass.ds(h * FT, FT)].rearrange("f p w -> p f w")).then_inc(s_hld, 16)

                def load_rows(h):
                    sp.dma_start(rowb[:].rearrange("p d t -> p (d t)"), d_negm[bass.ds(h, 1), :].to_broadcast([P, 2 * SEQ])).then_inc(s_rld, 16)

                load(0)
                load_rows(0)
                with sp.Fori(1, HEADS) as h:
                    sp.wait_ge(s_pj, NG * h - (NG - NPRJ))
                    sp.wait_ge(s_og, FT * h + 1)
                    load(h)
                    sp.wait_ge(s_pre, 2 * TA * h)
                    load_rows(h)

            @blk.gpsimd
            def _(pool):
                g = nc.gpsimd
                own = Counter(pool, s_po3)
                own(g.memset(lower[:], 0.0))
                own(g.memset(upin[:], 1.0))
                g.affine_select(out=lower[:], in_=lower[:], compare_op=ALU.is_gt, fill=1.0, base=0, pattern=[[1, P]], channel_multiplier=-1).then_inc(s_mask, 1)
                g.affine_select(out=upin[:], in_=upin[:], compare_op=ALU.is_ge, fill=0.0, base=0, pattern=[[1, P]], channel_multiplier=-1).then_inc(s_mask, 1)
                pool.wait_ge(s_mask, 2)
                with pool.Fori(0, HEADS) as h:
                    pool.wait_ge(s_rld, 16 * h + 16)
                    pool.wait_ge(s_nd, 2 * TL * h + 1)
                    g.tensor_copy(ah[:], acol[:, :, :, bass.ds(h, 1)].rearrange("p d t o -> p d (t o)")).then_inc(s_ah, 1)
                    pool.wait_ge(s_ah, h + 1)
                    g.tensor_tensor(padp[:], ident[:, 0:2], ident[:, 0:2], ALU.add)
                    for si in range(TA):
                        for d in range(2):
                            lo, hi = cols(d, si)
                            g.tensor_scalar(PW[:, d, si, lo:hi], rowb[:, d, lo:hi], ah[:, d, si:si + 1], 0.0, ALU.add, ALU.min).then_inc(s_pre, 1)
                    for j in range(TL):
                        for d in range(2):
                            pool.wait_ge(s_exp, h * 2 * TA + 2 * (TC + j) + d + 1)
                            dg = PW[:, d, TC + j, j * P:(j + 1) * P]
                            g.tensor_tensor(dg, dg, (upin if d == 0 else lower)[:], ALU.mult).then_inc(s_msk, 1)

            @blk.scalar
            def _(act):
                a = nc.scalar
                with act.Fori(0, HEADS) as h:
                    for f in range(FT):
                        act.wait_ge(s_pj, NG * h + f + 1)
                        act.wait_ge(s_y, FT * h + 1)
                        a.activation(og[:, f, :], bank[f % 4][:], ACT.Sigmoid).then_inc(s_pvA, 1)
                    for si in range(TA):
                        for d in range(2):
                            lo, hi = cols(d, si)
                            act.wait_ge(s_pre, h * 2 * TA + 2 * si + d + 1)
                            a.activation(PW[:, d, si, lo:hi], PW[:, d, si, lo:hi], ACT.Exp).then_inc(s_exp, 1)
                    for t in range(TA):
                        n = NPRJ - TA + t
                        act.wait_ge(s_pj, NG * h + n + 1)
                        act.wait_ge(s_nd, 2 * TL * h + 1)
                        a.activation(vv[:, t, :], bank[n % 4][:], ACT.Copy).then_inc(s_pvA, 1)

            @blk.vector
            def _(dve):
                v = nc.vector
                own = Counter(dve, s_d3)
                dve.wait_ge(s_nsk, 32)
                dve.wait_ge(s_mask, 2)
                v.memset(dcol[:], 0.0).then_inc(s_ndfree, 2)
                v.memset(st6[:], 0.0).then_inc(s_og, 1)
                v.memset(credy[:], 0.0).then_inc(s_y, 1)
                v.memset(pad[:], 0.0).then_inc(s_pvV, NV)
                PER = 2 * TL * 3 + TL + 2 + RSQ_STEPS + TL
                with dve.Fori(0, HEADS) as h:
                    own.enter(h, PER)
                    ch = FT * h
                    for f in range(FT):
                        dve.wait_ge(s_pvA, NA * h + f + 1)
                        fc = bass.ds(ch + f, 1)
                        yt = yT[:, fc, :].rearrange("p o n -> p (o n)")
                        v.scalar_tensor_tensor(out=yt, in0=xch[:, f, LAT0:XCW], scalar=skc[:, fc], in1=og[:, f, :], op0=ALU.mult, op1=ALU.mult)
                        v.tensor_scalar(og[:, f, :], og[:, f, :], ngc[:, fc], None, ALU.mult).then_inc(s_og, 1)
                    for i in range(QT):
                        n = FT + i
                        dve.wait_ge(s_pj, NG * h + n + 1)
                        v.tensor_copy(qT[:, i, :], bank[n % 4][:]).then_inc(s_pvV, 1)
                    for i in range(2 * QT):
                        n = FT + QT + i
                        dve.wait_ge(s_pj, NG * h + n + 1)
                        dst = kT[:, i // 2, CTX:NTOK] if i % 2 == 0 else kT[:, i // 2, 0:CTX]
                        v.tensor_scalar(dst, bank[n % 4][:, 0:SEQ if i % 2 == 0 else CTX], DQK ** -0.5, None, ALU.mult).then_inc(s_pvV, 1)
                    for si in range(TA):
                        n = NPRJ + si
                        dve.wait_ge(s_pj, NG * h + n + 1)
                        dve.wait_ge(s_exp, h * 2 * TA + 2 * si + 2)
                        if si >= TC:
                            dve.wait_ge(s_msk, h * 2 * TL + 2 * (si - TC) + 2)
                        for d in range(2):
                            lo, hi = cols(d, si)
                            ins = v.tensor_tensor(PW[:, d, si, lo:hi], PW[:, d, si, lo:hi], bank[n % 4][:, lo:hi], ALU.mult)
                        ins.then_inc(s_pvV, 1)
                    for g in range(2 * TL):
                        t, d = g // 2, g % 2
                        dve.wait_ge(s_nd, h * 2 * TL + g + 2)
                        den = bank[6 + g % 2][:, 0:1]
                        x = dcol[:, g:g + 1]
                        own(v.tensor_scalar(x, den, 0.0, ecol[:, d, t, bass.ds(h, 1)], ALU.add, ALU.max))
                        own(v.scalar_tensor_tensor(out=x, in0=den, scalar=-1.0, in1=x, op0=ALU.mult, op1=ALU.max))
                        own(v.reciprocal(x, x))
                        if d == 0:
                            v.tensor_scalar(hh_[:, t, :], bank[4 + g % 2][:], x, None, ALU.mult).then_inc(s_ndfree, 1)
                        else:
                            dve.wait_ge(s_ndfree, 2 + h * 2 * TL + g)
                            v.scalar_tensor_tensor(out=hh_[:, t, :], in0=bank[4 + g % 2][:], scalar=x, in1=hh_[:, t, :], op0=ALU.mult, op1=ALU.add).then_inc(s_ndfree, 1)
                            dve.wait_ge(s_ndfree, 2 + h * 2 * TL + g + 1)
                            own(v.bn_stats(st6[:, t, :], hh_[:, t, :]))
                    v.memset(pad[:], 0.0)
                    for t in range(TL - 1):
                        v.bn_aggr(mv[:, t, :], st6[:, t, :])
                    own(v.bn_aggr(mv[:, TL - 1, :], st6[:, TL - 1, :]))
                    own(v.tensor_scalar(var[:], mv[:, :, 1:2].rearrange("p t o -> p (t o)"), EPS, None, ALU.add))
                    rsqrt(v, own, r1[:], var[:], r2[:])
                    for t in range(TL):
                        own(v.tensor_scalar(hh_[:, t, :], hh_[:, t, :], mv[:, t, 0:1], var[:, t:t + 1], ALU.subtract, ALU.mult))
                    v.memset(pad[:], 0.0).then_inc(s_hn, 1)
                    for f in range(FT):
                        n = NPRJ + TA + f
                        dve.wait_ge(s_pj, NG * h + n + 1)
                        fc = bass.ds(ch + f, 1)
                        yt = yT[:, fc, :].rearrange("p o n -> p (o n)")
                        v.tensor_tensor(og[:, f, :], og[:, f, :], bank[n % 4][:], ALU.mult).then_inc(s_pvV, 1)
                        dve.wait_ge(s_pvV, NV + NV * h + owner[n][1])
                        v.tensor_tensor(yt, yt, og[:, f, :], ALU.add).then_inc(s_y, 1)
                    own.leave(HEADS, PER)

            @blk.tensor
            def _(pe):
                t_ = nc.tensor
                t_.matmul(bank[7][0:1, 511:512], ones[:, 0:1], ones[:, 0:1], start=True, stop=True).then_inc(s_nd, 1)
                with pe.Fori(0, HEADS) as h:
                    pe.wait_ge(s_hld, (h + 1) * 96)

                    def begin(n):
                        if n < 4:
                            who, c = owner[first[n]]
                            pe.wait_ge(s_pvV, NV * h + c)
                        else:
                            who, c = owner[n - 4]
                            if who == "A":
                                pe.wait_ge(s_pvA, NA * h + c)
                            else:
                                pe.wait_ge(s_pvV, NV + NV * h + c)
                        return bank[n % 4]

                    for n, (kind, i) in enumerate(GROUPS):
                        if kind == "s" and i == 0:
                            pe.wait_ge(s_pvV, NV + NV * h + 3 * QT)
                        if kind == "h" and i == 0:
                            pe.wait_ge(s_pvA, NA * h + NA)
                            pe.wait_ge(s_pvV, NV + NV * h + 3 * QT + TA)
                            for g in range(2 * TL):
                                t, d = g // 2, g % 2
                                pe.wait_ge(s_ndfree, h * 2 * TL + g + 1)
                                sis = list(range(TC)) + [TC + j for j in range(TL) if (j <= t if d == 0 else j >= t)]
                                for m, si in enumerate(sis):
                                    w = PW[:, d, si, t * P:(t + 1) * P]
                                    t_.matmul(bank[4 + g % 2][:], w, vv[:, si, :], start=(m == 0), stop=(m == len(sis) - 1))
                                    ins = t_.matmul(bank[6 + g % 2][:, 0:1], w, ones[:, 0:1], start=(m == 0), stop=(m == len(sis) - 1))
                                ins.then_inc(s_nd, 1)
                            pe.wait_ge(s_hn, h + 1)
                        b = begin(n)
                        if kind == "o":
                            for k in range(KD):
                                ins = t_.matmul(b[:], wo[:, k, i * P:(i + 1) * P], uT[:, k, CTX:NTOK], start=(k == 0), stop=(k == KD - 1))
                        elif kind in "qk":
                            w = qw if kind == "q" else kw
                            c = i if kind == "q" else i // 2
                            ctx_part = kind == "k" and i % 2 == 1
                            for f in range(FT):
                                x = xch[:, f, 0:CTX] if ctx_part else xch[:, f, LAT0:XCW]
                                ins = t_.matmul(b[:, 0:CTX] if ctx_part else b[:], w[:, f, c * P:(c + 1) * P], x, start=(f == 0), stop=(f == FT - 1))
                        elif kind == "v":
                            c0 = 1 + i * P if i < TC else 2 + i * P
                            for f in range(FT):
                                ins = t_.matmul(b[:], xmh[:, f, c0:c0 + P], vw[:, f, :], start=(f == 0), stop=(f == FT - 1))
                        elif kind == "s":
                            for c in range(QT):
                                ins = t_.matmul(b[:], kT[:, c, i * P:(i + 1) * P], qT[:, c, :], start=(c == 0), stop=(c == QT - 1))
                        else:
                            for t in range(TL):
                                ins = t_.transpose(b[:, t * P:(t + 1) * P], hh_[:, t, i * P:(i + 1) * P], ident[:])
                        ins.then_inc(s_pj, 1)
        if dbg is not None and stop == 3:
            return dump(nc, dbg, sem, [("o_yT", yT[:].rearrange("p a b -> p (a b)"))], [])
        with stage() as c4:
            ow = [sbt(c4, f"ow{i}", [P, FT, D]) for i in range(HEADS)]
            g1b = sbt(c4, "g1b", [P, D])
            tmp4 = sbt(c4, "tmp4", [P, 2, 512])
            s_x4 = sem("s_x4"); s_ow = [sem(f"s_ow{i}") for i in range(HEADS)]; s_o4 = sem("s_o4"); s_d4 = sem("s_d4")
            blk = c4.enter_context(nc.Block())

            @blk.sync
            def _(sp):
                for i in range(HEADS):
                    sp.dma_start(ow[i][:], I["m_out_w"][0, i * DH:(i + 1) * DH, :].rearrange("(f p) n -> p f n", p=P)).then_inc(s_ow[i], 16)
                    if i == 0:
                        sp.dma_start(hl[:], I["x"][0].rearrange("(t p) d -> p t d", p=P)).then_inc(s_x4, 16)
                        sp.dma_start(g1b[:], row_bcast(d_mod[0][:, 2 * D:3 * D])).then_inc(s_x4, 16)

            @blk.tensor
            def _(pe):
                for i in range(HEADS):
                    pe.wait_ge(s_ow[i], 16)
                    for t in range(TL):
                        for n in range(2):
                            for f in range(FT):
                                ins = nc.tensor.matmul(bank[2 * t + n][:], yT[:, i * FT + f, t * P:(t + 1) * P], ow[i][:, f, n * 512:(n + 1) * 512],
                                                       start=(i == 0 and f == 0), stop=(i == HEADS - 1 and f == FT - 1))
                            if i == HEADS - 1:
                                ins.then_inc(s_o4, 1)

            @blk.vector
            def _(dve):
                v = nc.vector
                own = Counter(dve, s_d4)
                dve.wait_ge(s_x4, 32)
                residual(dve, own, bank, s_o4, g1b, tmp4)
        c12.close()
        if dbg is not None and stop == 4:
            return dump(nc, dbg, sem, [("o_hl", hl[:].rearrange("p t d -> p (t d)"))], [])
        expert_ffn(0)
        if dbg is not None and stop == 5:
            return dump(nc, dbg, sem, [("o_hl", hl[:].rearrange("p t d -> p (t d)"))], [])
        hyena()
        if dbg is not None and stop == 6:
            return dump(nc, dbg, sem, [("o_hl", hl[:].rearrange("p t d -> p (t d)"))], [])
        expert_ffn(1)
        if dbg is not None and stop == 7:
            return dump(nc, dbg, sem, [("o_hl", hl[:].rearrange("p t d -> p (t d)"))], [])

        with stage() as c:
            fg = sbt(c, "fg", [P, D]); junk = sbt(c, "junkf", [P, D])
            ss = sbt(c, "ssz", [P, TL]); r1 = sbt(c, "r1z", [P, TL]); r2 = sbt(c, "r2z", [P, TL])
            s_fg = sem("s_fg"); s_sqf = sem("s_sqf"); s_df = sem("s_df"); s_of = sem("s_of"); s_out = sem("s_out")
            blk = c.enter_context(nc.Block())

            @blk.sync
            def _(sp):
                sp.dma_start(fg[:], row_bcast(I["final_g"].rearrange("(o n) -> o n", o=1))).then_inc(s_fg, 16)
                for t in range(TL):
                    sp.wait_ge(s_of, t + 1)
                    sp.dma_start(out[0, t * P:(t + 1) * P, :], hl[:, t, :]).then_inc(s_out, 16)
                sp.wait_ge(s_out, 16 * TL)

            @blk.scalar
            def _(act):
                for t in range(TL):
                    act.wait_ge(s_sqf, t)
                    nc.scalar.activation(junk[:], hl[:, t, :], ACT.Square, accum_out=ss[:, t:t + 1]).then_inc(s_sqf, 1)

            @blk.vector
            def _(dve):
                v = nc.vector
                own = Counter(dve, s_df)
                dve.wait_ge(s_sqf, TL)
                own(v.tensor_scalar(ss[:], ss[:], 1.0 / D, EPS, ALU.mult, ALU.add))
                rsqrt(v, own, r1[:], ss[:], r2[:])
                dve.wait_ge(s_fg, 16)
                for t in range(TL):
                    v.scalar_tensor_tensor(out=hl[:, t, :], in0=hl[:, t, :], scalar=ss[:, t:t + 1], in1=fg[:], op0=ALU.mult, op1=ALU.mult).then_inc(s_of, 1)


def dump(nc, dbg, sem, sb, dr):
    s = sem("s_dump")
    with ExitStack() as c:
        blk = c.enter_context(nc.Block())

        @blk.sync
        def _(sp):
            n = 0
            for name, ap in sb + dr:
                sp.dma_start(dbg[name], ap).then_inc(s, 16)
                n += 16
            sp.wait_ge(s, n)


def constants():
    t = np.arange(SEQ, dtype=np.float64)
    f = np.arange(FREQ, dtype=np.float64)
    n = 2 * FREQ
    ang = np.pi * np.outer(t, 2 * f + 1) / n
    dft = np.concatenate([np.cos(ang), np.sin(ang)], axis=1)
    m = t + SEQ // 2
    ang = np.pi * np.outer(2 * f + 1, m) / n
    idft = np.concatenate([np.cos(ang), np.sin(ang)], axis=0) * (2.0 / n)
    bands = np.arange(1, 17)
    a = (2.0 * np.pi / SEQ) * np.outer(bands, t)
    feat = np.concatenate([t[None] / (SEQ - 1), np.cos(a), np.sin(a)], axis=0)
    tau = np.abs(t - SEQ // 2) / (SEQ / 2)
    neg_tau = -tau.reshape(TL, P).T
    return {k: np.ascontiguousarray(x, dtype=np.float32) for k, x in
            {"dft": dft, "idft": idft, "feat_t": feat, "neg_tau": neg_tau}.items()}


NAMES = ["x", "c", "ctx", "c_ctx", "ada_w", "ada_b", "norm1_g", "norm2_g", "rg_w", "rg_b", "re_w", "re_b",
         "moe_w13", "moe_w2", "m_in_w", "m_conv_w", "m_conv_b", "m_q_w", "m_k_w", "m_v_w", "m_gate_w",
         "m_gate_b", "m_norm_g", "m_skip", "m_out_w", "h_in_w", "h_in_b", "h_sc_w", "h_sc_b", "h_f_w1",
         "h_f_b1", "h_f_freq", "h_f_w2", "h_f_b2", "h_f_w3", "h_decay", "h_fbias", "h_out_w", "h_out_b",
         "final_g"]


def kernel(**inputs):
    import concourse.bacc as bacc
    from concourse.bass_utils import run_bass_kernel_spmd

    nc = bacc.Bacc("TRN2", target_bir_lowering=False, num_devices=1)
    arrays, aps = {}, {}
    for name, a in [(n, inputs[n]) for n in NAMES] + list(constants().items()):
        a = np.ascontiguousarray(a)
        arrays["in_" + name] = a
        aps[name] = nc.dram_tensor("in_" + name, a.shape, mybir.dt.from_np(a.dtype), kind="ExternalInput").ap()
    out = nc.dram_tensor("out_latents", (1, SEQ, D), F32, kind="ExternalOutput").ap()
    build(nc, aps, out)
    r = run_bass_kernel_spmd(nc, [arrays], core_ids=[0])
    return r.results[0]["out_latents"]
```
